# Optimizing a Trainium2 kernel written in Bass

```python
import math
import jax
import jax.numpy as jnp
from jax import lax
import numpy as np

D_MODEL = 1024
BATCH = 1
SEQ = 128
DEPTH = 2
DEC_BATCH = 1
DEC_SEQ = 512
PAST_LEN = 128

GRID_W = 64
MIX_WIDTH = D_MODEL
A_WIDTH = MIX_WIDTH // 2
B_WIDTH = MIX_WIDTH - A_WIDTH
DK = 128
DV = 128
H_A = A_WIDTH // DV
N_DIR = 2
CHUNK = 64
N_POOL_GROUPS = 4
POOL_GROUP = D_MODEL // N_POOL_GROUPS
POOL_WINDOWS = (2, 4, 8, 16)
D_FF = 2816
N_MOD = 6
N_EVEN = (DEPTH + 1) // 2
N_ODD = DEPTH // 2
EPS = 1e-6
DT_MIN = 0.001
DT_MAX = 0.1
QKV_END = 3 * A_WIDTH
GATE_END = QKV_END + A_WIDTH
BETA_END = GATE_END + N_DIR * H_A
ALPHA_END = BETA_END + N_DIR * H_A
BG_END = ALPHA_END + B_WIDTH
CG_END = BG_END + B_WIDTH
IN_AB = CG_END + B_WIDTH

kernel_name = "hybrid_deltanet_shortconv_pool_diffusion_step"

def rmsnorm(x, g):
    x32 = x.astype(jnp.float32)
    y = x32 * lax.rsqrt(jnp.mean(x32 * x32, axis=-1, keepdims=True) + EPS)
    return (y * g.astype(jnp.float32)).astype(x.dtype)

def l2norm(x):
    return x * lax.rsqrt(jnp.sum(x * x, axis=-1, keepdims=True) + EPS)

def dwconv3(x, w):
    xp = jnp.pad(x, ((0, 0), (1, 1), (0, 0)))
    return xp[:, :-2] * w[0] + xp[:, 1:-1] * w[1] + xp[:, 2:] * w[2]

def sincos_2d(rows, cols, d):
    quarter = d // 4
    omega = 1.0 / (10000.0 ** (jnp.arange(quarter, dtype=jnp.float32) / quarter))
    er = jnp.arange(rows, dtype=jnp.float32)[:, None] * omega[None, :]
    ec = jnp.arange(cols, dtype=jnp.float32)[:, None] * omega[None, :]
    er = jnp.concatenate([jnp.sin(er), jnp.cos(er)], axis=-1)
    ec = jnp.concatenate([jnp.sin(ec), jnp.cos(ec)], axis=-1)
    pe = jnp.concatenate([jnp.broadcast_to(er[:, None, :], (rows, cols, d // 2)),
                          jnp.broadcast_to(ec[None, :, :], (rows, cols, d // 2))], axis=-1)
    return pe.reshape(rows * cols, d)

def _to_chunks(t):
    b, l, h = t.shape[:3]
    t = t.reshape((b, l // CHUNK, CHUNK, h) + t.shape[3:])
    return jnp.moveaxis(t, 3, 1)

def chunk_gated_delta(q, k, v, g, beta, s0):
    f32 = jnp.float32
    b, l, h, dk = q.shape
    dv = v.shape[-1]
    q = _to_chunks(q.astype(f32) * (dk ** -0.5))
    k = _to_chunks(k.astype(f32))
    v = _to_chunks(v.astype(f32))
    beta = _to_chunks(beta.astype(f32))
    gc = jnp.cumsum(_to_chunks(g.astype(f32)), axis=-1)
    tri = jnp.tril(jnp.ones((CHUNK, CHUNK), dtype=bool))
    strict = jnp.tril(jnp.ones((CHUNK, CHUNK), dtype=bool), k=-1)
    decay = jnp.exp(jnp.where(tri, gc[..., :, None] - gc[..., None, :], -jnp.inf))
    kb = k * beta[..., None]
    vb = v * beta[..., None]
    m = jnp.where(strict, jnp.einsum("bhncd,bhnsd->bhncs", kb, k) * decay, 0.0)
    a = m + jnp.eye(CHUNK, dtype=f32)
    u = lax.linalg.triangular_solve(a, vb, left_side=True, lower=True, unit_diagonal=True)
    w = lax.linalg.triangular_solve(a, kb * jnp.exp(gc)[..., None], left_side=True,
                                    lower=True, unit_diagonal=True)
    attn = jnp.where(tri, jnp.einsum("bhncd,bhnsd->bhncs", q, k) * decay, 0.0)
    qg = q * jnp.exp(gc)[..., None]
    kg = k * jnp.exp(gc[..., -1:] - gc)[..., None]
    g_last = jnp.exp(gc[..., -1])
    xs = tuple(jnp.moveaxis(t, 2, 0) for t in (qg, kg, u, w, attn, g_last))

    def step(s, inp):
        qg_i, kg_i, u_i, w_i, attn_i, gl_i = inp
        v_new = u_i - jnp.einsum("bhcd,bhde->bhce", w_i, s)
        o_i = (jnp.einsum("bhcd,bhde->bhce", qg_i, s)
               + jnp.einsum("bhcs,bhse->bhce", attn_i, v_new))
        s = s * gl_i[..., None, None] + jnp.einsum("bhcd,bhce->bhde", kg_i, v_new)
        return s, o_i

    s_fin, o = lax.scan(step, s0.astype(f32), xs)
    o = jnp.transpose(o, (1, 0, 3, 2, 4)).reshape(b, l, h, dv)
    return o, s_fin

def mixer_ab(h, s0, w_in, conv_qkv, a_log, dt_bias, o_norm_g, conv_b, w_out):
    b, l, _ = h.shape
    p = h @ w_in
    qkv = jax.nn.silu(dwconv3(p[..., :QKV_END], conv_qkv))
    q = l2norm(qkv[..., :A_WIDTH].reshape(b, l, H_A, DK).astype(jnp.float32))
    k = l2norm(qkv[..., A_WIDTH:2 * A_WIDTH].reshape(b, l, H_A, DK).astype(jnp.float32))
    v = qkv[..., 2 * A_WIDTH:QKV_END].reshape(b, l, H_A, DV)
    gate = p[..., QKV_END:GATE_END].reshape(b, l, H_A, DV).astype(jnp.float32)
    beta = jax.nn.sigmoid(p[..., GATE_END:BETA_END].astype(jnp.float32)).reshape(b, l, N_DIR, H_A)
    alpha = p[..., BETA_END:ALPHA_END].astype(jnp.float32).reshape(b, l, N_DIR, H_A)
    g = -jnp.exp(a_log.astype(jnp.float32)) * jax.nn.softplus(alpha + dt_bias.astype(jnp.float32))
    o_f, s_f = chunk_gated_delta(q, k, v, g[:, :, 0], beta[:, :, 0], s0[:, 0])
    flip = lambda t: jnp.flip(t, axis=1)
    o_b, s_b = chunk_gated_delta(flip(q), flip(k), flip(v), flip(g[:, :, 1]),
                                 flip(beta[:, :, 1]), s0[:, 1])
    o = rmsnorm(o_f + flip(o_b), o_norm_g) * jax.nn.silu(gate)
    o_a = o.reshape(b, l, A_WIDTH).astype(h.dtype)
    bg = p[..., ALPHA_END:BG_END]
    cg = p[..., BG_END:CG_END]
    hx = p[..., CG_END:IN_AB]
    y_b = bg * dwconv3(cg * hx, conv_b)
    y = jnp.concatenate([o_a, y_b], axis=-1) @ w_out
    return y, jnp.stack([s_f, s_b], axis=1).astype(h.dtype)

def multiscale_pool(h, w_pool, scale):
    b, l, d = h.shape
    hg = h.reshape(b, l, N_POOL_GROUPS, POOL_GROUP).astype(jnp.float32)
    cs = jnp.concatenate([jnp.zeros((b, 1, N_POOL_GROUPS, POOL_GROUP), jnp.float32),
                          jnp.cumsum(hg, axis=1)], axis=1)
    t = jnp.arange(l)
    means = []
    for gi, win in enumerate(POOL_WINDOWS):
        lo = jnp.clip(t - win // 2, 0, l)
        hi = jnp.clip(t - win // 2 + win, 0, l)
        s = cs[:, hi, gi] - cs[:, lo, gi]
        means.append(s / (hi - lo).astype(jnp.float32)[None, :, None])
    mixed = (jnp.stack(means, axis=2) - hg).astype(h.dtype)
    y = jnp.einsum("blgc,gcd->blgd", mixed, w_pool).reshape(b, l, d)
    return y * scale

def conv_ffn(h, w_gate, w_up, conv, w_down):
    u = dwconv3(h @ w_gate, conv)
    return (jax.nn.silu(u) * (h @ w_up)) @ w_down

def setup_inputs(seed: int = 0) -> dict:
    key = jax.random.key(seed)
    ks = jax.random.split(key, 24)
    f32 = jnp.float32

    def nrm(k, shape, s):
        return jax.random.normal(k, shape, f32) * s

    dt = jnp.exp(jax.random.uniform(ks[9], (N_EVEN, N_DIR, H_A), f32)
                 * (math.log(DT_MAX) - math.log(DT_MIN)) + math.log(DT_MIN))
    dt_bias = dt + jnp.log(-jnp.expm1(-dt))
    a_log = jnp.log(jax.random.uniform(ks[10], (N_EVEN, N_DIR, H_A), f32, 1.0, 16.0))
    return {
        "x_prompt": nrm(ks[0], (BATCH, SEQ, D_MODEL), 1.0),
        "x_sample": nrm(ks[1], (DEC_BATCH, DEC_SEQ, D_MODEL), 1.0),
        "state_delta": nrm(ks[2], (DEC_BATCH, N_EVEN, N_DIR, H_A, DK, DV), 0.05),
        "c": nrm(ks[3], (DEC_BATCH, D_MODEL), 1.0),
        "c_ctx": nrm(ks[4], (D_MODEL,), 1.0),
        "norm_mix_g": 1.0 + nrm(ks[5], (DEPTH, D_MODEL), 0.05),
        "norm_ffn_g": 1.0 + nrm(ks[6], (DEPTH, D_MODEL), 0.05),
        "w_ada": nrm(ks[7], (DEPTH, D_MODEL, N_MOD * D_MODEL), 0.5 * D_MODEL ** -0.5),
        "b_ada": nrm(ks[8], (DEPTH, N_MOD * D_MODEL), 0.02),
        "w_in_ab": nrm(ks[11], (N_EVEN, D_MODEL, IN_AB), D_MODEL ** -0.5),
        "conv_qkv": nrm(ks[12], (N_EVEN, 3, QKV_END), 3 ** -0.5),
        "a_log": a_log,
        "dt_bias": dt_bias,
        "o_norm_g": 1.0 + nrm(ks[13], (N_EVEN, DV), 0.05),
        "conv_b": nrm(ks[14], (N_EVEN, 3, B_WIDTH), 3 ** -0.5),
        "w_out_ab": nrm(ks[15], (N_EVEN, MIX_WIDTH, D_MODEL), MIX_WIDTH ** -0.5),
        "w_pool": nrm(ks[16], (N_ODD, N_POOL_GROUPS, POOL_GROUP, POOL_GROUP), POOL_GROUP ** -0.5),
        "pool_scale": 1.0 + nrm(ks[17], (N_ODD, D_MODEL), 0.1),
        "w_ffn_gate": nrm(ks[18], (DEPTH, D_MODEL, D_FF), D_MODEL ** -0.5),
        "w_ffn_up": nrm(ks[19], (DEPTH, D_MODEL, D_FF), D_MODEL ** -0.5),
        "ffn_conv": nrm(ks[20], (DEPTH, 3, D_FF), 3 ** -0.5),
        "w_ffn_down": nrm(ks[21], (DEPTH, D_FF, D_MODEL), D_FF ** -0.5),
        "final_norm_g": 1.0 + nrm(ks[22], (D_MODEL,), 0.05),
    }

def reference(x_prompt, x_sample, state_delta, c, c_ctx, norm_mix_g, norm_ffn_g, w_ada, b_ada,
              w_in_ab, conv_qkv, a_log, dt_bias, o_norm_g, conv_b, w_out_ab, w_pool, pool_scale,
              w_ffn_gate, w_ffn_up, ffn_conv, w_ffn_down, final_norm_g):

    def trunk(x, cond, states, is_context):
        finals = []
        for layer in range(DEPTH):
            mod = jax.nn.silu(cond) @ w_ada[layer] + b_ada[layer]
            shift1, scale1, gate1, shift2, scale2, gate2 = jnp.split(mod[:, None, :], N_MOD, axis=-1)
            h = rmsnorm(x, norm_mix_g[layer]) * (1 + scale1) + shift1
            if layer % 2 == 0:
                e = layer // 2
                y, s_fin = mixer_ab(h, states[:, e], w_in_ab[e], conv_qkv[e], a_log[e],
                                    dt_bias[e], o_norm_g[e], conv_b[e], w_out_ab[e])
                if is_context:
                    finals.append(s_fin)
            else:
                o = layer // 2
                y = multiscale_pool(h, w_pool[o], pool_scale[o])
            x = x + gate1 * y
            h = rmsnorm(x, norm_ffn_g[layer]) * (1 + scale2) + shift2
            x = x + gate2 * conv_ffn(h, w_ffn_gate[layer], w_ffn_up[layer], ffn_conv[layer],
                                     w_ffn_down[layer])
        return rmsnorm(x, final_norm_g), finals

    zero_states = jnp.zeros((x_prompt.shape[0], N_EVEN, N_DIR, H_A, DK, DV), x_prompt.dtype)
    y_prompt, finals = trunk(x_prompt, c_ctx[None, :], zero_states, True)
    new_state_delta = jnp.stack(finals, axis=1)

    rows = x_sample.shape[1] // GRID_W
    x_lat = x_sample + sincos_2d(rows, GRID_W, D_MODEL).astype(x_sample.dtype)[None]
    y_sample, _ = trunk(x_lat, c, state_delta, False)

    return (y_prompt, y_sample, new_state_delta)


_drawn_inputs = setup_inputs


def setup_inputs(seed=0):
    import zlib

    import numpy as np

    out = dict(_drawn_inputs(seed))
    spreads = {}
    factors = {'state_delta': 5.135, 'norm_ffn_g': 2.958, 'o_norm_g': 7.749, 'pool_scale': 4.495}
    for name, (base, spread) in spreads.items():
        noise = np.random.default_rng([zlib.crc32(name.encode()), seed]).standard_normal(out[name].shape)
        drawn = base * np.exp(spread * noise) if base else spread * noise
        out[name] = jnp.asarray(drawn.astype(out[name].dtype))
    for name, factor in factors.items():
        out[name] = (out[name] * factor).astype(out[name].dtype)
    return out
```

```python
from contextlib import ExitStack

import numpy as np

import concourse.bass as bass
from concourse import mybir

P = 128
D = 1024
KD = D // P
SEQ_S, SEQ_P = 512, 128
GRID_W = 64
S0 = 1
P0 = S0 + SEQ_S + 1
W = P0 + SEQ_P + 2
HALF = W // 2
RANGES = [(S0, SEQ_S, 0), (P0, SEQ_P, 1)]
NH, DK = 4, 128
NQKV, NGATE, NB = 12, 4, 4
D_FF = 2816
NF = D_FF // P
GROUPS = [8, 7, 7]
EPS = 1e-6
TILES = [S0 + P * t for t in range(SEQ_S // P)] + [P0]
NT = len(TILES)
LEVELS = 7
PADW = 8
WP = PADW + SEQ_S + PADW + SEQ_P + PADW
POOL_RANGES = [(PADW, S0, SEQ_S, 0), (PADW + SEQ_S + PADW, P0, SEQ_P, 1)]
SLOT = KD * P

F32 = mybir.dt.float32
F32R = mybir.dt.float32r
F16 = mybir.dt.float16
ALU = mybir.AluOpType
ACT = mybir.ActivationFunctionType
ds = bass.ds

PIECES = [(0, S0, HALF - S0, S0, 0), (1, 0, S0 + SEQ_S - HALF, HALF, 0), (1, P0 - HALF, SEQ_P, P0, 1)]

COLS, _at = {}, 0
for _name, _n in (("norm_mix", 2 * KD * 2), ("norm_ffn", 2 * KD * 2), ("pool_scale", KD * 2),
                  ("final", KD), ("tap_qkv", 3 * NQKV), ("tap_b", 3 * NB), ("tap_ffn", 2 * 3 * NF),
                  ("o_norm", 1), ("a_log", NT * 8), ("dt_bias", NT * 8), ("w_ba", KD * 16),
                  ("cond", KD * 2), ("b_ada", 96 * 2)):
    COLS[_name] = (_at, _n)
    _at += _n
NCOLS = _at


def plan():
    at = dict(u=0, A=0, B=0, C=0, f=0)
    segs = {"in": dict(at)}
    at["u"] += 28; at["A"] += 14; at["B"] += 14
    segs["out"] = dict(at)
    at["u"] += 8; at["C"] += 4; at["B"] += 4
    for layer in range(2):
        if layer == 1:
            segs["pool"] = dict(at)
            at["u"] += 2; at["C"] += 4; at["B"] += 4
        for g, nf in enumerate(GROUPS):
            segs["up", layer, g] = dict(at)
            at["u"] += 2 * nf; at["A"] += nf; at["B"] += nf; at["f"] += nf
            segs["down", layer, g] = dict(at)
            at["u"] += 8; at["C"] += 4; at["B"] += 4
    return segs


SEG = plan()
GROUP_AT = [sum(GROUPS[:g]) for g in range(len(GROUPS))]


class Steps:

    def __init__(self, eng, sem):
        self.eng, self.sem, self.done, self.more = eng, sem, 0, 0

    def tick(self, ins):
        ins.then_inc(self.sem, 1)
        self.done += 1

    def sync(self, back=0):
        self.eng.wait_ge(self.sem, self.more + self.done - back)

    def enter(self, i, per):
        self.start, self.per, self.more = self.done, per, i * per

    def leave(self, n):
        assert self.done - self.start == self.per, (self.done - self.start, self.per)
        self.more = 0
        self.done = self.start + n * self.per


def build(nc, t):
    ctx = ExitStack()
    with ctx:
        def sb(name, shape, dt=F32):
            return ctx.enter_context(nc.sbuf_tensor(name, shape, dt))

        def sem(name):
            return ctx.enter_context(nc.semaphore(name))

        x = sb("x", [P, KD, W])
        raw = [sb(f"raw{s}", [P, SLOT]) for s in range(2)]
        whi = [sb(f"whi{s}", [P, SLOT], F32R) for s in range(2)]
        wlo = [sb(f"wlo{s}", [P, SLOT], F32R) for s in range(2)]
        ada_raw = [sb(f"ada_raw{s}", [P, SLOT]) for s in range(2)]
        cols = sb("cols", [P, NCOLS])
        const = sb("const", [P, 4, P])
        mod = sb("mod", [P, 2, 6, KD, 2])
        silu_c = sb("silu_c", [P, KD, 2])
        wba_hi = sb("wba_hi", [P, KD, 16], F32R)
        wba_lo = sb("wba_lo", [P, KD, 16], F32R)
        bias = sb("bias", [P, 2])
        gates = sb("gates", [P, 12, NT * 8])
        junk = sb("junk", [P, P])
        ssq = sb("ssq", [P, 2, NT * NH])
        ident, tri_u, tri_l, ones = (const[:, j, :] for j in range(4))
        eps_col, scale_col = bias[:, 0:1], bias[:, 1:2]

        work = sb("work", [P, 10, W])
        pad = [work[:, 0, :], work[:, 1, :]]
        cv = [work[:, 2, :], work[:, 3, :]]
        h32 = [work[:, 4, :], work[:, 5, :]]
        sq = [work[:, 6, :], work[:, 7, :]]
        acc = work[:, 8, :]
        rstd = work[:, 9, :]
        flat = work[:, :, :].rearrange("p a b -> p (a b)")
        chain = [[flat[:, (2 * j + c) * 512:(2 * j + c + 1) * 512].rearrange("p (h e) -> p h e", h=NH)
                  for c in range(2)] for j in range(6)]
        dec, mt, tt, btx, bty, ys = chain
        bt = [[btx[c], bty[c]] for c in range(2)]
        rr, vn, to, kg, ss, sp_ = chain

        off_h = nc.sbuf_base
        size_h = 2 * KD * W * 4
        hhi = nc.alloc_sbuf_tensor_at("hhi", [P, KD, W], F32R, offset=off_h)
        hlo = nc.alloc_sbuf_tensor_at("hlo", [P, KD, W], F32R, offset=off_h + size_h // 2)
        rinv = nc.alloc_sbuf_tensor_at("rinv", [P, 2 * NT, NH, P], F32, offset=off_h)
        attn = nc.alloc_sbuf_tensor_at("attn", [P, 2 * NT, NH, P], F32, offset=off_h + NT * 2 * 2048)
        assert NT * 4 * 2048 <= size_h

        off_m = off_h + size_h
        qkv = nc.alloc_sbuf_tensor_at("qkv", [P, NQKV, W], F32, offset=off_m)
        osum = nc.alloc_sbuf_tensor_at("osum", [P, NT, NH, P], F32, offset=off_m + 8 * W * 4)
        o2 = off_m + NQKV * W * 4
        ktok = nc.alloc_sbuf_tensor_at("ktok", [P, NT, NH, P], F32, offset=o2)
        vtok = nc.alloc_sbuf_tensor_at("vtok", [P, NT, NH, P], F32, offset=o2 + NT * 2048)
        o3 = o2 + NT * 4096
        sgate = nc.alloc_sbuf_tensor_at("sgate", [P, NGATE, W], F32, offset=o3)
        yb = nc.alloc_sbuf_tensor_at("yb", [P, NB, W], F32, offset=o3 + NGATE * W * 4)
        o4 = o3 + (NGATE + NB) * W * 4
        lmask = nc.alloc_sbuf_tensor_at("lmask", [P, 2 * LEVELS, P], F16, offset=o4)
        end_m = o4 + 2 * LEVELS * P * 2
        pe_tab = nc.alloc_sbuf_tensor_at("pe_tab", [P, KD, SEQ_S], F32, offset=off_m)
        hidhi = nc.alloc_sbuf_tensor_at("hidhi", [P, KD, W], F32R, offset=off_m)
        hidlo = nc.alloc_sbuf_tensor_at("hidlo", [P, KD, W], F32R, offset=off_m + KD * W * 4)
        inv_at = off_m + 2 * KD * W * 4
        yout = nc.alloc_sbuf_tensor_at("yout", [P, KD, W], F32, offset=off_m)
        inv_n = nc.alloc_sbuf_tensor_at("inv_n", [P, 4, W], F32, offset=inv_at)
        hp = nc.alloc_sbuf_tensor_at("hp", [P, KD, WP], F32, offset=inv_at + 4 * W * 4)
        psum_w = nc.alloc_sbuf_tensor_at("psum_w", [P, 3, WP], F32, offset=off_m)
        assert inv_at + 4 * W * 4 + KD * WP * 4 <= end_m and end_m <= nc.sbuf_usable_end, end_m

        ps = ctx.enter_context(nc.psum_tensor("ps", [P, 8, 512], F32))
        pair = {n: ps[:, 2 * j:2 * j + 2, 0:HALF] for j, n in enumerate("ABCX")}
        bank = [ps[:, j, :].rearrange("p (h e) -> p h e", h=NH) for j in range(8)]
        ada_ps = [ps[:, 6 + s, 480:482] for s in range(2)]

        def halves(ap):
            return ap.rearrange("p (b n) -> p b n", b=2)

        def col(name, pattern=None, **dims):
            a, n = COLS[name]
            v = cols[:, a:a + n]
            return v.rearrange(pattern, **dims) if pattern else v

        g_mix = col("norm_mix", "p (l k c) -> p l k c", l=2, k=KD)
        g_ffn = col("norm_ffn", "p (l k c) -> p l k c", l=2, k=KD)
        g_pool = col("pool_scale", "p (k c) -> p k c", k=KD)
        g_final = col("final")
        tap_qkv = col("tap_qkv", "p (t n) -> p t n", t=3)
        tap_b = col("tap_b", "p (t n) -> p t n", t=3)
        tap_ffn = col("tap_ffn", "p (l t n) -> p l t n", l=2, t=3)
        g_o = col("o_norm")
        w_ba = col("w_ba", "p (k n) -> p k n", k=KD)
        cond = col("cond", "p (k c) -> p k c", k=KD)
        b_ada = col("b_ada", "p (n c) -> p n c", c=2)
        mod_n = mod[:].rearrange("p l s k c -> p (l s k) c")

        (beta, g_log, e_alog, gcs, egc, ekg, etot, negegc, tmp_a, tmp_b, tmp_c, tmp_d) = (
            gates[:, j, :] for j in range(12))

        s_cols = sem("cols_loaded")
        s_x = sem("x_loaded")
        s_const = sem("const_loaded")
        s_pe = sem("pe_loaded")
        s_state = sem("state_loaded")
        s_inv = sem("inv_loaded")
        s_raw = [sem(f"weights_loaded{s}") for s in range(2)]
        s_ada = [sem(f"ada_loaded{s}") for s in range(2)]
        s_go = sem("units_begun")
        s_whi = sem("weights_hi")
        s_split = sem("weights_split")
        s_unit = sem("units_multiplied")
        s_ev = {n: sem(f"pair{n}_read") for n in "ABC"}
        s_ada_pe = sem("ada_multiplied")
        s_mod = sem("mod_written")
        s_silu_c = sem("silu_c_ready")
        s_fill = sem("constants_filled")
        s_x0 = sem("x_with_positions")
        s_sq = sem("squares_ready")
        s_acc = sem("squares_added")
        s_norm = sem("square_sums")
        s_rstd = sem("rstd_ready")
        s_a = sem("normed_ready")
        s_aff = sem("modulated")
        s_hi = sem("h_hi_ready")
        s_h = sem("h_ready")
        s_conv = sem("convs_done")
        s_silu = sem("silus_done")
        s_hid_hi = sem("hidden_hi_ready")
        s_hid = sem("hidden_ready")
        s_dve = sem("dve_steps")
        s_act = sem("act_steps")
        s_out = sem("outputs_written")
        s_ychunk = sem("y_chunks")
        s_fold = sem("scales_folded")
        s_lmask = sem("level_masks_loaded")
        s_nst = sem("new_states_written")
        s_zero = sem("prompt_states_zero")
        s_pm = sem("pool_products")
        s_mixed = sem("pool_mixed")
        s_l2sq = sem("qk_squares")
        s_l2sum = sem("qk_square_sums")
        s_l2r = sem("qk_rsqrt")
        s_l2 = sem("qk_normed")
        s_ba = sem("beta_alpha_products")
        s_ga = sem("gate_steps_scalar")
        s_gd = sem("gate_steps_vector")
        s_gsum = sem("gate_sums")
        s_tr = sem("kv_transposed")
        s_tok = sem("kv_tokens_copied")
        s_gram = sem("gram_products")
        s_tg = [sem(f"tri_g{c}") for c in range(2)]
        s_bc = [sem(f"gc_rows{c}") for c in range(2)]
        s_dd = [sem(f"decay_arg{c}") for c in range(2)]
        s_dx = [sem(f"decay_exp{c}") for c in range(2)]
        s_mt = [sem(f"mt_ready{c}") for c in range(2)]
        s_at = [sem(f"attn_masked{c}") for c in range(2)]
        s_bt = [sem(f"level_block{c}") for c in range(2)]
        s_y = [sem(f"bt_product{c}") for c in range(2)]
        s_yc = [sem(f"bt_product_copied{c}") for c in range(2)]
        s_z = [sem(f"level_products{c}") for c in range(2)]
        s_up = [sem(f"level_updated{c}") for c in range(2)]
        s_kq = [sem(f"scan_kq{c}") for c in range(2)]
        s_r = [sem(f"scan_r{c}") for c in range(2)]
        s_t = [sem(f"scan_t{c}") for c in range(2)]
        s_tr3 = [sem(f"scan_solve{c}") for c in range(2)]
        s_vn = [sem(f"scan_vnew{c}") for c in range(2)]
        s_kg = [sem(f"scan_kg{c}") for c in range(2)]
        s_ap = [sem(f"scan_products{c}") for c in range(2)]
        s_st = [sem(f"scan_state{c}") for c in range(2)]
        s_to = [sem(f"scan_o{c}") for c in range(2)]
        s_orr = sem("o_rsqrt")
        s_on = sem("o_normed")
        s_oT = sem("o_transposed")
        s_oy = sem("o_gated")
        s_yhi = sem("y_hi")
        s_yready = sem("y_ready")

        def level_mask(d, lv):
            return lmask[:, d * LEVELS + lv, :].unsqueeze(1).to_broadcast([P, NH, P])

        def tri_mask(d):
            return (tri_u, tri_l)[d].unsqueeze(1).to_broadcast([P, NH, P])

        def scan_tile(c, s):
            return NT - 1 if s == NT - 1 else (s if c == 0 else NT - 2 - s)

        def first_visit(c, s):
            return s == NT - 1 and c == 0 or s < (NT - 1) // 2

        done_visits = [(c, s) for s in range(NT) for c in range(2) if not first_visit(c, s)]
        done_order = [scan_tile(c, s) for c, s in done_visits]

        block = ctx.enter_context(nc.Block())

        @block.sync
        def _(sp):
            def load(u, s, src, n=SLOT):
                sp.wait_ge(s_split, u - 1)
                sp.dma_start(raw[s][:, 0:n], src).then_inc(s_raw[s], 16)

            def load_ada(n, s):
                sp.wait_ge(s_ada_pe, n - 1)
                sp.dma_start(ada_raw[s][:], t["w_ada"][n]).then_inc(s_ada[s], 16)

            sp.dma_start(cols[:], t["cols"]).then_inc(s_cols, 16)
            sp.dma_start(const[:], t["const"]).then_inc(s_const, 16)
            for s in range(2):
                sp.dma_start(ada_raw[s][:], t["w_ada"][s]).then_inc(s_ada[s], 16)
            sp.dma_start(x[:], t["x"]).then_inc(s_x, 16)
            sp.dma_start(pe_tab[:], t["pe"]).then_inc(s_pe, 16)
            with sp.Fori(1, 8) as i:
                for s in range(2):
                    load_ada(i * 2 + s, s)
            for s in range(2):
                sp.dma_start(raw[s][:], t["w_in"][s]).then_inc(s_raw[s], 16)
            for s in range(2):
                load_ada(16 + s, s)
            with sp.Fori(1, 14) as i:
                for s in range(2):
                    load(i * 2 + s, s, t["w_in"][i * 2 + s])
                for s in range(2):
                    load_ada(i * 2 + 16 + s, s)
            sp.wait_ge(s_x0, KD)
            sp.dma_start(lmask[:], t["lmask"]).then_inc(s_lmask, 16)
            u = SEG["out"]["u"]
            for s in range(2):
                load(u + s, s, t["w_out"][s])
            for n in range(44, 48):
                load_ada(n, n % 2)
            for c in range(2):
                sp.wait_ge(s_y[c], LEVELS * NT)
                sp.dma_start(ss[c], t["state"][:, c]).then_inc(s_state, 16)
            for c in range(2):
                sp.wait_ge(s_st[c], NT)
                sp.dma_start(t["new_state"][:, c], sp_[c]).then_inc(s_nst, 16)
            with sp.Fori(1, 4) as i:
                for s in range(2):
                    load(i * 2 + (u + s), s, t["w_out"][i * 2 + s])
            for layer in range(2):
                if layer == 1:
                    u = SEG["pool"]["u"]
                    for s in range(2):
                        load(u + s, s, t["w_pool"][s])
                for g, nf in enumerate(GROUPS):
                    u = SEG["up", layer, g]["u"]
                    f0 = layer * NF + GROUP_AT[g]
                    with sp.Fori(0, nf) as i:
                        for s in range(2):
                            load(i * 2 + (u + s), s, t["w_gu"][i * 2 + (2 * f0 + s)])
                        if layer == 0:
                            for s in range(2):
                                load_ada(i * 2 + (48 + 2 * GROUP_AT[g] + s), s)
                    if layer == 0 and g == 0:
                        sp.wait_ge(s_unit, SEG["up", 0, 0]["u"])
                        sp.dma_start(inv_n[:], t["inv_n"]).then_inc(s_inv, 16)
                    if layer == 0 and g == 2:
                        for n in range(48 + 2 * NF, 96):
                            load_ada(n, n % 2)
                    u = SEG["down", layer, g]["u"]
                    with sp.Fori(0, 4) as i:
                        for s in range(2):
                            load(i * 2 + (u + s), s, t[f"w_dn{g}"][i * 2 + (8 * layer + s)], nf * P)
            for k in range(KD):
                sp.wait_ge(s_ychunk, k + 1)
                for (c0, n, cd) in RANGES:
                    sp.dma_start(t["y"][:, k, SEQ_S * cd:SEQ_S * cd + n], yout[:, k, c0:c0 + n]).then_inc(s_out, 16)
            sp.wait_ge(s_out, 16 * 2 * KD)
            sp.wait_ge(s_nst, 32)

        @block.gpsimd
        def _(pool):
            def split(u, half_u, s, n=SLOT, guard=True):
                pool.wait_ge(s_raw[s], half_u * 16 + 16)
                if guard:
                    pool.wait_ge(s_unit, u - 1)
                pool.sem_inc(s_go, 1)
                nc.gpsimd.tensor_scalar(whi[s][:, 0:n], raw[s][:, 0:n], 1.0, 0.0,
                                        ALU.mult, ALU.add).then_inc(s_whi, 1)
                pool.wait_ge(s_whi, u + 1)
                nc.gpsimd.tensor_tensor(wlo[s][:, 0:n], raw[s][:, 0:n], whi[s][:, 0:n].bitcast(F32),
                                        ALU.subtract).then_inc(s_split, 1)

            def split_pairs(u, n_pairs, n=SLOT, first=0):
                with pool.Fori(first, n_pairs) as i:
                    for s in range(2):
                        split(i * 2 + (u + s), i + u // 2, s, n)

            for s in range(2):
                split(s, 0, s, guard=False)
            split_pairs(0, 14, first=1)
            u = SEG["out"]["u"]
            for s in range(2):
                split(u + s, u // 2, s)
            pool.wait_ge(s_lmask, 16)
            for n in range(NT):
                for lv in range(LEVELS):
                    for c in range(2):
                        if lv == 0:
                            pool.wait_ge(s_mt[c], n + 1)
                        if LEVELS * n + lv >= 2:
                            pool.wait_ge(s_y[c], LEVELS * n + lv - 1)
                        if lv == 2:
                            pool.wait_ge(s_up[c], LEVELS * n + 1)
                        nc.gpsimd.tensor_tensor(bt[c][(LEVELS * n + lv) % 2], mt[c], level_mask(c, lv),
                                                ALU.mult).then_inc(s_bt[c], 1)
                        if lv == 0:
                            a = attn[:, 2 * n + c]
                            nc.gpsimd.tensor_tensor(a, a, tri_mask(c), ALU.mult).then_inc(s_at[c], 1)
            for s in range(NT):
                for c in range(2):
                    if s == 0:
                        pool.wait_ge(s_up[c], LEVELS * NT)
                        pool.wait_ge(s_y[c], LEVELS * NT)
                        pool.wait_ge(s_z[c], (LEVELS - 1) * NT)
                    else:
                        pool.wait_ge(s_ap[c], s)
                    tl = scan_tile(c, s)
                    for h in range(NH):
                        j = tl * 8 + c * NH + h
                        last = nc.gpsimd.tensor_scalar(kg[c][:, h], ktok[:, tl, h], ekg[:, j:j + 1], 1.0,
                                                       ALU.mult, ALU.mult)
                    last.then_inc(s_kg[c], 1)
            split_pairs(u, 4, first=1)
            for layer in range(2):
                if layer == 1:
                    split_pairs(SEG["pool"]["u"], 1)
                for g, nf in enumerate(GROUPS):
                    split_pairs(SEG["up", layer, g]["u"], nf)
                    split_pairs(SEG["down", layer, g]["u"], 4, nf * P)

        @block.tensor
        def _(pe):
            def products(pr, s, tiles, hi, lo, ks, wait_k=None):
                last = None
                for j, (tile, k) in enumerate(zip(tiles, ks)):
                    if wait_k is not None:
                        wait_k(j)
                    cs = slice(tile * P, tile * P + P)
                    for q, (wt, act) in enumerate(((whi, hi), (whi, lo), (wlo, hi))):
                        for b in range(2):
                            last = nc.tensor.matmul(pair[pr][:, b], wt[s][:, cs],
                                                    act[:, k, b * HALF:(b + 1) * HALF],
                                                    start=(j == 0 and q == 0),
                                                    stop=(j == len(tiles) - 1 and q == 2))
                return last

            def ada(n, half_n, s, guard=True):
                pe.wait_ge(s_ada[s], half_n * 16 + 16)
                if guard:
                    pe.wait_ge(s_mod, n - 1)
                for k in range(KD):
                    last = nc.tensor.matmul(ada_ps[s], ada_raw[s][:, k * P:(k + 1) * P], silu_c[:, k, :],
                                            start=(k == 0), stop=(k == KD - 1))
                last.then_inc(s_ada_pe, 1)

            def norm_sums(q):
                pe.wait_ge(s_acc, 9 * (q + 1))
                pe.wait_ge(s_mod, (16, 48, 96, 96, 96)[q])
                for b in range(2):
                    last = nc.tensor.matmul(pair["X"][:, b], ones, acc[:, b * HALF:(b + 1) * HALF],
                                            start=True, stop=True)
                last.then_inc(s_norm, 1)

            pe.wait_ge(s_silu_c, 1)
            for s in range(2):
                ada(s, 0, s, guard=False)
            with pe.Fori(1, 8) as i:
                for s in range(2):
                    ada(i * 2 + s, i, s)
            pe.wait_ge(s_const, 16)
            norm_sums(0)

            with pe.Fori(0, 14) as i:
                for s in range(2):
                    pe.wait_ge(s_split, i * 2 + (s + 1))
                    pe.wait_ge(s_ev["AB"[s]], i)
                    wait_k = (lambda j: pe.wait_ge(s_h, j + 1)) if s == 0 else None
                    products("AB"[s], s, range(KD), hhi, hlo, range(KD), wait_k).then_inc(s_unit, 1)
                for s in range(2):
                    ada(i * 2 + 16 + s, i + 8, s)
            for n in range(44, 48):
                ada(n, n // 2, n % 2)
            pe.wait_ge(s_mod, 48)
            for tl, c0 in enumerate(TILES):
                for k in range(KD):
                    for q, (a, b) in enumerate(((hhi, wba_hi), (hhi, wba_lo), (hlo, wba_hi))):
                        last = nc.tensor.matmul(ps[:, 7, 16 * tl:16 * tl + 16], a[:, k, c0:c0 + P], b[:, k, :],
                                                start=(k == 0 and q == 0), stop=(k == KD - 1 and q == 2))
            last.then_inc(s_ba, 1)
            for u in range(8):
                pe.wait_ge(s_l2sq, u + 1)
                if u < 2:
                    pe.wait_ge(s_ev["AB"[u]], 14)
                else:
                    pe.wait_ge(s_l2r, u - 1)
                for b in range(2):
                    last = nc.tensor.matmul(pair["AB"[u % 2]][:, b], ones, sq[u % 2][:, b * HALF:(b + 1) * HALF],
                                            start=True, stop=True)
                last.then_inc(s_l2sum, 1)
            pe.wait_ge(s_gd, 5)
            gv = g_log.rearrange("p (t j) -> p t j", t=NT)
            gps = ps[:, 7, 128:168].rearrange("p (t j) -> p t j", t=NT)
            for d in range(2):
                nc.tensor.matmul(gps[:, :, 4 * d:4 * d + 4], (tri_u, tri_l)[d], gv[:, :, 4 * d:4 * d + 4],
                                 start=True, stop=True)
            nc.tensor.matmul(ps[:, 7, 192:232], ones, g_log, start=True, stop=True).then_inc(s_gsum, 1)

            pe.wait_ge(s_l2, 8)
            for n in range(NT):
                c0 = TILES[n]
                for j, (dst, ch) in enumerate(((6, 4), (7, 8))):
                    if n == 0:
                        pe.wait_ge(s_ga, 9)
                    else:
                        pe.wait_ge(s_tok, 2 * n - 1 + j)
                    for h in range(NH):
                        last = nc.tensor.transpose(bank[dst][:, h], qkv[:, ch + h, c0:c0 + P], ident)
                    last.then_inc(s_tr, 1)
                if n:
                    pe.wait_ge(s_up[1], LEVELS * n)
                else:
                    pe.wait_ge(s_l2r, 8)
                for h in range(NH):
                    kt = qkv[:, 4 + h, c0:c0 + P]
                    nc.tensor.matmul(bank[0][:, h], kt, kt, start=True, stop=True)
                for h in range(NH):
                    last = nc.tensor.matmul(bank[1][:, h], qkv[:, 4 + h, c0:c0 + P], qkv[:, h, c0:c0 + P],
                                            start=True, stop=True)
                last.then_inc(s_gram, 1)
                for c in range(2):
                    pe.wait_ge(s_tg[c], n + 1)
                    if n:
                        pe.wait_ge(s_yc[c], (LEVELS - 1) * n)
                    nc.tensor.matmul(bank[2 + c], ones, dec[c], start=True, stop=True).then_inc(s_bc[c], 1)
                for lv in range(LEVELS):
                    for c in range(2):
                        pe.wait_ge(s_bt[c], LEVELS * n + lv + 1)
                        if lv == 0:
                            pe.wait_ge(s_dd[c], n + 1)
                        else:
                            pe.wait_ge(s_up[c], LEVELS * n + lv)
                            if lv > 1:
                                pe.wait_ge(s_yc[c], (LEVELS - 1) * n + lv - 1)
                        for h in range(NH):
                            last = nc.tensor.matmul(bank[2 + c][:, h], bt[c][(LEVELS * n + lv) % 2][:, h],
                                                    ident if lv == 0 else tt[c][:, h], start=True, stop=True)
                        last.then_inc(s_y[c], 1)
                    if lv == 0:
                        continue
                    for c in range(2):
                        zb, ztb = ((4, 5), (0, 1))[c]
                        if lv == 1 and c == 1:
                            for cc in range(2):
                                pe.wait_ge(s_mt[cc], n + 1)
                        pe.wait_ge(s_yc[c], (LEVELS - 1) * n + lv)
                        for h in range(NH):
                            if lv < LEVELS - 1:
                                nc.tensor.matmul(bank[zb][:, h], rinv[:, 2 * n + c, h], ys[c][:, h],
                                                 start=True, stop=True)
                            last = nc.tensor.matmul(bank[ztb][:, h], ys[c][:, h], rinv[:, 2 * n + c, h],
                                                    start=True, stop=True)
                        last.then_inc(s_z[c], 1)

            for s in range(NT):
                for c in range(2):
                    tl = scan_tile(c, s)
                    c0 = TILES[tl]
                    b0 = 4 * c
                    S = ss[c] if s < NT - 1 else sp_[c]
                    if s == 0:
                        pe.wait_ge(s_state, 32)
                        for cc in range(2):
                            pe.wait_ge(s_up[cc], LEVELS * NT)
                        pe.wait_ge(s_tok, 2 * NT)
                    elif s == NT - 1:
                        pe.wait_ge(s_zero, 2)
                        pe.wait_ge(s_vn[c], s)
                    else:
                        pe.wait_ge(s_st[c], s)
                    if s:
                        pe.wait_ge(s_t[c], s)
                    for h in range(NH):
                        nc.tensor.matmul(bank[b0][:, h], qkv[:, 4 + h, c0:c0 + P], S[:, h],
                                         start=True, stop=True)
                    for h in range(NH):
                        last = nc.tensor.matmul(bank[b0 + 1][:, h], qkv[:, h, c0:c0 + P], S[:, h],
                                                start=True, stop=True)
                    last.then_inc(s_kq[c], 1)
                for c in range(2):
                    tl = scan_tile(c, s)
                    pe.wait_ge(s_r[c], s + 1)
                    for h in range(NH):
                        last = nc.tensor.matmul(bank[4 * c][:, h], rinv[:, 2 * tl + c, h], rr[c][:, h],
                                                start=True, stop=True)
                    last.then_inc(s_tr3[c], 1)
                for c in range(2):
                    tl = scan_tile(c, s)
                    pe.wait_ge(s_vn[c], s + 1)
                    pe.wait_ge(s_kg[c], s + 1)
                    pe.wait_ge(s_at[c], NT)
                    if s:
                        pe.wait_ge(s_to[c], s)
                    for h in range(NH):
                        nc.tensor.matmul(bank[4 * c + 2][:, h], kg[c][:, h], vn[c][:, h], start=True, stop=True)
                    for h in range(NH):
                        last = nc.tensor.matmul(bank[4 * c + 3][:, h], attn[:, 2 * tl + c, h], vn[c][:, h],
                                                start=True, stop=True)
                    last.then_inc(s_ap[c], 1)
            for n in range(NT):
                pe.wait_ge(s_on, n + 1)
                if n >= 2:
                    pe.wait_ge(s_oy, n - 1)
                for h in range(NH):
                    last = nc.tensor.transpose(bank[n % 2][:, h], osum[:, done_order[n], h], ident)
                last.then_inc(s_oT, 1)

            def accumulate(seg, nf, hi, lo, ready):
                b = SEG[seg]
                with pe.Fori(0, 4) as i:
                    for s in range(2):
                        n = "CB"[s]
                        pe.wait_ge(s_split, i * 2 + (b["u"] + s + 1))
                        pe.wait_ge(s_ev[n], i + b[n])
                        products(n, s, range(nf), hi, lo, range(nf), ready if s == 0 else None)\
                            .then_inc(s_unit, 1)

            pe.wait_ge(s_yready, NB + NT)
            accumulate("out", KD, hhi, hlo, None)
            norm_sums(1)

            for layer in range(2):
                if layer == 1:
                    b = SEG["pool"]
                    for m in range(KD):
                        n = "CB"[m % 2]
                        if m % 4 == 0:
                            pe.wait_ge(s_split, b["u"] + m // 4 + 1)
                        pe.wait_ge(s_ev[n], b[n] + m // 2)
                        pe.wait_ge(s_h, 16 + 2 * (m // 2) + 2)
                        last = products(n, m // 4, (2 * (m % 4), 2 * (m % 4) + 1), hhi, hlo,
                                        (2 * (m // 2), 2 * (m // 2) + 1))
                        last.then_inc(s_unit if m % 4 == 3 else s_pm, 1)
                    norm_sums(3)
                for g, nf in enumerate(GROUPS):
                    b = SEG["up", layer, g]
                    hr = 8 if layer == 0 else 24
                    with pe.Fori(0, nf) as i:
                        for s in range(2):
                            pe.wait_ge(s_split, i * 2 + (b["u"] + s + 1))
                            pe.wait_ge(s_ev["AB"[s]], i + b["AB"[s]])
                            wait_k = (lambda j: pe.wait_ge(s_h, hr + j + 1)) if s == 0 and g == 0 else None
                            products("AB"[s], s, range(KD), hhi, hlo, range(KD), wait_k).then_inc(s_unit, 1)
                        if layer == 0:
                            for s in range(2):
                                ada(i * 2 + (48 + 2 * GROUP_AT[g] + s), i + (24 + GROUP_AT[g]), s)
                    if layer == 0 and g == 2:
                        for n in range(48 + 2 * NF, 96):
                            ada(n, n // 2, n % 2)
                    f = b["f"]
                    accumulate(("down", layer, g), nf, hidhi, hidlo, lambda j: pe.wait_ge(s_hid, f + j + 1))
                norm_sums(2 if layer == 0 else 4)

        @block.scalar
        def _(act):
            own = Steps(act, s_act)

            def rsqrt_of_sums(q):
                act.wait_ge(s_norm, q + 1)
                if q:
                    act.wait_ge(s_a, 8 * q)
                own.tick(nc.scalar.activation(halves(rstd), pair["X"], ACT.Ln, bias=eps_col, scale=1.0 / D))
                own.sync()
                nc.scalar.activation(rstd, rstd, ACT.Exp, scale=-0.5).then_inc(s_rstd, 1)

            def modulate(q, layer, part):
                rsqrt_of_sums(q)
                aff = 8 * q
                hi0 = (0, 8, None, 24)[q]
                with act.Fori(0, 4) as i:
                    for s in range(2):
                        k = i * 2 + s
                        act.wait_ge(s_a, i * 2 + (8 * q + s + 1))
                        act.wait_ge(s_h, i * 2 + hi0)
                        for c0, n, cd in RANGES:
                            last = nc.scalar.activation(h32[s][:, c0:c0 + n], pad[s][:, c0:c0 + n], ACT.Identity,
                                                        bias=mod[:, layer, 3 * part, ds(k, 1), cd],
                                                        scale=mod[:, layer, 3 * part + 1, ds(k, 1), cd])
                        last.then_inc(s_aff, 1)
                        act.wait_ge(s_aff, i * 2 + (aff + s + 1))
                        nc.scalar.activation(hhi[:, k, :], h32[s], ACT.Copy).then_inc(s_hi, 1)

            def squares(q, name_of, base):
                with act.Fori(0, 4) as i:
                    for s in range(2):
                        act.wait_ge(name_of[s], i * base[s][1] + (base[s][0] + 1))
                        act.wait_ge(s_acc, i * 2 + (9 * q + 1))
                        nc.scalar.activation(sq[s], x[:, i * 2 + s, :], ACT.Square).then_inc(s_sq, 1)

            def squares_after(q, seg):
                b = SEG[seg]
                squares(q, (s_ev["C"], s_ev["B"]), ((b["C"], 1), (b["B"], 1)))

            act.wait_ge(s_cols, 16)
            nc.scalar.activation(silu_c[:], cond, ACT.Silu).then_inc(s_silu_c, 1)
            squares(0, (s_x0, s_x0), ((0, 2), (1, 2)))
            act.wait_ge(s_fold, 1)
            modulate(0, 0, 0)

            with act.Fori(0, NQKV // 2) as i:
                for s in range(2):
                    act.wait_ge(s_unit, i * 2 + (s + 1))
                    act.wait_ge(s_conv, i * 2)
                    nc.scalar.activation(halves(pad[s]), pair["AB"[s]], ACT.Copy).then_inc(s_ev["AB"[s]], 1)
                    act.wait_ge(s_conv, i * 2 + (s + 1))
                    nc.scalar.activation(qkv[:, i * 2 + s, :], cv[s], ACT.Silu).then_inc(s_silu, 1)
            with act.Fori(0, NGATE // 2) as i:
                for s in range(2):
                    act.wait_ge(s_unit, i * 2 + (NQKV + s + 1))
                    nc.scalar.activation(halves(sgate[:, i * 2 + s, :]), pair["AB"[s]], ACT.Silu)\
                        .then_inc(s_ev["AB"[s]], 1)
            with act.Fori(0, 2) as i:
                for s in range(2):
                    act.wait_ge(s_unit, i * 6 + (NQKV + NGATE + 3 * s + 1))
                    act.wait_ge(s_ev["BA"[s]], i * 3 + (6 + 2 * s))
                    nc.scalar.activation(halves(h32[s]), pair["AB"[s]], ACT.Copy).then_inc(s_ev["AB"[s]], 1)

            act.wait_ge(s_ba, 1)
            act.wait_ge(s_fill, 3)
            bav = ps[:, 7, 0:16 * NT].rearrange("p (t j) -> p t j", t=NT)

            def tiles(v):
                return v.rearrange("p (t j) -> p t j", t=NT)
            nc.scalar.activation(tiles(tmp_a), bav[:, :, 0:8], ACT.Exp, scale=-1.0).then_inc(s_ga, 1)
            nc.scalar.activation(e_alog, col("a_log"), ACT.Exp).then_inc(s_ga, 1)
            act.wait_ge(s_gd, 1)
            nc.scalar.activation(tmp_c, tmp_b, ACT.Abs).then_inc(s_ga, 1)
            act.wait_ge(s_ga, 3)
            nc.scalar.activation(tmp_c, tmp_c, ACT.Exp, scale=-1.0).then_inc(s_ga, 1)
            act.wait_ge(s_ga, 4)
            nc.scalar.activation(tmp_c, tmp_c, ACT.Ln, bias=1.0).then_inc(s_ga, 1)
            for u in range(8):
                act.wait_ge(s_silu, NQKV)
                if u >= 2:
                    act.wait_ge(s_l2sum, u - 1)
                else:
                    act.wait_ge(s_acc, 9)
                nc.scalar.activation(sq[u % 2], qkv[:, u, :], ACT.Square).then_inc(s_l2sq, 1)
                act.wait_ge(s_l2sum, u + 1)
                if u >= 2:
                    act.wait_ge(s_l2, u - 1)
                own.tick(nc.scalar.activation(halves(pad[u % 2]), pair["AB"[u % 2]], ACT.Ln, bias=eps_col))
                own.sync()
                nc.scalar.activation(pad[u % 2], pad[u % 2], ACT.Exp, scale=-0.5,
                                     bias=scale_col if u < 4 else 0.0).then_inc(s_l2r, 1)
            act.wait_ge(s_gsum, 1)
            nc.scalar.activation(gcs, ps[:, 7, 128:168], ACT.Copy).then_inc(s_ga, 1)
            nc.scalar.activation(egc, ps[:, 7, 128:168], ACT.Exp).then_inc(s_ga, 1)
            nc.scalar.activation(etot, ps[:, 7, 192:232], ACT.Exp).then_inc(s_ga, 1)
            nc.scalar.activation(tmp_c, ps[:, 7, 192:232], ACT.Copy).then_inc(s_ga, 1)
            act.wait_ge(s_gd, 6)
            nc.scalar.activation(ekg, tmp_a, ACT.Exp).then_inc(s_ga, 1)

            for n in range(NT):
                for j, dst in enumerate((ktok, vtok)):
                    act.wait_ge(s_tr, 2 * n + j + 1)
                    nc.scalar.activation(dst[:, n], bank[6 + j], ACT.Copy).then_inc(s_tok, 1)
                for c in range(2):
                    act.wait_ge(s_dd[c], n + 1)
                    nc.scalar.activation(dec[c], dec[c], ACT.Exp).then_inc(s_dx[c], 1)
                for lv in range(1, LEVELS):
                    for c in range(2):
                        act.wait_ge(s_y[c], LEVELS * n + lv + 1)
                        if (LEVELS - 1) * n + lv > 1:
                            act.wait_ge(s_z[c], (LEVELS - 1) * n + lv - 1)
                        nc.scalar.activation(ys[c], bank[2 + c], ACT.Copy).then_inc(s_yc[c], 1)
            for s in range(NT):
                for c in range(2):
                    act.wait_ge(s_kq[c], s + 1)
                    if s:
                        act.wait_ge(s_to[c], s)
                    tl = scan_tile(c, s)
                    for h in range(NH):
                        j = tl * 8 + c * NH + h
                        last = nc.scalar.activation(to[c][:, h], bank[4 * c + 1][:, h], ACT.Copy,
                                                    scale=egc[:, j:j + 1])
                    last.then_inc(s_t[c], 1)
            for n in range(NT):
                c, s = done_visits[n]
                act.wait_ge(s_to[c], s + 1)
                for h in range(NH):
                    if n or h:
                        own.sync()
                    own.tick(nc.scalar.activation(junk[:], osum[:, done_order[n], h], ACT.Square,
                                                  accum_out=ssq[:, 0, n * NH + h:n * NH + h + 1]))
            own.sync()
            own.tick(nc.scalar.activation(ssq[:, 1], ssq[:, 0], ACT.Ln, bias=eps_col, scale=1.0 / DK))
            own.sync()
            nc.scalar.activation(ssq[:, 1], ssq[:, 1], ACT.Exp, scale=-0.5).then_inc(s_orr, 1)
            for j in range(NB):
                nc.scalar.activation(hhi[:, 4 + j, :], yb[:, j, :], ACT.Copy).then_inc(s_yhi, 1)
            for n in range(NT):
                act.wait_ge(s_oy, n + 1)
                c0 = TILES[done_order[n]]
                nc.scalar.activation(hhi[:, 0:NH, c0:c0 + P], chain[n % 2][0], ACT.Copy).then_inc(s_yhi, 1)

            squares_after(1, "out")
            modulate(1, 0, 1)
            for layer in range(2):
                if layer == 1:
                    rsqrt_of_sums(2)

                    def pool_modulate(k):
                        act.wait_ge(s_a, 16 + k + 1)
                        for (pc, c0, n, cd) in POOL_RANGES:
                            last = nc.scalar.activation(hp[:, k, pc:pc + n], pad[k % 2][:, c0:c0 + n], ACT.Identity,
                                                        bias=mod[:, 1, 0, k, cd:cd + 1],
                                                        scale=mod[:, 1, 1, k, cd:cd + 1])
                        last.then_inc(s_aff, 1)

                    pool_modulate(0)
                    for k in range(KD):
                        if k + 1 < KD:
                            pool_modulate(k + 1)
                        act.wait_ge(s_mixed, k + 1)
                        nc.scalar.activation(hhi[:, k, :], h32[k % 2], ACT.Copy).then_inc(s_hi, 1)
                    squares_after(3, "pool")
                    modulate(3, 1, 1)
                for g, nf in enumerate(GROUPS):
                    b = SEG["up", layer, g]
                    u, f = b["u"], b["f"]
                    with act.Fori(0, nf) as i:
                        act.wait_ge(s_unit, i * 2 + (u + 1))
                        act.wait_ge(s_conv, i + (NQKV + NB + f))
                        nc.scalar.activation(halves(pad[0]), pair["A"], ACT.Copy).then_inc(s_ev["A"], 1)
                        act.wait_ge(s_conv, i + (NQKV + NB + f + 1))
                        act.wait_ge(s_ev["B"], i + b["B"])
                        nc.scalar.activation(cv[1], cv[0], ACT.Silu).then_inc(s_silu, 1)
                        act.wait_ge(s_ev["B"], i + (b["B"] + 1))
                        nc.scalar.activation(hidhi[:, i, :], h32[0], ACT.Copy).then_inc(s_hid_hi, 1)
                squares_after(2 if layer == 0 else 4, ("down", layer, 2))
            rsqrt_of_sums(4)

        @block.vector
        def _(dve):
            own = Steps(dve, s_dve)

            def add_squares(i, q, s):
                dve.wait_ge(s_sq, i * 2 + (8 * q + s + 1))
                dve.wait_ge(s_acc, i * 2 + (9 * q + s + 1))
                nc.vector.tensor_tensor(acc, acc, sq[s], ALU.add).then_inc(s_acc, 1)

            def clear_acc(q):
                if q:
                    dve.wait_ge(s_norm, q)
                nc.vector.memset(acc, 0.0).then_inc(s_acc, 1)

            def update_x(seg, layer, part, q=None):
                b = SEG[seg]
                if q is not None:
                    clear_acc(q)
                with dve.Fori(0, 4) as i:
                    for s in range(2):
                        n = "CB"[s]
                        k = i * 2 + s
                        dve.wait_ge(s_unit, i * 2 + (b["u"] + s + 1))
                        for bk, pc, ln, xc, cd in PIECES:
                            last = nc.vector.scalar_tensor_tensor(
                                out=x[:, k, xc:xc + ln], in0=pair[n][:, bk, pc:pc + ln],
                                scalar=mod[:, layer, 3 * part + 2, ds(k, 1), cd],
                                in1=x[:, k, xc:xc + ln], op0=ALU.mult, op1=ALU.add)
                        last.then_inc(s_ev[n], 1)
                    if q is not None:
                        for s in range(2):
                            add_squares(i, q, s)

            def add_mod(n, s, guard=True):
                dve.wait_ge(s_ada_pe, n + 1)
                nc.vector.tensor_tensor(mod_n[:, n, :], ada_ps[s], b_ada[:, n, :], ALU.add).then_inc(s_mod, 1)

            def fold_scale(layer, part, g):
                v = mod[:, layer, 3 * part + 1]
                return nc.vector.scalar_tensor_tensor(out=v, in0=v, scalar=1.0, in1=g[:, layer],
                                                      op0=ALU.add, op1=ALU.mult)

            def apply_norm(q, lo0):
                dve.wait_ge(s_rstd, q + 1)
                with dve.Fori(0, 4) as i:
                    for s in range(2):
                        if q:
                            dve.wait_ge(s_aff, i * 2 + 8 * q)
                        else:
                            dve.wait_ge(s_aff, i * 2)
                        nc.vector.tensor_tensor(pad[s], x[:, i * 2 + s, :], rstd, ALU.mult).then_inc(s_a, 1)
                    if lo0 is not None:
                        for s in range(2):
                            k = i * 2 + s
                            dve.wait_ge(s_hi, k + lo0 + 1)
                            nc.vector.tensor_tensor(hlo[:, k, :], h32[s], hhi[:, k, :].bitcast(F32),
                                                    ALU.subtract).then_inc(s_h, 1)

            def conv(src, dst, taps, per=2):
                own.tick(nc.vector.tensor_scalar(dst[:, 1:W - 1], src[:, 1:W - 1], taps[1], None, ALU.mult))
                own.sync()
                own.tick(nc.vector.scalar_tensor_tensor(out=dst[:, 1:W - 1], in0=src[:, 0:W - 2], scalar=taps[0],
                                                        in1=dst[:, 1:W - 1], op0=ALU.mult, op1=ALU.add))
                own.sync()
                nc.vector.scalar_tensor_tensor(out=dst[:, 1:W - 1], in0=src[:, 2:W], scalar=taps[2],
                                               in1=dst[:, 1:W - 1], op0=ALU.mult, op1=ALU.add)\
                    .then_inc(s_conv, 1)

            def zero_pads(bufs):
                for v in bufs:
                    for a, b in ((0, S0), (S0 + SEQ_S, P0), (P0 + SEQ_P, W)):
                        last = nc.vector.memset(v[:, a:b], 0.0)
                return last

            nc.vector.memset(eps_col, EPS).then_inc(s_fill, 1)
            nc.vector.memset(scale_col, -0.5 * float(np.log(DK))).then_inc(s_fill, 1)
            zero_pads(h32 + cv).then_inc(s_fill, 1)
            clear_acc(0)
            dve.wait_ge(s_x, 16)
            dve.wait_ge(s_pe, 16)
            with dve.Fori(0, KD // 2) as i:
                for s in range(2):
                    k = i * 2 + s
                    nc.vector.tensor_tensor(x[:, k, S0:S0 + SEQ_S], x[:, k, S0:S0 + SEQ_S], pe_tab[:, k, :],
                                            ALU.add).then_inc(s_x0, 1)
                for s in range(2):
                    add_squares(i, 0, s)
            dve.wait_ge(s_cols, 16)
            own.tick(nc.vector.tensor_copy(wba_hi[:], w_ba))
            own.sync()
            own.tick(nc.vector.tensor_tensor(wba_lo[:], w_ba, wba_hi[:].bitcast(F32), ALU.subtract))
            with dve.Fori(0, 8) as i:
                for s in range(2):
                    add_mod(i * 2 + s, s)
            dve.wait_ge(s_mod, 16)
            fold_scale(0, 0, g_mix).then_inc(s_fold, 1)
            apply_norm(0, 0)

            with dve.Fori(0, NQKV // 2) as i:
                own.enter(i, 4)
                for s in range(2):
                    dve.wait_ge(s_ev["AB"[s]], i + 1)
                    dve.wait_ge(s_silu, i * 2)
                    conv(pad[s], cv[s], [tap_qkv[:, j, ds(i * 2 + s, 1)] for j in range(3)])
                for s in range(2):
                    add_mod(i * 2 + (16 + s), s)
            own.leave(NQKV // 2)
            with dve.Fori(0, NGATE // 2) as i:
                for s in range(2):
                    add_mod(i * 2 + (16 + NQKV + s), s)
            dve.wait_ge(s_silu, NQKV)
            with dve.Fori(0, 2) as i:
                own.enter(i, 4)
                for s in range(2):
                    u0 = NQKV + NGATE + 3 * s
                    pc, ph = "AB"[s], "BA"[s]
                    dve.wait_ge(s_ev[pc], i * 3 + (u0 // 2 + 1))
                    dve.wait_ge(s_unit, i * 6 + (u0 + 2))
                    nc.vector.tensor_tensor(halves(pad[s]), halves(h32[s]), pair[ph], ALU.mult)\
                        .then_inc(s_ev[ph], 1)
                    dve.wait_ge(s_ev[ph], i * 3 + ((u0 + 1) // 2 + 1))
                    conv(pad[s], cv[s], [tap_b[:, j, ds(i * 2 + s, 1)] for j in range(3)])
                    dve.wait_ge(s_conv, i * 2 + (NQKV + s + 1))
                    dve.wait_ge(s_unit, i * 6 + (u0 + 3))
                    nc.vector.tensor_tensor(halves(yb[:, i * 2 + s, :]), halves(cv[s]), pair[pc], ALU.mult)\
                        .then_inc(s_ev[pc], 1)
                    if s == 0:
                        for n in range(2):
                            add_mod(i * 6 + (16 + NQKV + NGATE + n), n)
                for n in range(4):
                    add_mod(i * 6 + (16 + NQKV + NGATE + 2 + n), n % 2)
            own.leave(2)

            for n in range(44, 48):
                add_mod(n, n % 2)
            dve.wait_ge(s_ba, 1)
            dve.wait_ge(s_ga, 1)
            bav = ps[:, 7, 0:16 * NT].rearrange("p (t j) -> p t j", t=NT)

            def tiles(v):
                return v.rearrange("p (t j) -> p t j", t=NT)
            nc.vector.tensor_tensor(tiles(tmp_b), bav[:, :, 8:16], tiles(col("dt_bias")), ALU.add).then_inc(s_gd, 1)
            nc.vector.tensor_scalar(tmp_a, tmp_a, 1.0, None, ALU.add).then_inc(s_gd, 1)
            dve.wait_ge(s_gd, 2)
            nc.vector.reciprocal(beta, tmp_a).then_inc(s_gd, 1)
            dve.wait_ge(s_ga, 5)
            nc.vector.scalar_tensor_tensor(out=tmp_d, in0=tmp_b, scalar=0.0, in1=tmp_c,
                                           op0=ALU.max, op1=ALU.add).then_inc(s_gd, 1)
            dve.wait_ge(s_gd, 4)
            nc.vector.scalar_tensor_tensor(out=g_log, in0=tmp_d, scalar=-1.0, in1=e_alog,
                                           op0=ALU.mult, op1=ALU.mult).then_inc(s_gd, 1)
            dve.wait_ge(s_mod, 48)
            fold_scale(0, 1, g_ffn).then_inc(s_fold, 1)
            for u in range(8):
                dve.wait_ge(s_l2r, u + 1)
                nc.vector.tensor_tensor(qkv[:, u, :], qkv[:, u, :], pad[u % 2], ALU.mult).then_inc(s_l2, 1)
            dve.wait_ge(s_ga, 9)
            nc.vector.tensor_tensor(tmp_a, tmp_c, gcs, ALU.subtract).then_inc(s_gd, 1)
            nc.vector.tensor_scalar(negegc, egc, -1.0, None, ALU.mult).then_inc(s_gd, 1)
            dve.wait_ge(s_l2, 8)
            dve.wait_ge(s_gd, 7)

            id4 = ident.unsqueeze(1).to_broadcast([P, NH, P])

            def tri_g(n, c):
                for h in range(NH):
                    j = n * 8 + c * NH + h
                    last = nc.vector.tensor_scalar(dec[c][:, h], (tri_u, tri_l)[c], g_log[:, j:j + 1], None, ALU.mult)
                last.then_inc(s_tg[c], 1)

            for n in range(NT):
                for c in range(2):
                    tri_g(n, c)
                for c in range(2):
                    dve.wait_ge(s_bc[c], n + 1)
                    for h in range(NH):
                        j = n * 8 + c * NH + h
                        last = nc.vector.tensor_scalar(dec[c][:, h], bank[2 + c][:, h], gcs[:, j:j + 1], 0.0,
                                                       ALU.subtract, ALU.min)
                    last.then_inc(s_dd[c], 1)
                dve.wait_ge(s_gram, n + 1)
                for c in range(2):
                    dve.wait_ge(s_dx[c], n + 1)
                    if n:
                        dve.wait_ge(s_bt[c], LEVELS * n)
                    for h in range(NH):
                        j = n * 8 + c * NH + h
                        nc.vector.scalar_tensor_tensor(out=mt[c][:, h], in0=dec[c][:, h], scalar=beta[:, j:j + 1],
                                                       in1=bank[0][:, h], op0=ALU.mult, op1=ALU.mult)
                    nc.vector.tensor_tensor(attn[:, 2 * n + c], dec[c], bank[1], ALU.mult).then_inc(s_mt[c], 1)
                for c in range(2):
                    dve.wait_ge(s_y[c], LEVELS * n + 1)
                    nc.vector.tensor_tensor(tt[c], id4, bank[2 + c], ALU.subtract)
                    nc.vector.tensor_tensor(rinv[:, 2 * n + c], id4, bt[c][(LEVELS * n) % 2], ALU.subtract)\
                        .then_inc(s_up[c], 1)
                for lv in range(1, LEVELS):
                    for c in range(2):
                        zb, ztb = ((4, 5), (0, 1))[c]
                        dve.wait_ge(s_z[c], (LEVELS - 1) * n + lv)
                        if lv < LEVELS - 1:
                            nc.vector.tensor_tensor(tt[c], tt[c], bank[zb], ALU.subtract)
                        r = rinv[:, 2 * n + c]
                        nc.vector.tensor_tensor(r, r, bank[ztb], ALU.subtract).then_inc(s_up[c], 1)

            for c in range(2):
                nc.vector.memset(sp_[c], 0.0).then_inc(s_zero, 1)
            for s in range(NT):
                for c in range(2):
                    tl = scan_tile(c, s)
                    dve.wait_ge(s_kq[c], s + 1)
                    for h in range(NH):
                        j = tl * 8 + c * NH + h
                        last = nc.vector.scalar_tensor_tensor(
                            out=rr[c][:, h], in0=bank[4 * c][:, h], scalar=negegc[:, j:j + 1],
                            in1=vtok[:, tl, h], op0=ALU.mult, op1=ALU.add)
                    last.then_inc(s_r[c], 1)
                for c in range(2):
                    tl = scan_tile(c, s)
                    dve.wait_ge(s_tr3[c], s + 1)
                    for h in range(NH):
                        j = tl * 8 + c * NH + h
                        last = nc.vector.tensor_scalar(vn[c][:, h], bank[4 * c][:, h], beta[:, j:j + 1], None,
                                                       ALU.mult)
                    last.then_inc(s_vn[c], 1)
                for c in range(2):
                    tl = scan_tile(c, s)
                    S = ss[c] if s < NT - 1 else sp_[c]
                    dve.wait_ge(s_ap[c], s + 1)
                    for h in range(NH):
                        j = tl * 8 + c * NH + h
                        last = nc.vector.scalar_tensor_tensor(
                            out=S[:, h], in0=S[:, h], scalar=etot[:, j:j + 1], in1=bank[4 * c + 2][:, h],
                            op0=ALU.mult, op1=ALU.add)
                    last.then_inc(s_st[c], 1)
                for c in range(2):
                    tl = scan_tile(c, s)
                    dve.wait_ge(s_t[c], s + 1)
                    if first_visit(c, s):
                        nc.vector.tensor_tensor(osum[:, tl], to[c], bank[4 * c + 3], ALU.add).then_inc(s_to[c], 1)
                    else:
                        dve.wait_ge(s_to[1 - c], s + 1 if s == NT - 1 else NT - 1 - s)
                        own.tick(nc.vector.tensor_tensor(osum[:, tl], osum[:, tl], to[c], ALU.add))
                        own.sync()
                        nc.vector.tensor_tensor(osum[:, tl], osum[:, tl], bank[4 * c + 3], ALU.add)\
                            .then_inc(s_to[c], 1)
            dve.wait_ge(s_orr, 1)
            for n in range(NT):
                for h in range(NH):
                    o = osum[:, done_order[n], h]
                    last = nc.vector.tensor_scalar(o, o, ssq[:, 1, n * NH + h:n * NH + h + 1], None, ALU.mult)
                last.then_inc(s_on, 1)
            for v in (hhi, hlo):
                for a, b in ((0, S0), (S0 + SEQ_S, P0), (P0 + SEQ_P, W)):
                    nc.vector.memset(v[:, 0:NH, a:b].bitcast(F32), 0.0)
            for j in range(NB):
                dve.wait_ge(s_yhi, j + 1)
                nc.vector.tensor_tensor(hlo[:, 4 + j, :], yb[:, j, :], hhi[:, 4 + j, :].bitcast(F32),
                                        ALU.subtract).then_inc(s_yready, 1)
            for n in range(NT):
                c0 = TILES[done_order[n]]
                dve.wait_ge(s_oT, n + 1)
                nc.vector.scalar_tensor_tensor(out=chain[n % 2][0], in0=bank[n % 2], scalar=g_o,
                                               in1=sgate[:, :, c0:c0 + P], op0=ALU.mult, op1=ALU.mult)\
                    .then_inc(s_oy, 1)
                dve.wait_ge(s_yhi, NB + n + 1)
                nc.vector.tensor_tensor(hlo[:, 0:NH, c0:c0 + P], chain[n % 2][0],
                                        hhi[:, 0:NH, c0:c0 + P].bitcast(F32), ALU.subtract).then_inc(s_yready, 1)
            dve.wait_ge(s_nst, 32)
            zero_pads(h32 + cv).then_inc(s_fill, 1)

            update_x("out", 0, 0, q=1)
            apply_norm(1, 8)

            def pooled(k):
                gi = k // 2
                win = 2 << gi
                src, m = hp[:, k, :], WP
                for lv in range(gi + 1):
                    m -= 1 << lv
                    dst = psum_w[:, lv % 2, :]
                    own.tick(nc.vector.tensor_tensor(dst[:, 0:m], src[:, 0:m], src[:, (1 << lv):(1 << lv) + m],
                                                     ALU.add))
                    own.sync()
                    src = dst
                for pc, c0, n, _ in POOL_RANGES:
                    own.tick(nc.vector.tensor_tensor(psum_w[:, 2, c0:c0 + n], src[:, pc - win // 2:pc - win // 2 + n],
                                                     inv_n[:, gi, c0:c0 + n], ALU.mult))
                own.sync()
                for pc, c0, n, _ in POOL_RANGES:
                    last = nc.vector.tensor_tensor(h32[k % 2][:, c0:c0 + n], psum_w[:, 2, c0:c0 + n],
                                                   hp[:, k, pc:pc + n], ALU.subtract)
                last.then_inc(s_mixed, 1)

            def pool_normed(k):
                if k > 1:
                    dve.wait_ge(s_aff, 16 + k - 1)
                nc.vector.tensor_tensor(pad[k % 2], x[:, k, :], rstd, ALU.mult).then_inc(s_a, 1)

            def pool_lo(k):
                dve.wait_ge(s_hi, 16 + k + 1)
                nc.vector.tensor_tensor(hlo[:, k, :], h32[k % 2], hhi[:, k, :].bitcast(F32),
                                        ALU.subtract).then_inc(s_h, 1)

            for layer in range(2):
                if layer == 1:
                    for a in (0, PADW + SEQ_S, WP - PADW):
                        nc.vector.memset(hp[:, :, a:a + PADW], 0.0)
                    dve.wait_ge(s_rstd, 3)
                    dve.wait_ge(s_inv, 16)
                    pool_normed(0)
                    for k in range(KD):
                        if k + 1 < KD:
                            pool_normed(k + 1)
                        dve.wait_ge(s_aff, 16 + k + 1)
                        pooled(k)
                        if k:
                            pool_lo(k - 1)
                    pool_lo(KD - 1)
                    b = SEG["pool"]
                    clear_acc(3)
                    for m in range(KD):
                        n = "CB"[m % 2]
                        if m % 4 < 3:
                            dve.wait_ge(s_pm, 3 * (m // 4) + m % 4 + 1)
                        else:
                            dve.wait_ge(s_unit, b["u"] + m // 4 + 1)
                        for bk, pc, ln, xc, cd in PIECES:
                            last = nc.vector.scalar_tensor_tensor(
                                out=x[:, m, xc:xc + ln], in0=pair[n][:, bk, pc:pc + ln],
                                scalar=mod[:, 1, 2, m, cd:cd + 1], in1=x[:, m, xc:xc + ln],
                                op0=ALU.mult, op1=ALU.add)
                        last.then_inc(s_ev[n], 1)
                        if m % 2:
                            for s in range(2):
                                add_squares(m // 2, 3, s)
                    apply_norm(3, 24)
                for g, nf in enumerate(GROUPS):
                    b = SEG["up", layer, g]
                    u, f = b["u"], b["f"]
                    with dve.Fori(0, nf) as i:
                        own.enter(i, 2)
                        dve.wait_ge(s_ev["A"], i + (b["A"] + 1))
                        dve.wait_ge(s_silu, i + (NQKV + f))
                        conv(pad[0], cv[0], [tap_ffn[:, layer, j, ds(i + GROUP_AT[g], 1)] for j in range(3)])
                        dve.wait_ge(s_silu, i + (NQKV + f + 1))
                        dve.wait_ge(s_unit, i * 2 + (u + 2))
                        dve.wait_ge(s_hid_hi, i + f)
                        nc.vector.tensor_tensor(halves(h32[0]), halves(cv[1]), pair["B"], ALU.mult)\
                            .then_inc(s_ev["B"], 1)
                        dve.wait_ge(s_hid_hi, i + (f + 1))
                        nc.vector.tensor_tensor(hidlo[:, i, :], h32[0], hidhi[:, i, :].bitcast(F32),
                                                ALU.subtract).then_inc(s_hid, 1)
                        if layer == 0:
                            for s in range(2):
                                add_mod(i * 2 + (48 + 2 * GROUP_AT[g] + s), s)
                    own.leave(nf)
                    if layer == 0 and g == 2:
                        for n in range(48 + 2 * NF, 96):
                            add_mod(n, n % 2)
                        dve.wait_ge(s_mod, 96)
                        fold_scale(1, 0, g_mix)
                        nc.vector.tensor_tensor(mod[:, 1, 2], mod[:, 1, 2], g_pool, ALU.mult)
                        fold_scale(1, 1, g_ffn).then_inc(s_fold, 1)
                    update_x(("down", layer, g), layer, 1, q=((2, 4)[layer] if g == 2 else None))
                if layer == 0:
                    pass
            dve.wait_ge(s_rstd, 5)
            for k in range(KD):
                nc.vector.scalar_tensor_tensor(out=yout[:, k, :], in0=x[:, k, :], scalar=g_final[:, k:k + 1],
                                               in1=rstd, op0=ALU.mult, op1=ALU.mult).then_inc(s_ychunk, 1)


IN_ORDER = list(range(NQKV + NGATE)) + [NQKV + NGATE + p * NB + j for j in range(NB) for p in (1, 2, 0)]


def kernel(**inputs):
    import concourse.bacc as bacc
    from concourse.bass_utils import run_bass_kernel_spmd

    a = {k: np.asarray(v) for k, v in inputs.items()}

    def tiles(w, rows):
        k, n = w.shape
        return np.ascontiguousarray(
            w.reshape(k // P, P, n // P, P).transpose(2, 1, 0, 3).reshape(n // P, P, rows * P))

    def chunks(v):
        v = v.reshape(v.shape[:-1] + (-1, P))
        return np.moveaxis(v, -1, 0)

    def twice(v):
        return np.repeat(v[..., None], 2, axis=-1)

    arrays = {}
    x = np.zeros((P, KD, W), np.float32)
    x[:, :, S0:S0 + SEQ_S] = a["x_sample"][0].T.reshape(KD, P, SEQ_S).transpose(1, 0, 2)
    x[:, :, P0:P0 + SEQ_P] = a["x_prompt"][0].T.reshape(KD, P, SEQ_P).transpose(1, 0, 2)
    arrays["x"] = x
    w_in = a["w_in_ab"][0]
    nqg = (NQKV + NGATE) * P
    main = tiles(np.concatenate([w_in[:, :nqg], w_in[:, nqg + 16:]], axis=1), KD)
    arrays["w_in"] = main[IN_ORDER]
    arrays["w_out"] = tiles(a["w_out_ab"][0], KD)
    wp = a["w_pool"][0].reshape(4, 2, P, 2, P).transpose(2, 0, 3, 1, 4)
    arrays["w_pool"] = np.ascontiguousarray(wp.reshape(P, 2, SLOT).transpose(1, 0, 2))
    arrays["w_gu"] = np.concatenate([
        np.stack([tiles(a["w_ffn_gate"][l], KD), tiles(a["w_ffn_up"][l], KD)], axis=1).reshape(2 * NF, P, SLOT)
        for l in range(2)])
    for g, nf in enumerate(GROUPS):
        rows = slice(GROUP_AT[g] * P, (GROUP_AT[g] + nf) * P)
        arrays[f"w_dn{g}"] = np.concatenate([tiles(a["w_ffn_down"][l][rows], nf) for l in range(2)])
    arrays["w_ada"] = np.concatenate([tiles(a["w_ada"][l], KD) for l in range(2)])
    ncol = nqg
    packed = {
        "norm_mix": twice(chunks(a["norm_mix_g"])),
        "norm_ffn": twice(chunks(a["norm_ffn_g"])),
        "pool_scale": twice(chunks(a["pool_scale"][0])),
        "final": chunks(a["final_norm_g"]),
        "tap_qkv": chunks(a["conv_qkv"][0]),
        "tap_b": chunks(a["conv_b"][0]),
        "tap_ffn": chunks(a["ffn_conv"]),
        "o_norm": a["o_norm_g"][0][:, None],
        "a_log": np.broadcast_to(a["a_log"][0].reshape(1, 1, 8), (P, NT, 8)),
        "dt_bias": np.broadcast_to(a["dt_bias"][0].reshape(1, 1, 8), (P, NT, 8)),
        "w_ba": w_in[:, ncol:ncol + 16].reshape(KD, P, 16).transpose(1, 0, 2),
        "cond": np.stack([chunks(a["c"][0]), chunks(a["c_ctx"])], axis=-1),
        "b_ada": twice(chunks(a["b_ada"].reshape(-1))),
    }
    cols = np.zeros((P, NCOLS), np.float32)
    for name, (at, n) in COLS.items():
        cols[:, at:at + n] = packed[name].reshape(P, n)
    arrays["cols"] = cols
    arrays["state"] = np.ascontiguousarray(a["state_delta"][0, 0].transpose(2, 0, 1, 3))

    quarter = D // 4
    omega = (1.0 / (10000.0 ** (np.arange(quarter, dtype=np.float32) / quarter))).astype(np.float32)

    def sincos(n):
        e = np.arange(n, dtype=np.float32)[:, None] * omega[None, :]
        return np.concatenate([np.sin(e), np.cos(e)], axis=-1)

    rows = SEQ_S // GRID_W
    pos = np.concatenate([np.broadcast_to(sincos(rows)[:, None, :], (rows, GRID_W, D // 2)),
                          np.broadcast_to(sincos(GRID_W)[None, :, :], (rows, GRID_W, D // 2))], axis=-1)
    arrays["pe"] = np.ascontiguousarray(
        pos.reshape(SEQ_S, D).T.reshape(KD, P, SEQ_S).transpose(1, 0, 2).astype(np.float32))
    r, c = np.arange(P)[:, None], np.arange(P)[None, :]
    arrays["const"] = np.stack([r == c, r <= c, r >= c, r >= 0 * c], axis=1).astype(np.float32)
    lm = np.zeros((P, 2 * LEVELS, P), np.float16)
    for lv in range(LEVELS):
        b = 1 << lv
        same = r // (2 * b) == c // (2 * b)
        lm[:, lv] = same & (r // b % 2 == 0) & (c // b % 2 == 1)
        lm[:, LEVELS + lv] = same & (r // b % 2 == 1) & (c // b % 2 == 0)
    arrays["lmask"] = lm
    inv = np.zeros((P, 4, W), np.float32)
    for gi in range(4):
        w = 2 << gi
        for c0, n, _ in RANGES:
            tk = np.arange(n)
            inv[:, gi, c0:c0 + n] = 1.0 / (np.clip(tk - w // 2 + w, 0, n) - np.clip(tk - w // 2, 0, n))
    arrays["inv_n"] = inv

    nc = bacc.Bacc("TRN2", target_bir_lowering=False, num_devices=1)
    t = {}
    for name, v in arrays.items():
        t[name] = nc.dram_tensor(f"in_{name}", v.shape, mybir.dt.from_np(v.dtype), kind="ExternalInput").ap()
    t["y"] = nc.dram_tensor("out_y", (P, KD, SEQ_S + SEQ_P), F32, kind="ExternalOutput").ap()
    t["new_state"] = nc.dram_tensor("out_state", (P, 2, NH, P), F32, kind="ExternalOutput").ap()
    build(nc, t)
    res = run_bass_kernel_spmd(nc, [{f"in_{k}": v for k, v in arrays.items()}], core_ids=[0]).results[0]
    y = res["out_y"].transpose(2, 1, 0).reshape(SEQ_S + SEQ_P, D)
    y_sample = np.ascontiguousarray(y[:SEQ_S])[None]
    y_prompt = np.ascontiguousarray(y[SEQ_S:])[None]
    new_state = np.ascontiguousarray(res["out_state"].transpose(1, 2, 0, 3))[None, None]
    return y_prompt, y_sample, new_state
```

```python
from contextlib import ExitStack

import numpy as np

import concourse.bass as bass
from concourse import mybir

P = 128
D = 1024
KD = D // P
SEQ_S, SEQ_P = 512, 128
GRID_W = 64
ROWS = SEQ_S // GRID_W
S0 = 1
P0 = S0 + SEQ_S + 1
W = P0 + SEQ_P + 2
HALF = W // 2
RANGES = [(S0, SEQ_S, 0), (P0, SEQ_P, 1)]
NH, DK = 4, 128
NQKV, NGATE, NB = 12, 4, 4
D_FF = 2816
NF = D_FF // P
ADA_COLS = 2 * P
ADA_FIRST = 16
ADA_LAST = 80
GROUPS = [8, 7, 7]
EPS = 1e-6
TILES = [S0 + P * t for t in range(SEQ_S // P)] + [P0]
NT = len(TILES)
LEVELS = 7
PADW = 8
WP = PADW + SEQ_S + PADW + SEQ_P + PADW
POOL_RANGES = [(PADW, S0, SEQ_S, 0), (PADW + SEQ_S + PADW, P0, SEQ_P, 1)]
SLOT = KD * P
PRIMED = 1

F32 = mybir.dt.float32
F32R = mybir.dt.float32r
F16 = mybir.dt.float16
ALU = mybir.AluOpType
ACT = mybir.ActivationFunctionType
ds = bass.ds

PIECES = [(0, S0, HALF - S0, S0, 0), (1, 0, S0 + SEQ_S - HALF, HALF, 0), (1, P0 - HALF, SEQ_P, P0, 1)]

COLS, _at = {}, 0
for _name, _n in (("norm_mix", 2 * KD * 2), ("norm_ffn", 2 * KD * 2), ("pool_scale", KD * 2),
                  ("final", KD), ("tap_qkv", 3 * NQKV), ("tap_b", 3 * NB), ("tap_ffn", 2 * 3 * NF),
                  ("o_norm", 1), ("a_log", NT * 8), ("dt_bias", NT * 8), ("w_ba", KD * 16),
                  ("cond", KD * 2), ("b_ada", 96 * 2), ("sel", 2)):
    COLS[_name] = (_at, _n)
    _at += _n
NCOLS = _at


def plan():
    at = dict(u=0, A=PRIMED, B=PRIMED, C=PRIMED, f=0)
    segs = {"in": dict(at)}
    at["u"] += 28; at["A"] += 14; at["B"] += 14
    segs["out"] = dict(at)
    at["u"] += 8; at["C"] += 4; at["B"] += 4
    for layer in range(2):
        if layer == 1:
            segs["pool"] = dict(at)
            at["u"] += 2; at["C"] += 4; at["B"] += 4
        for g, nf in enumerate(GROUPS):
            segs["up", layer, g] = dict(at)
            at["u"] += 2 * nf; at["A"] += nf; at["B"] += nf; at["f"] += nf
            segs["down", layer, g] = dict(at)
            at["u"] += 8; at["C"] += 4; at["B"] += 4
    return segs


SEG = plan()
L2_AFTER = [1, 2, 4, 5]
ADA_SLOTS = [(n, lv) for n in range(NT) for lv in range(0 if n >= NT - 2 else 1, LEVELS)]
assert len(ADA_SLOTS) == (ADA_LAST - ADA_FIRST) // 2
GROUP_AT = [sum(GROUPS[:g]) for g in range(len(GROUPS))]


class Steps:

    def __init__(self, eng, sem):
        self.eng, self.sem, self.done, self.more = eng, sem, 0, 0

    def tick(self, ins):
        ins.then_inc(self.sem, 1)
        self.done += 1

    def sync(self, back=0):
        self.eng.wait_ge(self.sem, self.more + self.done - back)

    def enter(self, i, per):
        self.start, self.per, self.more = self.done, per, i * per

    def leave(self, n):
        assert self.done - self.start == self.per, (self.done - self.start, self.per)
        self.more = 0
        self.done = self.start + n * self.per


def build(nc, t):
    ctx = ExitStack()
    with ctx:
        def sb(name, shape, dt=F32):
            return ctx.enter_context(nc.sbuf_tensor(name, shape, dt))

        def sem(name):
            return ctx.enter_context(nc.semaphore(name))

        x = sb("x", [P, KD, W])
        raw = [sb(f"raw{s}", [P, SLOT]) for s in range(2)]
        whi = [sb(f"whi{s}", [P, SLOT], F32R) for s in range(2)]
        wlo = [sb(f"wlo{s}", [P, SLOT], F32R) for s in range(2)]
        ada_raw = [sb(f"ada_raw{s}", [P, SLOT]) for s in range(2)]
        cols = sb("cols", [P, NCOLS])
        const = sb("const", [P, 4, P])
        mod = sb("mod", [P, 2, 6, KD, 2])
        silu_c = sb("silu_c", [P, KD, 2])
        c_parts = sb("c_parts", [P, 2, KD, 4], F32R)
        ada_rows = sb("ada_rows", [4, ADA_COLS])
        wba_hi = sb("wba_hi", [P, KD, 16], F32R)
        wba_lo = sb("wba_lo", [P, KD, 16], F32R)
        bias = sb("bias", [P, 2])
        gates = sb("gates", [P, 12, NT * 8])
        junk = sb("junk", [P, P])
        ssq = sb("ssq", [P, 2, NT * NH])
        ident, tri_u, tri_l, ones = (const[:, j, :] for j in range(4))
        eps_col, scale_col = bias[:, 0:1], bias[:, 1:2]

        work = sb("work", [P, 10, W])
        pad = [work[:, 0, :], work[:, 1, :]]
        cv = [work[:, 2, :], work[:, 3, :]]
        h32 = [work[:, 4, :], work[:, 5, :]]
        sq = [work[:, 6, :], work[:, 7, :]]
        acc = work[:, 8, :]
        rstd = work[:, 9, :]
        flat = work[:, :, :].rearrange("p a b -> p (a b)")
        chain = [[flat[:, (2 * j + c) * 512:(2 * j + c + 1) * 512].rearrange("p (h e) -> p h e", h=NH)
                  for c in range(2)] for j in range(6)]
        dec, mt, tt, btx, bty, ys = chain
        bt = [[btx[c], bty[c]] for c in range(2)]
        rr, vn, to, kg, ss, sp_ = chain

        off_h = nc.sbuf_base
        size_h = 2 * KD * W * 4
        hhi = nc.alloc_sbuf_tensor_at("hhi", [P, KD, W], F32R, offset=off_h)
        hlo = nc.alloc_sbuf_tensor_at("hlo", [P, KD, W], F32R, offset=off_h + size_h // 2)
        rinv = nc.alloc_sbuf_tensor_at("rinv", [P, 2 * NT, NH, P], F32, offset=off_h)
        attn = nc.alloc_sbuf_tensor_at("attn", [P, 2 * NT, NH, P], F32, offset=off_h + NT * 2 * 2048)
        assert NT * 4 * 2048 <= size_h

        off_m = off_h + size_h
        qkv = nc.alloc_sbuf_tensor_at("qkv", [P, NQKV, W], F32, offset=off_m)
        osum = nc.alloc_sbuf_tensor_at("osum", [P, NT, NH, P], F32, offset=off_m + 8 * W * 4)
        o2 = off_m + NQKV * W * 4
        ktok = nc.alloc_sbuf_tensor_at("ktok", [P, NT, NH, P], F32, offset=o2)
        vtok = nc.alloc_sbuf_tensor_at("vtok", [P, NT, NH, P], F32, offset=o2 + NT * 2048)
        lnn = nc.alloc_sbuf_tensor_at("lnn", [P, 8, W], F32, offset=o2)
        o3 = o2 + max(NT * 4096, 8 * W * 4)
        sgate = nc.alloc_sbuf_tensor_at("sgate", [P, NGATE, W], F32, offset=o3)
        yb = nc.alloc_sbuf_tensor_at("yb", [P, NB, W], F32, offset=o3 + NGATE * W * 4)
        o4 = o3 + (NGATE + NB) * W * 4
        lmask = nc.alloc_sbuf_tensor_at("lmask", [P, 2 * LEVELS, P], F16, offset=o4)
        end_m = o4 + 2 * LEVELS * P * 2
        ada_first = nc.alloc_sbuf_tensor_at("ada_first", [P, ADA_FIRST, SLOT], F32, offset=off_m)
        pe_tab = nc.alloc_sbuf_tensor_at("pe_tab", [P, 4, ROWS + GRID_W], F32, offset=off_h)
        assert ADA_FIRST * SLOT * 4 <= o4 - off_m
        hidhi = nc.alloc_sbuf_tensor_at("hidhi", [P, KD, W], F32R, offset=off_m)
        hidlo = nc.alloc_sbuf_tensor_at("hidlo", [P, KD, W], F32R, offset=off_m + KD * W * 4)
        inv_at = off_m + 2 * KD * W * 4
        yout = nc.alloc_sbuf_tensor_at("yout", [P, KD, W], F32, offset=off_m)
        inv_n = nc.alloc_sbuf_tensor_at("inv_n", [P, 4, W], F32, offset=inv_at)
        hp = nc.alloc_sbuf_tensor_at("hp", [P, KD, WP], F32, offset=inv_at + 4 * W * 4)
        psum_w = nc.alloc_sbuf_tensor_at("psum_w", [P, 3, WP], F32, offset=off_m)
        assert inv_at + 4 * W * 4 + KD * WP * 4 <= end_m and end_m <= nc.sbuf_usable_end, end_m

        ps = ctx.enter_context(nc.psum_tensor("ps", [P, 8, 512], F32))
        pair = {n: ps[:, 2 * j:2 * j + 2, 0:HALF] for j, n in enumerate("ABCX")}
        bank = [ps[:, j, :].rearrange("p (h e) -> p h e", h=NH) for j in range(8)]

        def halves(ap):
            return ap.rearrange("p (b n) -> p b n", b=2)

        def col(name, pattern=None, **dims):
            a, n = COLS[name]
            v = cols[:, a:a + n]
            return v.rearrange(pattern, **dims) if pattern else v

        g_mix = col("norm_mix", "p (l k c) -> p l k c", l=2, k=KD)
        g_ffn = col("norm_ffn", "p (l k c) -> p l k c", l=2, k=KD)
        g_pool = col("pool_scale", "p (k c) -> p k c", k=KD)
        g_final = col("final")
        tap_qkv = col("tap_qkv", "p (t n) -> p t n", t=3)
        tap_b = col("tap_b", "p (t n) -> p t n", t=3)
        tap_ffn = col("tap_ffn", "p (l t n) -> p l t n", l=2, t=3)
        g_o = col("o_norm")
        w_ba = col("w_ba", "p (k n) -> p k n", k=KD)
        cond = col("cond", "p (k c) -> p k c", k=KD)
        b_ada = col("b_ada", "p (n c) -> p n c", c=2)
        mod_n = mod[:].rearrange("p l s k c -> p (l s k) c")

        (beta, g_log, e_alog, gcs, egc, ekg, etot, negegc, tmp_a, tmp_b, tmp_c, tmp_d) = (
            gates[:, j, :] for j in range(12))

        s_cols = sem("cols_loaded")
        s_x = sem("x_loaded")
        s_const = sem("const_loaded")
        s_pe = sem("pe_loaded")
        s_ada1 = [sem(f"ada_first_loaded{q}") for q in range(4)]
        s_state = sem("state_loaded")
        s_inv = sem("inv_loaded")
        s_raw = [sem(f"weights_loaded{s}") for s in range(2)]
        s_ada = [sem(f"ada_loaded{s}") for s in range(4)]
        s_go = sem("units_begun")
        s_whi = sem("weights_hi")
        s_split = sem("weights_split")
        s_unit = sem("units_multiplied")
        s_ev = {n: sem(f"pair{n}_read") for n in "ABC"}
        s_c_parts = sem("c_parts_ready")
        s_ada_hi = sem("ada_hi")
        s_ada_lo = sem("ada_lo")
        s_ada_pe = sem("ada_multiplied")
        s_ada_cp = sem("ada_rows_copied")
        s_ada_t = sem("ada_columns")
        s_mod = sem("mod_batches_written")
        s_silu_c = sem("silu_c_ready")
        s_fill = sem("constants_filled")
        s_x0 = sem("x_with_positions")
        s_sq = sem("squares_ready")
        s_acc = sem("squares_added")
        s_norm = sem("square_sums")
        s_rstd = sem("rstd_ready")
        s_a = sem("normed_ready")
        s_aff = sem("modulated")
        s_hi = sem("h_hi_ready")
        s_h = sem("h_ready")
        s_conv = sem("convs_done")
        s_silu = sem("silus_done")
        s_hid_hi = sem("hidden_hi_ready")
        s_hid = sem("hidden_ready")
        s_dve = sem("dve_steps")
        s_act = sem("act_steps")
        s_out = sem("outputs_written")
        s_ychunk = sem("y_chunks")
        s_fold = sem("scales_folded")
        s_lmask = sem("level_masks_loaded")
        s_nst = sem("new_states_written")
        s_zero = sem("prompt_states_zero")
        s_pm = sem("pool_products")
        s_mixed = sem("pool_mixed")
        s_l2sq = sem("qk_squares")
        s_l2sum = sem("qk_square_sums")
        s_l2ln = sem("qk_logs")
        s_l2r = sem("qk_rsqrt")
        s_l2 = sem("qk_normed")
        s_bat = sem("beta_alpha_rows")
        s_ba = sem("beta_alpha_products")
        s_ga = sem("gate_steps_scalar")
        s_gd = sem("gate_steps_vector")
        s_gsum = sem("gate_sums")
        s_tr = sem("kv_transposed")
        s_tok = sem("kv_tokens_copied")
        s_gram = sem("gram_products")
        s_tg = [sem(f"tri_g{c}") for c in range(2)]
        s_bc = [sem(f"gc_rows{c}") for c in range(2)]
        s_dd = [sem(f"decay_arg{c}") for c in range(2)]
        s_dx = [sem(f"decay_exp{c}") for c in range(2)]
        s_mt = [sem(f"mt_ready{c}") for c in range(2)]
        s_at = [sem(f"attn_masked{c}") for c in range(2)]
        s_bt = [sem(f"level_block{c}") for c in range(2)]
        s_y = [sem(f"bt_product{c}") for c in range(2)]
        s_yc = [sem(f"bt_product_copied{c}") for c in range(2)]
        s_z = [sem(f"level_products{c}") for c in range(2)]
        s_up = [sem(f"level_updated{c}") for c in range(2)]
        s_kq = [sem(f"scan_kq{c}") for c in range(2)]
        s_r = [sem(f"scan_r{c}") for c in range(2)]
        s_t = [sem(f"scan_t{c}") for c in range(2)]
        s_tr3 = [sem(f"scan_solve{c}") for c in range(2)]
        s_vn = [sem(f"scan_vnew{c}") for c in range(2)]
        s_kg = [sem(f"scan_kg{c}") for c in range(2)]
        s_ap = [sem(f"scan_products{c}") for c in range(2)]
        s_st = [sem(f"scan_state{c}") for c in range(2)]
        s_to = [sem(f"scan_o{c}") for c in range(2)]
        s_orr = sem("o_rsqrt")
        s_on = sem("o_normed")
        s_oT = sem("o_transposed")
        s_oy = sem("o_gated")
        s_yhi = sem("y_hi")
        s_yready = sem("y_ready")

        def level_mask(d, lv):
            return lmask[:, d * LEVELS + lv, :].unsqueeze(1).to_broadcast([P, NH, P])

        def tri_mask(d):
            return (tri_u, tri_l)[d].unsqueeze(1).to_broadcast([P, NH, P])

        def scan_tile(c, s):
            return NT - 1 if s == NT - 1 else (s if c == 0 else NT - 2 - s)

        def first_visit(c, s):
            return s == NT - 1 and c == 0 or s < (NT - 1) // 2

        done_visits = [(c, s) for s in range(NT) for c in range(2) if not first_visit(c, s)]
        done_order = [scan_tile(c, s) for c, s in done_visits]

        batches = [(0, ADA_FIRST)]
        for n in range(NT):
            batches.append((sum(batches[-1]), 2 * sum(m == n for m, _ in ADA_SLOTS)))
        batches.append((ADA_LAST, 96 - ADA_LAST))
        batch_end = [sum(b) // 2 - 1 for b in batches]
        row_banks = [(4, 5)] + [(7, 7)] * (NT + 1)
        col_bank = [0] + [7] * (NT + 1)

        def batch_of(n):
            return next(b for b in range(len(batches)) if n < sum(batches[b]))

        def ada_row(n):
            return ps[0:4, row_banks[batch_of(n)][n // 2 % 2], 0:ADA_COLS]

        def ada_source(n):
            return ada_first[:, n, :] if n < ADA_FIRST else (ada_raw + raw)[n % 4][:]

        block = ctx.enter_context(nc.Block())

        @block.sync
        def _(sp):
            def load(u, s, src, n=SLOT):
                sp.wait_ge(s_split, u - 1)
                sp.dma_start(raw[s][:, 0:n], src).then_inc(s_raw[s], 16)

            def load_ada(n, s):
                sp.wait_ge(s_ada_lo, n + (ADA_FIRST - 3))
                sp.dma_start((ada_raw + raw)[s][:], t["w_ada"][n + ADA_FIRST]).then_inc(s_ada[s], 16)

            def load_ada_direct(n, s):
                sp.wait_ge(s_ada_pe, n - 1)
                sp.dma_start(ada_raw[s][:], t["w_ada"][n]).then_inc(s_ada[s], 16)

            for sm in (*s_ev.values(), s_conv, s_silu, s_aff, s_h, s_hid_hi, s_l2ln):
                sp.sem_inc(sm, PRIMED)
            sp.dma_start(cols[:], t["cols"]).then_inc(s_cols, 16)
            sp.dma_start(pe_tab[:], t["pe"]).then_inc(s_pe, 16)
            sp.dma_start(x[:], t["x"]).then_inc(s_x, 16)
            n = ADA_FIRST // 4
            for q in range(4):
                sp.dma_start(ada_first[:, n * q:n * (q + 1), :],
                             t["w_ada"][n * q:n * (q + 1)].rearrange("u p f -> p u f")).then_inc(s_ada1[q], 16)
            sp.dma_start(const[:], t["const"]).then_inc(s_const, 16)
            for s in range(2):
                sp.dma_start(raw[s][:], t["w_in"][s]).then_inc(s_raw[s], 16)
            for s in range(2):
                sp.dma_start(ada_raw[s][:], t["w_ada"][ADA_FIRST + s]).then_inc(s_ada[s], 16)
            sp.dma_start(lmask[:], t["lmask"]).then_inc(s_lmask, 16)
            with sp.Fori(1, 14) as i:
                for s in range(2):
                    load(i * 2 + s, s, t["w_in"][i * 2 + s])
            sp.wait_ge(s_split, 28)
            for s in range(2):
                sp.dma_start(raw[s][:], t["w_ada"][ADA_FIRST + 2 + s]).then_inc(s_ada[2 + s], 16)
            with sp.Fori(1, (ADA_LAST - ADA_FIRST) // 4) as i:
                for s in range(4):
                    load_ada(i * 4 + s, s)
            u = SEG["out"]["u"]
            sp.wait_ge(s_ada_lo, ADA_LAST)
            for s in range(2):
                load(u + s, s, t["w_out"][s])
            for s in range(2):
                load_ada_direct(ADA_LAST + s, s)
            for c in range(2):
                sp.wait_ge(s_y[c], LEVELS * NT)
                sp.dma_start(ss[c], t["state"][:, c]).then_inc(s_state, 16)
            for c in range(2):
                sp.wait_ge(s_st[c], NT)
                sp.dma_start(t["new_state"][:, c], sp_[c]).then_inc(s_nst, 16)
            with sp.Fori(1, 4) as i:
                for s in range(2):
                    load(i * 2 + (u + s), s, t["w_out"][i * 2 + s])
            for layer in range(2):
                if layer == 1:
                    u = SEG["pool"]["u"]
                    for s in range(2):
                        load(u + s, s, t["w_pool"][s])
                    for s in range(2):
                        load(u + 2 + s, s, t["w_gu"][2 * NF + s])
                    with sp.Fori(ADA_LAST // 2 + 1, 96 // 2) as i:
                        for s in range(2):
                            load_ada_direct(i * 2 + s, s)
                for g, nf in enumerate(GROUPS):
                    u = SEG["up", layer, g]["u"]
                    f0 = layer * NF + GROUP_AT[g]
                    with sp.Fori(1 if (layer, g) == (1, 0) else 0, nf) as i:
                        for s in range(2):
                            load(i * 2 + (u + s), s, t["w_gu"][i * 2 + (2 * f0 + s)])
                    if layer == 0 and g == 0:
                        sp.wait_ge(s_unit, SEG["up", 0, 0]["u"])
                        sp.dma_start(inv_n[:], t["inv_n"]).then_inc(s_inv, 16)
                    u = SEG["down", layer, g]["u"]
                    with sp.Fori(0, 4) as i:
                        for s in range(2):
                            load(i * 2 + (u + s), s, t[f"w_dn{g}"][i * 2 + (8 * layer + s)], nf * P)
            for k in range(KD):
                sp.wait_ge(s_ychunk, k + 1)
                for (c0, n, cd) in RANGES:
                    sp.dma_start(t["y"][:, k, SEQ_S * cd:SEQ_S * cd + n], yout[:, k, c0:c0 + n]).then_inc(s_out, 16)
            sp.wait_ge(s_out, 16 * 2 * KD)
            sp.wait_ge(s_nst, 32)

        @block.gpsimd
        def _(pool):
            def split(u, half_u, s, n=SLOT, guard=True):
                pool.wait_ge(s_raw[s], half_u * 16 + 16)
                if guard:
                    pool.wait_ge(s_unit, u - 1)
                pool.sem_inc(s_go, 1)
                nc.gpsimd.tensor_scalar(whi[s][:, 0:n], raw[s][:, 0:n], 1.0, 0.0,
                                        ALU.mult, ALU.add).then_inc(s_whi, 1)
                pool.wait_ge(s_whi, u + 1)
                nc.gpsimd.tensor_tensor(wlo[s][:, 0:n], raw[s][:, 0:n], whi[s][:, 0:n].bitcast(F32),
                                        ALU.subtract).then_inc(s_split, 1)

            def split_pairs(u, n_pairs, n=SLOT, first=0):
                with pool.Fori(first, n_pairs) as i:
                    for s in range(2):
                        split(i * 2 + (u + s), i + u // 2, s, n)

            def ada_lo(n):
                s = n % 2
                pool.wait_ge(s_ada_hi, n + 1)
                nc.gpsimd.tensor_tensor(wlo[s][:], ada_source(n), whi[s][:].bitcast(F32),
                                        ALU.subtract).then_inc(s_ada_lo, 1)

            pool.wait_ge(s_ada_pe, ADA_FIRST)
            for s in range(2):
                split(s, 0, s, guard=False)
            split_pairs(0, 14, first=1)
            pool.wait_ge(s_lmask, 16)
            def level_blocks(n, lv):
                for c in range(2):
                    if lv == 0:
                        pool.wait_ge(s_mt[c], n + 1)
                    if LEVELS * n + lv >= 2:
                        pool.wait_ge(s_y[c], LEVELS * n + lv - 1)
                    if lv == 2:
                        pool.wait_ge(s_up[c], LEVELS * n + 1)
                    nc.gpsimd.tensor_tensor(bt[c][(LEVELS * n + lv) % 2], mt[c], level_mask(c, lv),
                                            ALU.mult).then_inc(s_bt[c], 1)

            def mask_attention(n):
                for c in range(2):
                    a = attn[:, 2 * n + c]
                    nc.gpsimd.tensor_tensor(a, a, tri_mask(c), ALU.mult).then_inc(s_at[c], 1)

            for n in range(NT):
                level_blocks(n, 0)
                for lv in range(LEVELS):
                    if (n, lv) in ADA_SLOTS:
                        g = ADA_FIRST // 2 + ADA_SLOTS.index((n, lv))
                        for s in range(2):
                            ada_lo(2 * g + s)
                    if lv + 1 < LEVELS:
                        level_blocks(n, lv + 1)
                    if lv == 1:
                        mask_attention(n)
            u = SEG["out"]["u"]
            pool.wait_ge(s_ada_pe, ADA_LAST)
            for s in range(2):
                split(u + s, u // 2, s)
            for s in range(NT):
                for c in range(2):
                    if s == 0:
                        pool.wait_ge(s_up[c], LEVELS * NT)
                        pool.wait_ge(s_y[c], LEVELS * NT)
                        pool.wait_ge(s_z[c], (LEVELS - 1) * NT)
                    else:
                        pool.wait_ge(s_ap[c], s)
                    tl = scan_tile(c, s)
                    for h in range(NH):
                        j = tl * 8 + c * NH + h
                        last = nc.gpsimd.tensor_scalar(kg[c][:, h], ktok[:, tl, h], ekg[:, j:j + 1], 1.0,
                                                       ALU.mult, ALU.mult)
                    last.then_inc(s_kg[c], 1)
            split_pairs(u, 4, first=1)
            for layer in range(2):
                if layer == 1:
                    split_pairs(SEG["pool"]["u"], 1)
                for g, nf in enumerate(GROUPS):
                    split_pairs(SEG["up", layer, g]["u"], nf)
                    split_pairs(SEG["down", layer, g]["u"], 4, nf * P)

        @block.tensor
        def _(pe):
            def products(pr, s, tiles, hi, lo, ks, wait_k=None):
                last = None
                for j, (tile, k) in enumerate(zip(tiles, ks)):
                    if wait_k is not None:
                        wait_k(j)
                    cs = slice(tile * P, tile * P + P)
                    for q, (wt, act) in enumerate(((whi, hi), (whi, lo), (wlo, hi))):
                        for b in range(2):
                            last = nc.tensor.matmul(pair[pr][:, b], wt[s][:, cs],
                                                    act[:, k, b * HALF:(b + 1) * HALF],
                                                    start=(j == 0 and q == 0),
                                                    stop=(j == len(tiles) - 1 and q == 2))
                return last

            def ada(n):
                b = batch_of(n)
                s = n % 2
                if n == batches[b][0] and b:
                    pe.wait_ge(s_mod, b)
                pe.wait_ge(s_ada_lo, n + 1)
                for k in range(4):
                    for q, w in enumerate((whi, wlo)):
                        last = nc.tensor.matmul(ada_row(n), c_parts[:, q, 4 * s + k, :],
                                                w[s][:, k * ADA_COLS:(k + 1) * ADA_COLS],
                                                start=(s == 0 and k == 0 and q == 0),
                                                stop=(s == 1 and k == 3 and q == 1))
                last.then_inc(s_ada_pe, 1)

            def ada_columns(g):
                b = batch_of(2 * g)
                pe.wait_ge(s_ada_cp, g + 1)
                for h in range(2):
                    at = ADA_COLS + 2 * (2 * g + h - batches[b][0])
                    last = nc.tensor.matmul(ps[:, col_bank[b], at:at + 2], ada_rows[:, h * P:(h + 1) * P],
                                            col("sel")[0:4], start=True, stop=True)
                last.then_inc(s_ada_t, 1)

            def ada_direct(n):
                if n == ADA_LAST:
                    pe.wait_ge(s_mod, NT + 1)
                pe.wait_ge(s_ada[n % 2], 16 * ((ADA_LAST - ADA_FIRST) // 4 + (n - ADA_LAST) // 2 + 1))
                for k in range(KD):
                    at = ADA_COLS + 2 * (n - ADA_LAST)
                    last = nc.tensor.matmul(ps[:, 7, at:at + 2], ada_raw[n % 2][:, k * P:(k + 1) * P],
                                            silu_c[:, k, :], start=(k == 0), stop=(k == KD - 1))
                last.then_inc(s_ada_pe, 1)

            def norm_sums(q):
                pe.wait_ge(s_acc, 9 * (q + 1))
                if q:
                    pe.wait_ge(s_mod, (None, NT + 1, NT + 1, NT + 2, NT + 2)[q])
                for b in range(2):
                    last = nc.tensor.matmul(pair["X"][:, b], ones, acc[:, b * HALF:(b + 1) * HALF],
                                            start=True, stop=True)
                last.then_inc(s_norm, 1)

            pe.wait_ge(s_c_parts, 1)
            for g in range(ADA_FIRST // 2):
                ada(2 * g)
                if g:
                    ada_columns(g - 1)
                ada(2 * g + 1)
            ada_columns(ADA_FIRST // 2 - 1)
            pe.wait_ge(s_const, 16)
            norm_sums(0)

            def in_unit(u, half_u, s, wait_k=None):
                pe.wait_ge(s_split, u + 1)
                pe.wait_ge(s_ev["AB"[s]], half_u + PRIMED)
                products("AB"[s], s, range(KD), hhi, hlo, range(KD), wait_k).then_inc(s_unit, 1)

            with pe.Fori(0, NQKV // 2) as i:
                for s in range(2):
                    in_unit(i * 2 + s, i, s, (lambda j: pe.wait_ge(s_h, PRIMED + j + 1)) if s == 0 else None)
            pe.wait_ge(s_mod, 1)
            for k in range(KD):
                for q, (a, b) in enumerate(((wba_hi, hhi), (wba_hi, hlo), (wba_lo, hhi))):
                    for h in range(2):
                        last = nc.tensor.matmul(pair["C"][0:16, h], a[:, k, :], b[:, k, h * HALF:(h + 1) * HALF],
                                                start=(k == 0 and q == 0), stop=(k == KD - 1 and q == 2))
            last.then_inc(s_bat, 1)
            with pe.Fori(NQKV // 2, (NQKV + NGATE) // 2) as i:
                for s in range(2):
                    in_unit(i * 2 + s, i, s)
            pe.wait_ge(s_gd, 1)
            for tl, c0 in enumerate(TILES):
                last = nc.tensor.transpose(ps[:, 7, 16 * tl:16 * tl + 16], acc[0:16, c0:c0 + P],
                                           ident[0:16, 0:16])
            last.then_inc(s_ba, 1)
            with pe.Fori(0, 2) as i:
                for j in range(6):
                    in_unit(i * 6 + (NQKV + NGATE + j), i * 3 + (NQKV + NGATE + j) // 2, j % 2)
                    if j in L2_AFTER:
                        m = L2_AFTER.index(j)
                        pe.wait_ge(s_l2sq, i * 4 + (m + 1))
                        if j == L2_AFTER[0]:
                            pe.wait_ge(s_ga, 1)
                            pe.wait_ge(s_gd, 2)
                        pe.wait_ge(s_l2ln, i * 4 + (PRIMED + m))
                        for b in range(2):
                            last = nc.tensor.matmul(pair["X"][:, b], ones, sq[m % 2][:, b * HALF:(b + 1) * HALF],
                                                    start=True, stop=True)
                        last.then_inc(s_l2sum, 1)
            pe.wait_ge(s_gd, 6)
            pe.wait_ge(s_l2ln, PRIMED + 8)
            gv = g_log.rearrange("p (t j) -> p t j", t=NT)
            gps = ps[:, 7, 128:168].rearrange("p (t j) -> p t j", t=NT)
            for d in range(2):
                nc.tensor.matmul(gps[:, :, 4 * d:4 * d + 4], (tri_u, tri_l)[d], gv[:, :, 4 * d:4 * d + 4],
                                 start=True, stop=True)
            nc.tensor.matmul(ps[:, 7, 192:232], ones, g_log, start=True, stop=True).then_inc(s_gsum, 1)

            pe.wait_ge(s_l2, 8)

            def tokens(n, j):
                if n + j:
                    pe.wait_ge(s_tok, 2 * n + j)
                for h in range(NH):
                    last = nc.tensor.transpose(bank[6][:, h], qkv[:, 4 + 4 * j + h, TILES[n]:TILES[n] + P], ident)
                last.then_inc(s_tr, 1)

            for n in range(NT):
                c0 = TILES[n]
                if n:
                    pe.wait_ge(s_up[1], LEVELS * n)
                else:
                    for p in "AB":
                        pe.wait_ge(s_ev[p], PRIMED + 14)
                for h in range(NH):
                    kt = qkv[:, 4 + h, c0:c0 + P]
                    nc.tensor.matmul(bank[0][:, h], kt, kt, start=True, stop=True)
                for h in range(NH):
                    last = nc.tensor.matmul(bank[1][:, h], qkv[:, 4 + h, c0:c0 + P], qkv[:, h, c0:c0 + P],
                                            start=True, stop=True)
                last.then_inc(s_gram, 1)
                for c in range(2):
                    pe.wait_ge(s_tg[c], n + 1)
                    if n:
                        pe.wait_ge(s_yc[c], (LEVELS - 1) * n)
                    nc.tensor.matmul(bank[2 + c], ones, dec[c], start=True, stop=True).then_inc(s_bc[c], 1)
                if n == 0:
                    pe.wait_ge(s_ga, 9)
                tokens(n, 0)
                for lv in range(LEVELS):
                    for c in range(2):
                        pe.wait_ge(s_bt[c], LEVELS * n + lv + 1)
                        if lv == 0:
                            pe.wait_ge(s_dd[c], n + 1)
                        else:
                            pe.wait_ge(s_up[c], LEVELS * n + lv)
                            if lv > 1:
                                pe.wait_ge(s_yc[c], (LEVELS - 1) * n + lv - 1)
                        for h in range(NH):
                            last = nc.tensor.matmul(bank[2 + c][:, h], bt[c][(LEVELS * n + lv) % 2][:, h],
                                                    ident if lv == 0 else tt[c][:, h], start=True, stop=True)
                        last.then_inc(s_y[c], 1)
                    g = ADA_FIRST // 2 + ADA_SLOTS.index((n, lv)) if (n, lv) in ADA_SLOTS else None
                    if g is not None:
                        if g - 1 not in batch_end:
                            ada_columns(g - 1)
                        ada(2 * g)
                    if lv == 0:
                        tokens(n, 1)
                        if g is not None:
                            ada(2 * g + 1)
                        continue
                    for c in range(2):
                        zb, ztb = ((4, 5), (0, 1))[c]
                        if lv == 1 and c == 1:
                            for cc in range(2):
                                pe.wait_ge(s_mt[cc], n + 1)
                        pe.wait_ge(s_yc[c], (LEVELS - 1) * n + lv)
                        for h in range(NH):
                            if lv < LEVELS - 1:
                                nc.tensor.matmul(bank[zb][:, h], rinv[:, 2 * n + c, h], ys[c][:, h],
                                                 start=True, stop=True)
                            last = nc.tensor.matmul(bank[ztb][:, h], ys[c][:, h], rinv[:, 2 * n + c, h],
                                                    start=True, stop=True)
                        last.then_inc(s_z[c], 1)
                    ada(2 * g + 1)
                ada_columns(g)

            for s in range(NT):
                for c in range(2):
                    tl = scan_tile(c, s)
                    c0 = TILES[tl]
                    b0 = 4 * c
                    S = ss[c] if s < NT - 1 else sp_[c]
                    if s == 0:
                        pe.wait_ge(s_state, 32)
                        for cc in range(2):
                            pe.wait_ge(s_up[cc], LEVELS * NT)
                        pe.wait_ge(s_tok, 2 * NT)
                        pe.wait_ge(s_mod, NT + 1)
                    elif s == NT - 1:
                        pe.wait_ge(s_zero, 2)
                        pe.wait_ge(s_vn[c], s)
                    else:
                        pe.wait_ge(s_st[c], s)
                    if s:
                        pe.wait_ge(s_t[c], s)
                    for h in range(NH):
                        nc.tensor.matmul(bank[b0][:, h], qkv[:, 4 + h, c0:c0 + P], S[:, h],
                                         start=True, stop=True)
                    for h in range(NH):
                        last = nc.tensor.matmul(bank[b0 + 1][:, h], qkv[:, h, c0:c0 + P], S[:, h],
                                                start=True, stop=True)
                    last.then_inc(s_kq[c], 1)
                for c in range(2):
                    tl = scan_tile(c, s)
                    pe.wait_ge(s_r[c], s + 1)
                    for h in range(NH):
                        last = nc.tensor.matmul(bank[4 * c][:, h], rinv[:, 2 * tl + c, h], rr[c][:, h],
                                                start=True, stop=True)
                    last.then_inc(s_tr3[c], 1)
                for c in range(2):
                    tl = scan_tile(c, s)
                    pe.wait_ge(s_vn[c], s + 1)
                    pe.wait_ge(s_kg[c], s + 1)
                    pe.wait_ge(s_at[c], NT)
                    if s:
                        pe.wait_ge(s_to[c], s)
                    for h in range(NH):
                        nc.tensor.matmul(bank[4 * c + 2][:, h], kg[c][:, h], vn[c][:, h], start=True, stop=True)
                    for h in range(NH):
                        last = nc.tensor.matmul(bank[4 * c + 3][:, h], attn[:, 2 * tl + c, h], vn[c][:, h],
                                                start=True, stop=True)
                    last.then_inc(s_ap[c], 1)
            for n in range(NT):
                pe.wait_ge(s_on, n + 1)
                if n >= 2:
                    pe.wait_ge(s_oy, n - 1)
                for h in range(NH):
                    last = nc.tensor.transpose(bank[n % 2][:, h], osum[:, done_order[n], h], ident)
                last.then_inc(s_oT, 1)

            def accumulate(seg, nf, hi, lo, ready):
                b = SEG[seg]
                with pe.Fori(0, 4) as i:
                    for s in range(2):
                        n = "CB"[s]
                        pe.wait_ge(s_split, i * 2 + (b["u"] + s + 1))
                        pe.wait_ge(s_ev[n], i + b[n])
                        products(n, s, range(nf), hi, lo, range(nf), ready if s == 0 else None)\
                            .then_inc(s_unit, 1)

            pe.wait_ge(s_yready, NB + NT)
            accumulate("out", KD, hhi, hlo, None)
            norm_sums(1)

            for layer in range(2):
                if layer == 1:
                    b = SEG["pool"]
                    pe.wait_ge(s_rstd, 3)
                    for m in range(KD):
                        n = "CB"[m % 2]
                        if m in (0, 2):
                            for n_ada in range(ADA_LAST + 4 * m, ADA_LAST + 4 * m + 8):
                                ada_direct(n_ada)
                        if m % 4 == 0:
                            pe.wait_ge(s_split, b["u"] + m // 4 + 1)
                        pe.wait_ge(s_ev[n], b[n] + m // 2)
                        pe.wait_ge(s_h, PRIMED + 16 + 2 * (m // 2) + 2)
                        last = products(n, m // 4, (2 * (m % 4), 2 * (m % 4) + 1), hhi, hlo,
                                        (2 * (m // 2), 2 * (m // 2) + 1))
                        last.then_inc(s_unit if m % 4 == 3 else s_pm, 1)
                    norm_sums(3)
                for g, nf in enumerate(GROUPS):
                    b = SEG["up", layer, g]
                    hr = 8 if layer == 0 else 24
                    with pe.Fori(0, nf) as i:
                        for s in range(2):
                            pe.wait_ge(s_split, i * 2 + (b["u"] + s + 1))
                            pe.wait_ge(s_ev["AB"[s]], i + b["AB"[s]])
                            wait_k = (lambda j: pe.wait_ge(s_h, PRIMED + hr + j + 1)) if s == 0 and g == 0 else None
                            products("AB"[s], s, range(KD), hhi, hlo, range(KD), wait_k).then_inc(s_unit, 1)
                    f = b["f"]
                    accumulate(("down", layer, g), nf, hidhi, hidlo, lambda j: pe.wait_ge(s_hid, f + j + 1))
                norm_sums(2 if layer == 0 else 4)

        @block.scalar
        def _(act):
            own = Steps(act, s_act)

            def rsqrt_of_sums(q):
                act.wait_ge(s_norm, q + 1)
                if q:
                    act.wait_ge(s_a, 8 * q)
                own.tick(nc.scalar.activation(halves(rstd), pair["X"], ACT.Ln, bias=eps_col, scale=1.0 / D))
                own.sync()
                nc.scalar.activation(rstd, rstd, ACT.Exp, scale=-0.5).then_inc(s_rstd, 1)

            def modulate(q, layer, part):
                rsqrt_of_sums(q)
                aff = 8 * q + PRIMED
                hi0 = (0, 8, None, 24)[q] + PRIMED
                with act.Fori(0, 4) as i:
                    for s in range(2):
                        k = i * 2 + s
                        act.wait_ge(s_a, i * 2 + (8 * q + s + 1))
                        act.wait_ge(s_h, i * 2 + hi0)
                        for c0, n, cd in RANGES:
                            last = nc.scalar.activation(h32[s][:, c0:c0 + n], pad[s][:, c0:c0 + n], ACT.Identity,
                                                        bias=mod[:, layer, 3 * part, ds(k, 1), cd],
                                                        scale=mod[:, layer, 3 * part + 1, ds(k, 1), cd])
                        last.then_inc(s_aff, 1)
                        act.wait_ge(s_aff, i * 2 + (aff + s + 1))
                        nc.scalar.activation(hhi[:, k, :], h32[s], ACT.Copy).then_inc(s_hi, 1)

            def squares(q, name_of, base):
                with act.Fori(0, 4) as i:
                    for s in range(2):
                        act.wait_ge(name_of[s], i * base[s][1] + (base[s][0] + 1))
                        act.wait_ge(s_acc, i * 2 + (9 * q + 1))
                        nc.scalar.activation(sq[s], x[:, i * 2 + s, :], ACT.Square).then_inc(s_sq, 1)

            def squares_after(q, seg):
                b = SEG[seg]
                squares(q, (s_ev["C"], s_ev["B"]), ((b["C"], 1), (b["B"], 1)))

            def ada_hi(n):
                s = n % 2
                if n < ADA_FIRST:
                    if n % 4 == 0:
                        act.wait_ge(s_ada1[n // 4], 16)
                else:
                    act.wait_ge(s_ada[n % 4], 16 * ((n - ADA_FIRST) // 4 + 1))
                if n >= 2:
                    act.wait_ge(s_ada_pe, n - 1)
                nc.scalar.activation(whi[s][:], ada_source(n), ACT.Copy).then_inc(s_ada_hi, 1)

            def ada_copy(g):
                act.wait_ge(s_ada_pe, 2 * g + 2)
                if g:
                    act.wait_ge(s_ada_t, g)
                nc.scalar.activation(ada_rows[:], ada_row(2 * g), ACT.Copy)\
                    .then_inc(s_ada_cp, 1)

            act.wait_ge(s_cols, 16)
            nc.scalar.activation(silu_c[:], cond, ACT.Silu).then_inc(s_silu_c, 1)
            squares(0, (s_x0, s_x0), ((0, 2), (1, 2)))
            ada_hi(0)
            ada_hi(1)
            for g in range(ADA_FIRST // 2):
                if g + 1 < ADA_FIRST // 2:
                    ada_hi(2 * g + 2)
                ada_copy(g)
                if g + 1 < ADA_FIRST // 2:
                    ada_hi(2 * g + 3)
            act.wait_ge(s_fold, 1)
            modulate(0, 0, 0)

            with act.Fori(0, NQKV // 2) as i:
                for s in range(2):
                    act.wait_ge(s_unit, i * 2 + (s + 1))
                    act.wait_ge(s_conv, i * 2 + PRIMED)
                    nc.scalar.activation(halves(pad[s]), pair["AB"[s]], ACT.Copy).then_inc(s_ev["AB"[s]], 1)
                    act.wait_ge(s_conv, i * 2 + (PRIMED + s + 1))
                    nc.scalar.activation(qkv[:, i * 2 + s, :], cv[s], ACT.Silu).then_inc(s_silu, 1)
            with act.Fori(0, NGATE // 2) as i:
                for s in range(2):
                    act.wait_ge(s_unit, i * 2 + (NQKV + s + 1))
                    nc.scalar.activation(halves(sgate[:, i * 2 + s, :]), pair["AB"[s]], ACT.Silu)\
                        .then_inc(s_ev["AB"[s]], 1)
            act.wait_ge(s_ba, 1)
            act.wait_ge(s_fill, 3)
            bav = ps[:, 7, 0:16 * NT].rearrange("p (t j) -> p t j", t=NT)

            def tiles(v):
                return v.rearrange("p (t j) -> p t j", t=NT)
            nc.scalar.activation(tiles(tmp_a), bav[:, :, 0:8], ACT.Exp, scale=-1.0).then_inc(s_ga, 1)
            nc.scalar.activation(e_alog, col("a_log"), ACT.Exp).then_inc(s_ga, 1)
            act.wait_ge(s_gd, 2)
            nc.scalar.activation(tmp_c, tmp_b, ACT.Abs).then_inc(s_ga, 1)
            act.wait_ge(s_ga, 3)
            nc.scalar.activation(tmp_c, tmp_c, ACT.Exp, scale=-1.0).then_inc(s_ga, 1)
            act.wait_ge(s_ga, 4)
            nc.scalar.activation(tmp_c, tmp_c, ACT.Ln, bias=1.0).then_inc(s_ga, 1)
            act.wait_ge(s_silu, PRIMED + NQKV)
            act.wait_ge(s_acc, 9)
            with act.Fori(0, 2) as i:
                def c_gate(s):
                    act.wait_ge(s_unit, i * 6 + (NQKV + NGATE + 3 * s + 1))
                    act.wait_ge(s_ev["BA"[s]], i * 3 + (PRIMED + 6 + 2 * s))
                    nc.scalar.activation(halves(h32[s]), pair["AB"[s]], ACT.Copy).then_inc(s_ev["AB"[s]], 1)

                def square(m):
                    act.wait_ge(s_l2ln, i * 4 + (PRIMED + max(m - 1, 0)))
                    nc.scalar.activation(sq[m % 2], qkv[:, ds(i * 4 + m, 1), :], ACT.Square).then_inc(s_l2sq, 1)

                def log(m):
                    act.wait_ge(s_l2sum, i * 4 + (m + 1))
                    nc.scalar.activation(halves(lnn[:, i * 4 + m, :]), pair["X"], ACT.Ln, bias=eps_col)\
                        .then_inc(s_l2ln, 1)

                c_gate(0)
                square(0)
                square(1)
                log(0)
                square(2)
                log(1)
                c_gate(1)
                square(3)
                log(2)
                log(3)
            for u in range(8):
                act.wait_ge(s_l2ln, PRIMED + u + 1)
                nc.scalar.activation(lnn[:, u, :], lnn[:, u, :], ACT.Exp, scale=-0.5,
                                     bias=scale_col if u < 4 else 0.0).then_inc(s_l2r, 1)
            act.wait_ge(s_gsum, 1)
            nc.scalar.activation(gcs, ps[:, 7, 128:168], ACT.Copy).then_inc(s_ga, 1)
            nc.scalar.activation(egc, ps[:, 7, 128:168], ACT.Exp).then_inc(s_ga, 1)
            nc.scalar.activation(etot, ps[:, 7, 192:232], ACT.Exp).then_inc(s_ga, 1)
            nc.scalar.activation(tmp_c, ps[:, 7, 192:232], ACT.Copy).then_inc(s_ga, 1)
            act.wait_ge(s_gd, 7)
            nc.scalar.activation(ekg, tmp_a, ACT.Exp).then_inc(s_ga, 1)

            act.wait_ge(s_unit, 28)
            ada_hi(ADA_FIRST)
            for n in range(NT):
                for c in range(2):
                    act.wait_ge(s_dd[c], n + 1)
                    nc.scalar.activation(dec[c], dec[c], ACT.Exp).then_inc(s_dx[c], 1)
                if n == 0:
                    act.wait_ge(s_l2, 8)
                for j, dst in enumerate((ktok, vtok)):
                    act.wait_ge(s_tr, 2 * n + j + 1)
                    nc.scalar.activation(dst[:, n], bank[6], ACT.Copy).then_inc(s_tok, 1)
                for lv in range(LEVELS):
                    g = ADA_FIRST // 2 + ADA_SLOTS.index((n, lv)) if (n, lv) in ADA_SLOTS else None
                    if g is not None:
                        if g - 1 not in batch_end:
                            ada_copy(g - 1)
                        ada_hi(2 * g + 1)
                    for c in range(2 if lv else 0):
                        act.wait_ge(s_y[c], LEVELS * n + lv + 1)
                        if (LEVELS - 1) * n + lv > 1:
                            act.wait_ge(s_z[c], (LEVELS - 1) * n + lv - 1)
                        nc.scalar.activation(ys[c], bank[2 + c], ACT.Copy).then_inc(s_yc[c], 1)
                    if g is not None and 2 * g + 2 < ADA_LAST:
                        ada_hi(2 * g + 2)
                ada_copy(g)
            for s in range(NT):
                for c in range(2):
                    act.wait_ge(s_kq[c], s + 1)
                    if s:
                        act.wait_ge(s_to[c], s)
                    tl = scan_tile(c, s)
                    for h in range(NH):
                        j = tl * 8 + c * NH + h
                        last = nc.scalar.activation(to[c][:, h], bank[4 * c + 1][:, h], ACT.Copy,
                                                    scale=egc[:, j:j + 1])
                    last.then_inc(s_t[c], 1)
            for n in range(NT):
                c, s = done_visits[n]
                act.wait_ge(s_to[c], s + 1)
                for h in range(NH):
                    if n or h:
                        own.sync()
                    own.tick(nc.scalar.activation(junk[:], osum[:, done_order[n], h], ACT.Square,
                                                  accum_out=ssq[:, 0, n * NH + h:n * NH + h + 1]))
            own.sync()
            own.tick(nc.scalar.activation(ssq[:, 1], ssq[:, 0], ACT.Ln, bias=eps_col, scale=1.0 / DK))
            own.sync()
            nc.scalar.activation(ssq[:, 1], ssq[:, 1], ACT.Exp, scale=-0.5).then_inc(s_orr, 1)
            for j in range(NB):
                nc.scalar.activation(hhi[:, 4 + j, :], yb[:, j, :], ACT.Copy).then_inc(s_yhi, 1)
            for n in range(NT):
                act.wait_ge(s_oy, n + 1)
                c0 = TILES[done_order[n]]
                nc.scalar.activation(hhi[:, 0:NH, c0:c0 + P], chain[n % 2][0], ACT.Copy).then_inc(s_yhi, 1)

            squares_after(1, "out")
            modulate(1, 0, 1)
            for layer in range(2):
                if layer == 1:
                    rsqrt_of_sums(2)

                    def pool_modulate(k):
                        act.wait_ge(s_a, 16 + k + 1)
                        for (pc, c0, n, cd) in POOL_RANGES:
                            last = nc.scalar.activation(hp[:, k, pc:pc + n], pad[k % 2][:, c0:c0 + n], ACT.Identity,
                                                        bias=mod[:, 1, 0, k, cd:cd + 1],
                                                        scale=mod[:, 1, 1, k, cd:cd + 1])
                        last.then_inc(s_aff, 1)

                    pool_modulate(0)
                    for k in range(KD):
                        if k + 1 < KD:
                            pool_modulate(k + 1)
                        act.wait_ge(s_mixed, k + 1)
                        nc.scalar.activation(hhi[:, k, :], h32[k % 2], ACT.Copy).then_inc(s_hi, 1)
                    squares_after(3, "pool")
                    modulate(3, 1, 1)
                for g, nf in enumerate(GROUPS):
                    b = SEG["up", layer, g]
                    u, f = b["u"], b["f"]
                    with act.Fori(0, nf) as i:
                        act.wait_ge(s_unit, i * 2 + (u + 1))
                        act.wait_ge(s_conv, i + (PRIMED + NQKV + NB + f))
                        nc.scalar.activation(halves(pad[0]), pair["A"], ACT.Copy).then_inc(s_ev["A"], 1)
                        act.wait_ge(s_conv, i + (PRIMED + NQKV + NB + f + 1))
                        act.wait_ge(s_ev["B"], i + b["B"])
                        nc.scalar.activation(cv[1], cv[0], ACT.Silu).then_inc(s_silu, 1)
                        act.wait_ge(s_ev["B"], i + (b["B"] + 1))
                        nc.scalar.activation(hidhi[:, i, :], h32[0], ACT.Copy).then_inc(s_hid_hi, 1)
                squares_after(2 if layer == 0 else 4, ("down", layer, 2))
            rsqrt_of_sums(4)

        @block.vector
        def _(dve):
            own = Steps(dve, s_dve)

            def add_squares(i, q, s):
                dve.wait_ge(s_sq, i * 2 + (8 * q + s + 1))
                dve.wait_ge(s_acc, i * 2 + (9 * q + s + 1))
                nc.vector.tensor_tensor(acc, acc, sq[s], ALU.add).then_inc(s_acc, 1)

            def clear_acc(q):
                if q:
                    dve.wait_ge(s_norm, q)
                nc.vector.memset(acc, 0.0).then_inc(s_acc, 1)

            def update_x(seg, layer, part, q=None):
                b = SEG[seg]
                if q is not None:
                    clear_acc(q)
                with dve.Fori(0, 4) as i:
                    for s in range(2):
                        n = "CB"[s]
                        k = i * 2 + s
                        dve.wait_ge(s_unit, i * 2 + (b["u"] + s + 1))
                        for bk, pc, ln, xc, cd in PIECES:
                            last = nc.vector.scalar_tensor_tensor(
                                out=x[:, k, xc:xc + ln], in0=pair[n][:, bk, pc:pc + ln],
                                scalar=mod[:, layer, 3 * part + 2, ds(k, 1), cd],
                                in1=x[:, k, xc:xc + ln], op0=ALU.mult, op1=ALU.add)
                        last.then_inc(s_ev[n], 1)
                    if q is not None:
                        for s in range(2):
                            add_squares(i, q, s)

            def add_batch(b):
                first, n = batches[b]
                if b <= NT:
                    dve.wait_ge(s_ada_t, batch_end[b] + 1)
                else:
                    dve.wait_ge(s_ada_pe, first + n)
                nc.vector.tensor_tensor(mod_n[:, first:first + n, :],
                                        ps[:, col_bank[b], ADA_COLS:ADA_COLS + 2 * n]
                                        .rearrange("p (n c) -> p n c", c=2),
                                        b_ada[:, first:first + n, :], ALU.add).then_inc(s_mod, 1)

            def fold_scale(layer, part, g):
                v = mod[:, layer, 3 * part + 1]
                return nc.vector.scalar_tensor_tensor(out=v, in0=v, scalar=1.0, in1=g[:, layer],
                                                      op0=ALU.add, op1=ALU.mult)

            def apply_norm(q, lo0):
                dve.wait_ge(s_rstd, q + 1)
                with dve.Fori(0, 4) as i:
                    for s in range(2):
                        dve.wait_ge(s_aff, i * 2 + (8 * q + PRIMED))
                        nc.vector.tensor_tensor(pad[s], x[:, i * 2 + s, :], rstd, ALU.mult).then_inc(s_a, 1)
                    if lo0 is not None:
                        for s in range(2):
                            k = i * 2 + s
                            dve.wait_ge(s_hi, k + lo0 + 1)
                            nc.vector.tensor_tensor(hlo[:, k, :], h32[s], hhi[:, k, :].bitcast(F32),
                                                    ALU.subtract).then_inc(s_h, 1)

            def conv(src, dst, taps, per=2):
                own.tick(nc.vector.tensor_scalar(dst[:, 1:W - 1], src[:, 1:W - 1], taps[1], None, ALU.mult))
                own.sync()
                own.tick(nc.vector.scalar_tensor_tensor(out=dst[:, 1:W - 1], in0=src[:, 0:W - 2], scalar=taps[0],
                                                        in1=dst[:, 1:W - 1], op0=ALU.mult, op1=ALU.add))
                own.sync()
                nc.vector.scalar_tensor_tensor(out=dst[:, 1:W - 1], in0=src[:, 2:W], scalar=taps[2],
                                               in1=dst[:, 1:W - 1], op0=ALU.mult, op1=ALU.add)\
                    .then_inc(s_conv, 1)

            def zero_pads(bufs):
                for v in bufs:
                    for a, b in ((0, S0), (S0 + SEQ_S, P0), (P0 + SEQ_P, W)):
                        last = nc.vector.memset(v[:, a:b], 0.0)
                return last

            nc.vector.memset(eps_col, EPS).then_inc(s_fill, 1)
            nc.vector.memset(scale_col, -0.5 * float(np.log(DK))).then_inc(s_fill, 1)
            zero_pads(h32 + cv).then_inc(s_fill, 1)
            clear_acc(0)
            dve.wait_ge(s_silu_c, 1)
            for q in range(2):
                own.tick(nc.vector.tensor_copy(c_parts[:, q, :, 0:2], silu_c[:]))
            nc.vector.memset(c_parts[:, 1, :, 2:4].bitcast(F32), 0.0)
            own.sync()
            nc.vector.tensor_tensor(c_parts[:, 0, :, 2:4], silu_c[:], c_parts[:, 0, :, 0:2].bitcast(F32),
                                    ALU.subtract).then_inc(s_c_parts, 1)
            dve.wait_ge(s_x, 16)
            dve.wait_ge(s_pe, 16)
            def add_position(k):
                v = x[:, k, S0:S0 + SEQ_S].rearrange("p (r g) -> p r g", r=ROWS)
                if k < KD // 2:
                    tab = pe_tab[:, k, 0:ROWS].unsqueeze(2).to_broadcast([P, ROWS, GRID_W])
                else:
                    tab = pe_tab[:, k - KD // 2, ROWS:].unsqueeze(1).to_broadcast([P, ROWS, GRID_W])
                nc.vector.tensor_tensor(v, v, tab, ALU.add).then_inc(s_x0, 1)

            for k in range(2):
                add_position(k)
            for i in range(KD // 2):
                if i + 1 < KD // 2:
                    for s in range(2):
                        add_position(i * 2 + 2 + s)
                for s in range(2):
                    add_squares(i, 0, s)
            dve.wait_ge(s_cols, 16)
            own.tick(nc.vector.tensor_copy(wba_hi[:], w_ba))
            own.sync()
            own.tick(nc.vector.tensor_tensor(wba_lo[:], w_ba, wba_hi[:].bitcast(F32), ALU.subtract))
            for n in range(ADA_FIRST):
                dve.wait_ge(s_ada_hi, n + 1)
                nc.vector.tensor_tensor(wlo[n % 2][:], ada_source(n), whi[n % 2][:].bitcast(F32),
                                        ALU.subtract).then_inc(s_ada_lo, 1)
            add_batch(0)
            dve.wait_ge(s_mod, 1)
            fold_scale(0, 0, g_mix).then_inc(s_fold, 1)
            apply_norm(0, 0)

            with dve.Fori(0, NQKV // 2) as i:
                own.enter(i, 4)
                for s in range(2):
                    dve.wait_ge(s_ev["AB"[s]], i + (PRIMED + 1))
                    dve.wait_ge(s_silu, i * 2 + PRIMED)
                    conv(pad[s], cv[s], [tap_qkv[:, j, ds(i * 2 + s, 1)] for j in range(3)])
            own.leave(NQKV // 2)
            dve.wait_ge(s_bat, 1)
            nc.vector.tensor_copy(halves(acc)[0:16], pair["C"][0:16]).then_inc(s_gd, 1)
            dve.wait_ge(s_ba, 1)
            dve.wait_ge(s_ga, 1)
            bav = ps[:, 7, 0:16 * NT].rearrange("p (t j) -> p t j", t=NT)

            def tiles(v):
                return v.rearrange("p (t j) -> p t j", t=NT)
            nc.vector.tensor_tensor(tiles(tmp_b), bav[:, :, 8:16], tiles(col("dt_bias")), ALU.add).then_inc(s_gd, 1)
            nc.vector.tensor_scalar(tmp_a, tmp_a, 1.0, None, ALU.add).then_inc(s_gd, 1)
            dve.wait_ge(s_gd, 3)
            nc.vector.reciprocal(beta, tmp_a).then_inc(s_gd, 1)
            dve.wait_ge(s_ga, 5)
            nc.vector.scalar_tensor_tensor(out=tmp_d, in0=tmp_b, scalar=0.0, in1=tmp_c,
                                           op0=ALU.max, op1=ALU.add).then_inc(s_gd, 1)
            dve.wait_ge(s_gd, 5)
            nc.vector.scalar_tensor_tensor(out=g_log, in0=tmp_d, scalar=-1.0, in1=e_alog,
                                           op0=ALU.mult, op1=ALU.mult).then_inc(s_gd, 1)
            dve.wait_ge(s_silu, PRIMED + NQKV)
            with dve.Fori(0, 2) as i:
                own.enter(i, 4)
                for s in range(2):
                    u0 = NQKV + NGATE + 3 * s
                    pc, ph = "AB"[s], "BA"[s]
                    dve.wait_ge(s_ev[pc], i * 3 + (PRIMED + u0 // 2 + 1))
                    dve.wait_ge(s_unit, i * 6 + (u0 + 2))
                    nc.vector.tensor_tensor(halves(pad[s]), halves(h32[s]), pair[ph], ALU.mult)\
                        .then_inc(s_ev[ph], 1)
                    dve.wait_ge(s_ev[ph], i * 3 + (PRIMED + (u0 + 1) // 2 + 1))
                    conv(pad[s], cv[s], [tap_b[:, j, ds(i * 2 + s, 1)] for j in range(3)])
                    dve.wait_ge(s_conv, i * 2 + (PRIMED + NQKV + s + 1))
                    dve.wait_ge(s_unit, i * 6 + (u0 + 3))
                    nc.vector.tensor_tensor(halves(yb[:, i * 2 + s, :]), halves(cv[s]), pair[pc], ALU.mult)\
                        .then_inc(s_ev[pc], 1)
            own.leave(2)

            for u in range(8):
                dve.wait_ge(s_l2r, u + 1)
                nc.vector.tensor_tensor(qkv[:, u, :], qkv[:, u, :], lnn[:, u, :], ALU.mult).then_inc(s_l2, 1)
            dve.wait_ge(s_ga, 9)
            nc.vector.tensor_tensor(tmp_a, tmp_c, gcs, ALU.subtract).then_inc(s_gd, 1)
            nc.vector.tensor_scalar(negegc, egc, -1.0, None, ALU.mult).then_inc(s_gd, 1)
            dve.wait_ge(s_gd, 8)

            id4 = ident.unsqueeze(1).to_broadcast([P, NH, P])

            def tri_g(n, c):
                for h in range(NH):
                    j = n * 8 + c * NH + h
                    last = nc.vector.tensor_scalar(dec[c][:, h], (tri_u, tri_l)[c], g_log[:, j:j + 1], None, ALU.mult)
                last.then_inc(s_tg[c], 1)

            for n in range(NT):
                for c in range(2):
                    tri_g(n, c)
                for c in range(2):
                    dve.wait_ge(s_bc[c], n + 1)
                    for h in range(NH):
                        j = n * 8 + c * NH + h
                        last = nc.vector.tensor_scalar(dec[c][:, h], bank[2 + c][:, h], gcs[:, j:j + 1], 0.0,
                                                       ALU.subtract, ALU.min)
                    last.then_inc(s_dd[c], 1)
                dve.wait_ge(s_gram, n + 1)
                for c in range(2):
                    dve.wait_ge(s_dx[c], n + 1)
                    if n:
                        dve.wait_ge(s_bt[c], LEVELS * n)
                    for h in range(NH):
                        j = n * 8 + c * NH + h
                        nc.vector.scalar_tensor_tensor(out=mt[c][:, h], in0=dec[c][:, h], scalar=beta[:, j:j + 1],
                                                       in1=bank[0][:, h], op0=ALU.mult, op1=ALU.mult)
                    nc.vector.tensor_tensor(attn[:, 2 * n + c], dec[c], bank[1], ALU.mult).then_inc(s_mt[c], 1)
                for c in range(2):
                    dve.wait_ge(s_y[c], LEVELS * n + 1)
                    nc.vector.tensor_tensor(tt[c], id4, bank[2 + c], ALU.subtract)
                    nc.vector.tensor_tensor(rinv[:, 2 * n + c], id4, bt[c][(LEVELS * n) % 2], ALU.subtract)\
                        .then_inc(s_up[c], 1)
                for lv in range(1, LEVELS):
                    for c in range(2):
                        zb, ztb = ((4, 5), (0, 1))[c]
                        dve.wait_ge(s_z[c], (LEVELS - 1) * n + lv)
                        if lv < LEVELS - 1:
                            nc.vector.tensor_tensor(tt[c], tt[c], bank[zb], ALU.subtract)
                        r = rinv[:, 2 * n + c]
                        nc.vector.tensor_tensor(r, r, bank[ztb], ALU.subtract).then_inc(s_up[c], 1)
                add_batch(n + 1)
            dve.wait_ge(s_mod, NT + 1)
            fold_scale(0, 1, g_ffn).then_inc(s_fold, 1)

            for c in range(2):
                nc.vector.memset(sp_[c], 0.0).then_inc(s_zero, 1)
            for s in range(NT):
                for c in range(2):
                    tl = scan_tile(c, s)
                    dve.wait_ge(s_kq[c], s + 1)
                    for h in range(NH):
                        j = tl * 8 + c * NH + h
                        last = nc.vector.scalar_tensor_tensor(
                            out=rr[c][:, h], in0=bank[4 * c][:, h], scalar=negegc[:, j:j + 1],
                            in1=vtok[:, tl, h], op0=ALU.mult, op1=ALU.add)
                    last.then_inc(s_r[c], 1)
                for c in range(2):
                    tl = scan_tile(c, s)
                    dve.wait_ge(s_tr3[c], s + 1)
                    for h in range(NH):
                        j = tl * 8 + c * NH + h
                        last = nc.vector.tensor_scalar(vn[c][:, h], bank[4 * c][:, h], beta[:, j:j + 1], None,
                                                       ALU.mult)
                    last.then_inc(s_vn[c], 1)
                for c in range(2):
                    tl = scan_tile(c, s)
                    S = ss[c] if s < NT - 1 else sp_[c]
                    dve.wait_ge(s_ap[c], s + 1)
                    for h in range(NH):
                        j = tl * 8 + c * NH + h
                        last = nc.vector.scalar_tensor_tensor(
                            out=S[:, h], in0=S[:, h], scalar=etot[:, j:j + 1], in1=bank[4 * c + 2][:, h],
                            op0=ALU.mult, op1=ALU.add)
                    last.then_inc(s_st[c], 1)
                for c in range(2):
                    tl = scan_tile(c, s)
                    dve.wait_ge(s_t[c], s + 1)
                    if first_visit(c, s):
                        nc.vector.tensor_tensor(osum[:, tl], to[c], bank[4 * c + 3], ALU.add).then_inc(s_to[c], 1)
                    else:
                        dve.wait_ge(s_to[1 - c], s + 1 if s == NT - 1 else NT - 1 - s)
                        own.tick(nc.vector.tensor_tensor(osum[:, tl], osum[:, tl], to[c], ALU.add))
                        own.sync()
                        nc.vector.tensor_tensor(osum[:, tl], osum[:, tl], bank[4 * c + 3], ALU.add)\
                            .then_inc(s_to[c], 1)
            dve.wait_ge(s_orr, 1)
            for n in range(NT):
                for h in range(NH):
                    o = osum[:, done_order[n], h]
                    last = nc.vector.tensor_scalar(o, o, ssq[:, 1, n * NH + h:n * NH + h + 1], None, ALU.mult)
                last.then_inc(s_on, 1)
            for v in (hhi, hlo):
                for a, b in ((0, S0), (S0 + SEQ_S, P0), (P0 + SEQ_P, W)):
                    nc.vector.memset(v[:, 0:NH, a:b].bitcast(F32), 0.0)
            for j in range(NB):
                dve.wait_ge(s_yhi, j + 1)
                nc.vector.tensor_tensor(hlo[:, 4 + j, :], yb[:, j, :], hhi[:, 4 + j, :].bitcast(F32),
                                        ALU.subtract).then_inc(s_yready, 1)
            for n in range(NT):
                c0 = TILES[done_order[n]]
                dve.wait_ge(s_oT, n + 1)
                nc.vector.scalar_tensor_tensor(out=chain[n % 2][0], in0=bank[n % 2], scalar=g_o,
                                               in1=sgate[:, :, c0:c0 + P], op0=ALU.mult, op1=ALU.mult)\
                    .then_inc(s_oy, 1)
                dve.wait_ge(s_yhi, NB + n + 1)
                nc.vector.tensor_tensor(hlo[:, 0:NH, c0:c0 + P], chain[n % 2][0],
                                        hhi[:, 0:NH, c0:c0 + P].bitcast(F32), ALU.subtract).then_inc(s_yready, 1)
            dve.wait_ge(s_nst, 32)
            zero_pads(h32 + cv).then_inc(s_fill, 1)

            update_x("out", 0, 0, q=1)
            apply_norm(1, 8)

            def pooled(k):
                gi = k // 2
                win = 2 << gi
                src, m = hp[:, k, :], WP
                for lv in range(gi + 1):
                    m -= 1 << lv
                    dst = psum_w[:, lv % 2, :]
                    own.tick(nc.vector.tensor_tensor(dst[:, 0:m], src[:, 0:m], src[:, (1 << lv):(1 << lv) + m],
                                                     ALU.add))
                    own.sync()
                    src = dst
                for pc, c0, n, _ in POOL_RANGES:
                    own.tick(nc.vector.tensor_tensor(psum_w[:, 2, c0:c0 + n], src[:, pc - win // 2:pc - win // 2 + n],
                                                     inv_n[:, gi, c0:c0 + n], ALU.mult))
                own.sync()
                for pc, c0, n, _ in POOL_RANGES:
                    last = nc.vector.tensor_tensor(h32[k % 2][:, c0:c0 + n], psum_w[:, 2, c0:c0 + n],
                                                   hp[:, k, pc:pc + n], ALU.subtract)
                last.then_inc(s_mixed, 1)

            def pool_normed(k):
                if k > 1:
                    dve.wait_ge(s_aff, PRIMED + 16 + k - 1)
                nc.vector.tensor_tensor(pad[k % 2], x[:, k, :], rstd, ALU.mult).then_inc(s_a, 1)

            def pool_lo(k):
                dve.wait_ge(s_hi, 16 + k + 1)
                nc.vector.tensor_tensor(hlo[:, k, :], h32[k % 2], hhi[:, k, :].bitcast(F32),
                                        ALU.subtract).then_inc(s_h, 1)

            for layer in range(2):
                if layer == 1:
                    for a in (0, PADW + SEQ_S, WP - PADW):
                        nc.vector.memset(hp[:, :, a:a + PADW], 0.0)
                    dve.wait_ge(s_rstd, 3)
                    dve.wait_ge(s_inv, 16)
                    pool_normed(0)
                    for k in range(KD):
                        if k + 1 < KD:
                            pool_normed(k + 1)
                        dve.wait_ge(s_aff, PRIMED + 16 + k + 1)
                        pooled(k)
                        if k:
                            pool_lo(k - 1)
                    pool_lo(KD - 1)
                    b = SEG["pool"]
                    add_batch(NT + 1)
                    dve.wait_ge(s_mod, NT + 2)
                    fold_scale(1, 1, g_ffn).then_inc(s_fold, 1)
                    clear_acc(3)
                    for m in range(KD):
                        n = "CB"[m % 2]
                        if m % 4 < 3:
                            dve.wait_ge(s_pm, 3 * (m // 4) + m % 4 + 1)
                        else:
                            dve.wait_ge(s_unit, b["u"] + m // 4 + 1)
                        for bk, pc, ln, xc, cd in PIECES:
                            last = nc.vector.scalar_tensor_tensor(
                                out=x[:, m, xc:xc + ln], in0=pair[n][:, bk, pc:pc + ln],
                                scalar=mod[:, 1, 2, m, cd:cd + 1], in1=x[:, m, xc:xc + ln],
                                op0=ALU.mult, op1=ALU.add)
                        last.then_inc(s_ev[n], 1)
                        if m % 2:
                            for s in range(2):
                                add_squares(m // 2, 3, s)
                    apply_norm(3, 24)
                for g, nf in enumerate(GROUPS):
                    b = SEG["up", layer, g]
                    u, f = b["u"], b["f"]
                    with dve.Fori(0, nf) as i:
                        own.enter(i, 2)
                        dve.wait_ge(s_ev["A"], i + (b["A"] + 1))
                        dve.wait_ge(s_silu, i + (PRIMED + NQKV + f))
                        conv(pad[0], cv[0], [tap_ffn[:, layer, j, ds(i + GROUP_AT[g], 1)] for j in range(3)])
                        dve.wait_ge(s_silu, i + (PRIMED + NQKV + f + 1))
                        dve.wait_ge(s_unit, i * 2 + (u + 2))
                        dve.wait_ge(s_hid_hi, i + (f + PRIMED))
                        nc.vector.tensor_tensor(halves(h32[0]), halves(cv[1]), pair["B"], ALU.mult)\
                            .then_inc(s_ev["B"], 1)
                        dve.wait_ge(s_hid_hi, i + (f + PRIMED + 1))
                        nc.vector.tensor_tensor(hidlo[:, i, :], h32[0], hidhi[:, i, :].bitcast(F32),
                                                ALU.subtract).then_inc(s_hid, 1)
                    own.leave(nf)
                    if layer == 0 and g == 2:
                        fold_scale(1, 0, g_mix)
                        nc.vector.tensor_tensor(mod[:, 1, 2], mod[:, 1, 2], g_pool, ALU.mult).then_inc(s_fold, 1)
                    update_x(("down", layer, g), layer, 1, q=((2, 4)[layer] if g == 2 else None))
                if layer == 0:
                    pass
            dve.wait_ge(s_rstd, 5)
            for k in range(KD):
                nc.vector.scalar_tensor_tensor(out=yout[:, k, :], in0=x[:, k, :], scalar=g_final[:, k:k + 1],
                                               in1=rstd, op0=ALU.mult, op1=ALU.mult).then_inc(s_ychunk, 1)


IN_ORDER = list(range(NQKV + NGATE)) + [NQKV + NGATE + p * NB + j for j in range(NB) for p in (1, 2, 0)]


def kernel(**inputs):
    import concourse.bacc as bacc
    from concourse.bass_utils import run_bass_kernel_spmd

    a = {k: np.asarray(v) for k, v in inputs.items()}

    def tiles(w, rows):
        k, n = w.shape
        return np.ascontiguousarray(
            w.reshape(k // P, P, n // P, P).transpose(2, 1, 0, 3).reshape(n // P, P, rows * P))

    def chunks(v):
        v = v.reshape(v.shape[:-1] + (-1, P))
        return np.moveaxis(v, -1, 0)

    def twice(v):
        return np.repeat(v[..., None], 2, axis=-1)

    arrays = {}
    x = np.zeros((P, KD, W), np.float32)
    x[:, :, S0:S0 + SEQ_S] = a["x_sample"][0].T.reshape(KD, P, SEQ_S).transpose(1, 0, 2)
    x[:, :, P0:P0 + SEQ_P] = a["x_prompt"][0].T.reshape(KD, P, SEQ_P).transpose(1, 0, 2)
    arrays["x"] = x
    w_in = a["w_in_ab"][0]
    nqg = (NQKV + NGATE) * P
    main = tiles(np.concatenate([w_in[:, :nqg], w_in[:, nqg + 16:]], axis=1), KD)
    arrays["w_in"] = main[IN_ORDER]
    arrays["w_out"] = tiles(a["w_out_ab"][0], KD)
    wp = a["w_pool"][0].reshape(4, 2, P, 2, P).transpose(2, 0, 3, 1, 4)
    arrays["w_pool"] = np.ascontiguousarray(wp.reshape(P, 2, SLOT).transpose(1, 0, 2))
    arrays["w_gu"] = np.concatenate([
        np.stack([tiles(a["w_ffn_gate"][l], KD), tiles(a["w_ffn_up"][l], KD)], axis=1).reshape(2 * NF, P, SLOT)
        for l in range(2)])
    for g, nf in enumerate(GROUPS):
        rows = slice(GROUP_AT[g] * P, (GROUP_AT[g] + nf) * P)
        arrays[f"w_dn{g}"] = np.concatenate([tiles(a["w_ffn_down"][l][rows], nf) for l in range(2)])
    w_ada = np.concatenate([a["w_ada"][0], a["w_ada"][1]], axis=1)
    groups = w_ada[:, :ADA_LAST * P].reshape(2, 4, P, ADA_LAST // 2, ADA_COLS)
    arrays["w_ada"] = np.concatenate([
        groups.transpose(3, 0, 2, 1, 4).reshape(ADA_LAST, P, SLOT), tiles(w_ada[:, ADA_LAST * P:], KD)])
    ncol = nqg
    packed = {
        "norm_mix": twice(chunks(a["norm_mix_g"])),
        "norm_ffn": twice(chunks(a["norm_ffn_g"])),
        "pool_scale": twice(chunks(a["pool_scale"][0])),
        "final": chunks(a["final_norm_g"]),
        "tap_qkv": chunks(a["conv_qkv"][0]),
        "tap_b": chunks(a["conv_b"][0]),
        "tap_ffn": chunks(a["ffn_conv"]),
        "o_norm": a["o_norm_g"][0][:, None],
        "a_log": np.broadcast_to(a["a_log"][0].reshape(1, 1, 8), (P, NT, 8)),
        "dt_bias": np.broadcast_to(a["dt_bias"][0].reshape(1, 1, 8), (P, NT, 8)),
        "w_ba": w_in[:, ncol:ncol + 16].reshape(KD, P, 16).transpose(1, 0, 2),
        "cond": np.stack([chunks(a["c"][0]), chunks(a["c_ctx"])], axis=-1),
        "sel": (np.arange(P)[:, None] % 2 == np.arange(2)[None, :]).astype(np.float32),
        "b_ada": twice(chunks(a["b_ada"].reshape(-1))),
    }
    cols = np.zeros((P, NCOLS), np.float32)
    for name, (at, n) in COLS.items():
        cols[:, at:at + n] = packed[name].reshape(P, n)
    arrays["cols"] = cols
    arrays["state"] = np.ascontiguousarray(a["state_delta"][0, 0].transpose(2, 0, 1, 3))

    quarter = D // 4
    omega = (1.0 / (10000.0 ** (np.arange(quarter, dtype=np.float32) / quarter))).astype(np.float32)

    def sincos(n):
        e = np.arange(n, dtype=np.float32)[:, None] * omega[None, :]
        return np.concatenate([np.sin(e), np.cos(e)], axis=-1)

    pe = np.zeros((P, 4, ROWS + GRID_W), np.float32)
    pe[:, :, :ROWS] = sincos(ROWS).T.reshape(4, P, ROWS).transpose(1, 0, 2)
    pe[:, :, ROWS:] = sincos(GRID_W).T.reshape(4, P, GRID_W).transpose(1, 0, 2)
    arrays["pe"] = pe
    r, c = np.arange(P)[:, None], np.arange(P)[None, :]
    arrays["const"] = np.stack([r == c, r <= c, r >= c, r >= 0 * c], axis=1).astype(np.float32)
    lm = np.zeros((P, 2 * LEVELS, P), np.float16)
    for lv in range(LEVELS):
        b = 1 << lv
        same = r // (2 * b) == c // (2 * b)
        lm[:, lv] = same & (r // b % 2 == 0) & (c // b % 2 == 1)
        lm[:, LEVELS + lv] = same & (r // b % 2 == 1) & (c // b % 2 == 0)
    arrays["lmask"] = lm
    inv = np.zeros((P, 4, W), np.float32)
    for gi in range(4):
        w = 2 << gi
        for c0, n, _ in RANGES:
            tk = np.arange(n)
            inv[:, gi, c0:c0 + n] = 1.0 / (np.clip(tk - w // 2 + w, 0, n) - np.clip(tk - w // 2, 0, n))
    arrays["inv_n"] = inv

    nc = bacc.Bacc("TRN2", target_bir_lowering=False, num_devices=1)
    t = {}
    for name, v in arrays.items():
        t[name] = nc.dram_tensor(f"in_{name}", v.shape, mybir.dt.from_np(v.dtype), kind="ExternalInput").ap()
    t["y"] = nc.dram_tensor("out_y", (P, KD, SEQ_S + SEQ_P), F32, kind="ExternalOutput").ap()
    t["new_state"] = nc.dram_tensor("out_state", (P, 2, NH, P), F32, kind="ExternalOutput").ap()
    build(nc, t)
    res = run_bass_kernel_spmd(nc, [{f"in_{k}": v for k, v in arrays.items()}], core_ids=[0]).results[0]
    y = res["out_y"].transpose(2, 1, 0).reshape(SEQ_S + SEQ_P, D)
    y_sample = np.ascontiguousarray(y[:SEQ_S])[None]
    y_prompt = np.ascontiguousarray(y[SEQ_S:])[None]
    new_state = np.ascontiguousarray(res["out_state"].transpose(1, 2, 0, 3))[None, None]
    return y_prompt, y_sample, new_state
```

```python
from contextlib import ExitStack

import numpy as np

import concourse.bass as bass
from concourse import mybir

P = 128
D = 1024
KD = D // P
SEQ_S, SEQ_P = 512, 128
GRID_W = 64
ROWS = SEQ_S // GRID_W
S0 = 1
P0 = S0 + SEQ_S + 1
W = P0 + SEQ_P + 2
HALF = W // 2
RANGES = [(S0, SEQ_S, 0), (P0, SEQ_P, 1)]
NH, DK = 4, 128
NQKV, NGATE, NB = 12, 4, 4
D_FF = 2816
NF = D_FF // P
ADA_COLS = 2 * P
ADA_FIRST = 16
ADA_LAST = 80
ADA_DIRECT = [4, 8, 4]
ADA_POOL = 7
ADA_USES = [[80, 82, 92, 94], [81, 83, 91, 93, 95]]
GROUPS = [8, 7, 7]
EPS = 1e-6
TILES = [S0 + P * t for t in range(SEQ_S // P)] + [P0]
NT = len(TILES)
LEVELS = 7
PADW = 8
WP = PADW + SEQ_S + PADW + SEQ_P + PADW
POOL_RANGES = [(PADW, S0, SEQ_S, 0), (PADW + SEQ_S + PADW, P0, SEQ_P, 1)]
SLOT = KD * P
PRIMED = 4

F32 = mybir.dt.float32
F32R = mybir.dt.float32r
F16 = mybir.dt.float16
ALU = mybir.AluOpType
ACT = mybir.ActivationFunctionType
ds = bass.ds

PIECES = [(0, S0, HALF - S0, S0, 0), (1, 0, S0 + SEQ_S - HALF, HALF, 0), (1, P0 - HALF, SEQ_P, P0, 1)]

COLS, _at = {}, 0
for _name, _n in (("norm_mix", 2 * KD * 2), ("norm_ffn", 2 * KD * 2), ("pool_scale", KD * 2),
                  ("final", KD), ("tap_qkv", 3 * NQKV), ("tap_b", 3 * NB), ("tap_ffn", 2 * 3 * NF),
                  ("o_norm", 1), ("a_log", NT * 8), ("dt_bias", NT * 8), ("w_ba", KD * 16),
                  ("cond", KD * 2), ("b_ada", 96 * 2), ("sel", 2)):
    COLS[_name] = (_at, _n)
    _at += _n
NCOLS = _at


def plan():
    at = dict(u=0, A=PRIMED, B=PRIMED, C=PRIMED, f=0)
    segs = {"in": dict(at)}
    at["u"] += 28; at["A"] += 14; at["B"] += 14
    segs["out"] = dict(at)
    at["u"] += 8; at["C"] += 4; at["B"] += 4
    for layer in range(2):
        if layer == 1:
            segs["pool"] = dict(at)
            at["u"] += 2; at["C"] += 4; at["B"] += 4
        for g, nf in enumerate(GROUPS):
            segs["up", layer, g] = dict(at)
            at["u"] += 2 * nf; at["A"] += nf; at["B"] += nf; at["f"] += nf
            segs["down", layer, g] = dict(at)
            at["u"] += 8; at["C"] += 4; at["B"] += 4
    return segs


SEG = plan()
L2_AFTER = [1, 2, 4, 5]
ADA_SLOTS = [(n, lv) for n in range(NT) for lv in range(0 if n >= NT - 2 else 1, LEVELS)]
assert len(ADA_SLOTS) == (ADA_LAST - ADA_FIRST) // 2
ADA_BEFORE = [range(ADA_LAST + a, ADA_LAST + b) for a, b in ((4, 6), (6, 8), (8, 10), (10, 12))]
GROUP_AT = [sum(GROUPS[:g]) for g in range(len(GROUPS))]


class Steps:

    def __init__(self, eng, sem):
        self.eng, self.sem, self.done, self.more = eng, sem, 0, 0

    def tick(self, ins):
        ins.then_inc(self.sem, 1)
        self.done += 1

    def sync(self, back=0):
        if self.done:
            self.eng.wait_ge(self.sem, self.more + self.done - back)

    def enter(self, i, per):
        self.start, self.per, self.more = self.done, per, i * per

    def leave(self, n):
        assert self.done - self.start == self.per, (self.done - self.start, self.per)
        self.more = 0
        self.done = self.start + n * self.per


def build(nc, t):
    ctx = ExitStack()
    with ctx:
        def sb(name, shape, dt=F32):
            return ctx.enter_context(nc.sbuf_tensor(name, shape, dt))

        def sem(name):
            return ctx.enter_context(nc.semaphore(name))

        x = sb("x", [P, KD, W])
        raw = [sb(f"raw{s}", [P, SLOT]) for s in range(2)]
        whi = [sb(f"whi{s}", [P, SLOT], F32R) for s in range(2)]
        wlo = [sb(f"wlo{s}", [P, SLOT], F32R) for s in range(2)]
        ada_raw = [sb(f"ada_raw{s}", [P, SLOT]) for s in range(2)]
        cols = sb("cols", [P, NCOLS])
        const = sb("const", [P, 4, P])
        mod = sb("mod", [P, 2, 6, KD, 2])
        silu_c = sb("silu_c", [P, KD, 2])
        c_parts = sb("c_parts", [P, 2, KD, 4], F32R)
        warm = sb("warm", [P, 1])
        ada_rows = sb("ada_rows", [4, ADA_COLS])
        wba_hi = sb("wba_hi", [P, KD, 16], F32R)
        wba_lo = sb("wba_lo", [P, KD, 16], F32R)
        bias = sb("bias", [P, 2])
        gates = sb("gates", [P, 12, NT * 8])
        junk = sb("junk", [P, NH, P])
        ssq = sb("ssq", [P, 2, NT * NH])
        ident, tri_u, tri_l, ones = (const[:, j, :] for j in range(4))
        eps_col, scale_col = bias[:, 0:1], bias[:, 1:2]

        work = sb("work", [P, 10, W])
        pad = [work[:, 0, :], work[:, 1, :]]
        cv = [work[:, 2, :], work[:, 3, :]]
        h32 = [work[:, 4, :], work[:, 5, :]]
        hb = h32 + cv
        sq = [work[:, 6, :], work[:, 7, :]]
        acc = work[:, 8, :]
        rstd = work[:, 9, :]
        flat = work[:, :, :].rearrange("p a b -> p (a b)")
        chain = [[flat[:, (2 * j + c) * 512:(2 * j + c + 1) * 512].rearrange("p (h e) -> p h e", h=NH)
                  for c in range(2)] for j in range(6)]
        dec, mt, tt, btx, bty, ys = chain
        bt = [[btx[c], bty[c]] for c in range(2)]
        rr, vn, to, kg = chain[:4]
        ss, sp_ = ([ada_raw[j][:, c * 512:(c + 1) * 512].rearrange("p (h e) -> p h e", h=NH) for c in range(2)]
                   for j in range(2))

        off_h = nc.sbuf_base
        size_h = 2 * KD * W * 4
        hhi = nc.alloc_sbuf_tensor_at("hhi", [P, KD, W], F32R, offset=off_h)
        hlo = nc.alloc_sbuf_tensor_at("hlo", [P, KD, W], F32R, offset=off_h + size_h // 2)
        rinv = nc.alloc_sbuf_tensor_at("rinv", [P, 2 * NT, NH, P], F32, offset=off_h)
        attn = nc.alloc_sbuf_tensor_at("attn", [P, 2 * NT, NH, P], F32, offset=off_h + NT * 2 * 2048)
        assert NT * 4 * 2048 <= size_h

        off_m = off_h + size_h
        qkv = nc.alloc_sbuf_tensor_at("qkv", [P, NQKV, W], F32, offset=off_m)
        osum = nc.alloc_sbuf_tensor_at("osum", [P, NT, NH, P], F32, offset=off_m + 8 * W * 4)
        o2 = off_m + NQKV * W * 4
        ktok = nc.alloc_sbuf_tensor_at("ktok", [P, NT, NH, P], F32, offset=o2)
        vtok = nc.alloc_sbuf_tensor_at("vtok", [P, NT, NH, P], F32, offset=o2 + NT * 2048)
        lnn = nc.alloc_sbuf_tensor_at("lnn", [P, 8, W], F32, offset=o2)
        o3 = o2 + max(NT * 4096, 8 * W * 4)
        sgate = nc.alloc_sbuf_tensor_at("sgate", [P, NGATE, W], F32, offset=o3)
        yb = nc.alloc_sbuf_tensor_at("yb", [P, NB, W], F32, offset=o3 + NGATE * W * 4)
        o4 = o3 + (NGATE + NB) * W * 4
        lmask = nc.alloc_sbuf_tensor_at("lmask", [P, 2 * LEVELS, P], F16, offset=o4)
        end_m = o4 + 2 * LEVELS * P * 2
        ada_first = nc.alloc_sbuf_tensor_at("ada_first", [P, ADA_FIRST, SLOT], F32, offset=off_m)
        pe_tab = nc.alloc_sbuf_tensor_at("pe_tab", [P, 4, ROWS + GRID_W], F32, offset=off_h)
        more = [nc.alloc_sbuf_tensor_at(f"more{j}", [P, SLOT], F32R, offset=off_h + 2048 + j * SLOT * 4)
                for j in range(4)]
        assert ADA_FIRST * SLOT * 4 <= o4 - off_m
        hidhi = nc.alloc_sbuf_tensor_at("hidhi", [P, KD, W], F32R, offset=off_m)
        hidlo = nc.alloc_sbuf_tensor_at("hidlo", [P, KD, W], F32R, offset=off_m + KD * W * 4)
        inv_at = off_m + 2 * KD * W * 4
        yout = nc.alloc_sbuf_tensor_at("yout", [P, KD, W], F32, offset=off_h)
        inv_n = nc.alloc_sbuf_tensor_at("inv_n", [P, 4, W], F32, offset=inv_at)
        hp = nc.alloc_sbuf_tensor_at("hp", [P, KD, WP], F32, offset=inv_at + 4 * W * 4)
        psum_w = nc.alloc_sbuf_tensor_at("psum_w", [P, 4, WP], F32, offset=off_m)
        ada_pool = nc.alloc_sbuf_tensor_at("ada_pool", [P, ADA_POOL, SLOT], F32, offset=off_m + 4 * WP * 4)
        assert 4 * WP * 4 + ADA_POOL * SLOT * 4 <= 2 * KD * W * 4
        assert inv_at + 4 * W * 4 + KD * WP * 4 <= end_m and end_m <= nc.sbuf_usable_end, end_m

        ps = ctx.enter_context(nc.psum_tensor("ps", [P, 8, 512], F32))
        pair = {n: ps[:, 2 * j:2 * j + 2, 0:HALF] for j, n in enumerate("ABCX")}
        bank = [ps[:, j, :].rearrange("p (h e) -> p h e", h=NH) for j in range(8)]

        def halves(ap):
            return ap.rearrange("p (b n) -> p b n", b=2)

        def col(name, pattern=None, **dims):
            a, n = COLS[name]
            v = cols[:, a:a + n]
            return v.rearrange(pattern, **dims) if pattern else v

        g_mix = col("norm_mix", "p (l k c) -> p l k c", l=2, k=KD)
        g_ffn = col("norm_ffn", "p (l k c) -> p l k c", l=2, k=KD)
        g_pool = col("pool_scale", "p (k c) -> p k c", k=KD)
        g_final = col("final")
        tap_qkv = col("tap_qkv", "p (t n) -> p t n", t=3)
        tap_b = col("tap_b", "p (t n) -> p t n", t=3)
        tap_ffn = col("tap_ffn", "p (l t n) -> p l t n", l=2, t=3)
        g_o = col("o_norm")
        w_ba = col("w_ba", "p (k n) -> p k n", k=KD)
        cond = col("cond", "p (k c) -> p k c", k=KD)
        b_ada = col("b_ada", "p (n c) -> p n c", c=2)
        mod_n = mod[:].rearrange("p l s k c -> p (l s k) c")

        (beta, g_log, e_alog, gcs, egc, ekg, etot, negegc, tmp_a, tmp_b, tmp_c, tmp_d) = (
            gates[:, j, :] for j in range(12))

        s_cols = sem("cols_loaded")
        s_x = sem("x_loaded")
        s_const = sem("const_loaded")
        s_pe = sem("pe_loaded")
        s_ada1 = [sem(f"ada_first_loaded{q}") for q in range(4)]
        s_state = sem("state_loaded")
        s_inv = sem("inv_loaded")
        s_raw = [sem(f"weights_loaded{s}") for s in range(2)]
        s_ada = [sem(f"ada_loaded{s}") for s in range(4)]
        s_go = sem("units_begun")
        s_whi = sem("weights_hi")
        s_split = sem("weights_split")
        s_unit = sem("units_multiplied")
        s_ev = {n: sem(f"pair{n}_read") for n in "ABC"}
        s_c_parts = sem("c_parts_ready")
        s_ada_hi = sem("ada_hi")
        s_ada_lo = sem("ada_lo")
        s_ada_pe = sem("ada_multiplied")
        s_ada_cp = sem("ada_rows_copied")
        s_ada_t = sem("ada_columns")
        s_mod = sem("mod_batches_written")
        s_silu_c = sem("silu_c_ready")
        s_fill = sem("constants_filled")
        s_x0 = sem("x_with_positions")
        s_sq = sem("squares_ready")
        s_acc = sem("squares_added")
        s_norm = sem("square_sums")
        s_rstd = sem("rstd_ready")
        s_a = sem("normed_ready")
        s_aff = sem("modulated")
        s_hi = sem("h_hi_ready")
        s_h = sem("h_ready")
        s_conv = sem("convs_done")
        s_silu = sem("silus_done")
        s_hid_hi = sem("hidden_hi_ready")
        s_hid = sem("hidden_ready")
        s_dve = sem("dve_steps")
        s_act = sem("act_steps")
        s_out = sem("outputs_written")
        s_xg = sem("x_scaled")
        s_ychunk = [sem(f"y_chunks_{e}") for e in ("vector", "gpsimd")]
        s_fold = sem("scales_folded")
        s_lmask = sem("level_masks_loaded")
        s_nst = sem("new_states_written")
        s_zero = sem("prompt_states_zero")
        s_pm = sem("pool_products")
        s_mean = sem("pool_means")
        s_ada_pool = sem("ada_pool_loaded")
        s_mixed = sem("pool_mixed")
        s_l2sq = sem("qk_squares")
        s_l2sum = sem("qk_square_sums")
        s_l2ln = sem("qk_logs")
        s_l2r = sem("qk_rsqrt")
        s_l2 = sem("qk_normed")
        s_bat = sem("beta_alpha_rows")
        s_ba = sem("beta_alpha_products")
        s_ga = sem("gate_steps_scalar")
        s_gd = sem("gate_steps_vector")
        s_gsum = sem("gate_sums")
        s_tr = sem("kv_transposed")
        s_tok = sem("kv_tokens_copied")
        s_gram = sem("gram_products")
        s_tg = [sem(f"tri_g{c}") for c in range(2)]
        s_bc = [sem(f"gc_rows{c}") for c in range(2)]
        s_dd = [sem(f"decay_arg{c}") for c in range(2)]
        s_dx = [sem(f"decay_exp{c}") for c in range(2)]
        s_mt = [sem(f"mt_ready{c}") for c in range(2)]
        s_am = sem("attn_decayed")
        s_at = [sem(f"attn_masked{c}") for c in range(2)]
        s_bt = [sem(f"level_block{c}") for c in range(2)]
        s_y = [sem(f"bt_product{c}") for c in range(2)]
        s_yc = [sem(f"bt_product_copied{c}") for c in range(2)]
        s_z = [sem(f"level_products{c}") for c in range(2)]
        s_up = [sem(f"level_updated{c}") for c in range(2)]
        s_kq = [sem(f"scan_kq{c}") for c in range(2)]
        s_r = [sem(f"scan_r{c}") for c in range(2)]
        s_t = [sem(f"scan_t{c}") for c in range(2)]
        s_tr3 = [sem(f"scan_solve{c}") for c in range(2)]
        s_vn = [sem(f"scan_vnew{c}") for c in range(2)]
        s_kg = [sem(f"scan_kg{c}") for c in range(2)]
        s_ap = [sem(f"scan_products{c}") for c in range(2)]
        s_st = [sem(f"scan_state{c}") for c in range(2)]
        s_to = [sem(f"scan_o{c}") for c in range(2)]
        s_orr = sem("o_rsqrt")
        s_on = sem("o_normed")
        s_oT = sem("o_transposed")
        s_oy = sem("o_gated")
        s_yhi = sem("y_hi")
        s_yready = sem("y_ready")

        def level_mask(d, lv):
            return lmask[:, d * LEVELS + lv, :].unsqueeze(1).to_broadcast([P, NH, P])

        def tri_mask(d):
            return (tri_u, tri_l)[d].unsqueeze(1).to_broadcast([P, NH, P])

        def scan_tile(c, s):
            return NT - 1 if s == NT - 1 else (s if c == 0 else NT - 2 - s)

        def first_visit(c, s):
            return s == NT - 1 and c == 0 or s < (NT - 1) // 2

        done_visits = [(c, s) for s in range(NT) for c in range(2) if not first_visit(c, s)]
        done_order = [scan_tile(c, s) for c, s in done_visits]

        O_BANKS = (0, 1, 6, 7)

        batches = [(0, ADA_FIRST)]
        for n in range(NT):
            batches.append((sum(batches[-1]), 2 * sum(m == n for m, _ in ADA_SLOTS)))
        for n in ADA_DIRECT:
            batches.append((sum(batches[-1]), n))
        batch_end = [sum(b) // 2 - 1 for b in batches]
        row_banks = [(4, 5)] + [(7, 7)] * NT
        col_bank = [0] + [7] * (NT + 1) + [0, 7]

        def batch_of(n):
            return next(b for b in range(len(batches)) if n < sum(batches[b]))

        def ada_row(n):
            return ps[0:4, row_banks[batch_of(n)][n // 2 % 2], 0:ADA_COLS]

        def ada_split(n):
            j = n % 4 if n < ADA_FIRST else n % 2
            return (whi + more[0:2])[j], (wlo + more[2:4])[j]

        def ada_source(n):
            return ada_first[:, n, :] if n < ADA_FIRST else (ada_raw + raw)[n % 4][:]

        block = ctx.enter_context(nc.Block())

        @block.sync
        def _(sp):
            def load(u, s, src, n=SLOT):
                sp.wait_ge(s_split, u - 1)
                sp.dma_start(raw[s][:, 0:n], src).then_inc(s_raw[s], 16)

            def load_ada(n, s):
                sp.wait_ge(s_ada_lo, n + (ADA_FIRST - 3))
                sp.dma_start((ada_raw + raw)[s][:], t["w_ada"][n + ADA_FIRST]).then_inc(s_ada[s], 16)

            def load_ada_direct(n, s):
                i = ADA_USES[s].index(n)
                if i:
                    sp.wait_ge(s_ada_pe, ADA_USES[s][i - 1] + 1)
                sp.dma_start(ada_raw[s][:], t["w_ada"][n]).then_inc(s_ada[s], 16)

            for sm in (*s_ev.values(), s_conv, s_silu, s_aff, s_h, s_hid_hi, s_l2ln):
                sp.sem_inc(sm, PRIMED)
            sp.dma_start(cols[:], t["cols"]).then_inc(s_cols, 16)
            sp.dma_start(pe_tab[:], t["pe"]).then_inc(s_pe, 16)
            sp.dma_start(x[:], t["x"]).then_inc(s_x, 16)
            sp.dma_start(const[:], t["const"]).then_inc(s_const, 16)
            n = ADA_FIRST // 4
            for q in range(4):
                sp.dma_start(ada_first[:, n * q:n * (q + 1), :],
                             t["w_ada"][n * q:n * (q + 1)].rearrange("u p f -> p u f")).then_inc(s_ada1[q], 16)
            for s in range(2):
                sp.dma_start(raw[s][:], t["w_in"][s]).then_inc(s_raw[s], 16)
            for s in range(2):
                sp.dma_start(ada_raw[s][:], t["w_ada"][ADA_FIRST + s]).then_inc(s_ada[s], 16)
            sp.dma_start(lmask[:], t["lmask"]).then_inc(s_lmask, 16)
            with sp.Fori(1, 14) as i:
                for s in range(2):
                    load(i * 2 + s, s, t["w_in"][i * 2 + s])
            sp.wait_ge(s_split, 28)
            for s in range(2):
                sp.dma_start(raw[s][:], t["w_ada"][ADA_FIRST + 2 + s]).then_inc(s_ada[2 + s], 16)
            with sp.Fori(1, (ADA_LAST - ADA_FIRST) // 4) as i:
                for s in range(4):
                    load_ada(i * 4 + s, s)
            sp.wait_ge(s_ada_lo, ADA_LAST)
            for c in range(2):
                sp.dma_start(ss[c], t["state"][:, c]).then_inc(s_state, 16)
            u = SEG["out"]["u"]
            for s in range(2):
                load(u + s, s, t["w_out"][s])
            for c in range(2):
                sp.wait_ge(s_st[c], NT)
                sp.dma_start(t["new_state"][:, c], sp_[c]).then_inc(s_nst, 16)
            with sp.Fori(1, 4) as i:
                for s in range(2):
                    load(i * 2 + (u + s), s, t["w_out"][i * 2 + s])
            sp.wait_ge(s_nst, 32)
            for s in range(2):
                load_ada_direct(ADA_LAST + s, s)
            for layer in range(2):
                if layer == 1:
                    u = SEG["pool"]["u"]
                    for s in range(2):
                        load(u + s, s, t["w_pool"][s])
                    n = ADA_LAST + ADA_DIRECT[0]
                    sp.wait_ge(s_unit, u)
                    sp.dma_start(ada_pool[:], t["w_ada"][n:n + ADA_POOL].rearrange("u p f -> p u f"))\
                        .then_inc(s_ada_pool, 16)
                u = SEG["up", layer, 0]["u"]
                for s in range(2):
                    load(u + s, s, t["w_gu"][2 * NF * layer + s])
                for n in ((82, 83, 91, 92), (93, 94, 95))[layer]:
                    load_ada_direct(n, n % 2)
                for g, nf in enumerate(GROUPS):
                    u = SEG["up", layer, g]["u"]
                    f0 = layer * NF + GROUP_AT[g]
                    with sp.Fori(0 if g else 1, nf) as i:
                        for s in range(2):
                            load(i * 2 + (u + s), s, t["w_gu"][i * 2 + (2 * f0 + s)])
                    if layer == 0 and g == 0:
                        sp.wait_ge(s_unit, SEG["up", 0, 0]["u"])
                        sp.dma_start(inv_n[:], t["inv_n"]).then_inc(s_inv, 16)
                    u = SEG["down", layer, g]["u"]
                    with sp.Fori(0, 4) as i:
                        for s in range(2):
                            load(i * 2 + (u + s), s, t[f"w_dn{g}"][i * 2 + (8 * layer + s)], nf * P)
            for k in range(KD):
                e = k % 3 == 2
                sp.wait_ge(s_ychunk[e], (k + 1) // 3 if e else k + 1 - (k + 1) // 3)
                for (c0, n, cd) in RANGES:
                    sp.dma_start(t["y"][:, k, SEQ_S * cd:SEQ_S * cd + n], yout[:, k, c0:c0 + n]).then_inc(s_out, 16)
            sp.wait_ge(s_out, 16 * 2 * KD)
            sp.wait_ge(s_nst, 32)

        @block.gpsimd
        def _(pool):
            def split(u, half_u, s, n=SLOT, guard=True):
                pool.wait_ge(s_raw[s], half_u * 16 + 16)
                if guard:
                    pool.wait_ge(s_unit, u - 1)
                pool.sem_inc(s_go, 1)
                nc.gpsimd.tensor_scalar(whi[s][:, 0:n], raw[s][:, 0:n], 1.0, 0.0,
                                        ALU.mult, ALU.add).then_inc(s_whi, 1)
                pool.wait_ge(s_whi, u + 1)
                nc.gpsimd.tensor_tensor(wlo[s][:, 0:n], raw[s][:, 0:n], whi[s][:, 0:n].bitcast(F32),
                                        ALU.subtract).then_inc(s_split, 1)

            def split_pairs(u, n_pairs, n=SLOT, first=0):
                with pool.Fori(first, n_pairs) as i:
                    for s in range(2):
                        split(i * 2 + (u + s), i + u // 2, s, n)

            def ada_lo(n):
                pool.wait_ge(s_ada_hi, n + 1)
                hi, lo = ada_split(n)
                nc.gpsimd.tensor_tensor(lo[:], ada_source(n), hi[:].bitcast(F32),
                                        ALU.subtract).then_inc(s_ada_lo, 1)

            pool.wait_ge(s_ada_pe, ADA_FIRST)
            for s in range(2):
                split(s, 0, s, guard=False)
            split_pairs(0, 14, first=1)
            pool.wait_ge(s_lmask, 16)
            def level_blocks(n, lv):
                for c in range(2):
                    if lv == 0:
                        pool.wait_ge(s_mt[c], n + 1)
                    if LEVELS * n + lv >= 2:
                        pool.wait_ge(s_y[c], LEVELS * n + lv - 1)
                    if lv == 2:
                        pool.wait_ge(s_up[c], LEVELS * n + 1)
                    nc.gpsimd.tensor_tensor(bt[c][(LEVELS * n + lv) % 2], mt[c], level_mask(c, lv),
                                            ALU.mult).then_inc(s_bt[c], 1)

            for n in range(NT):
                level_blocks(n, 0)
                for lv in range(LEVELS):
                    if (n, lv) in ADA_SLOTS:
                        g = ADA_FIRST // 2 + ADA_SLOTS.index((n, lv))
                        for s in range(2):
                            ada_lo(2 * g + s)
                    if lv + 1 < LEVELS:
                        level_blocks(n, lv + 1)
            u = SEG["out"]["u"]
            pool.wait_ge(s_ada_pe, ADA_LAST)
            for s in range(2):
                split(u + s, u // 2, s)
            for s in range(NT):
                for c in range(2):
                    if s == 0:
                        pool.wait_ge(s_up[c], LEVELS * NT)
                        pool.wait_ge(s_y[c], LEVELS * NT)
                        pool.wait_ge(s_z[c], (LEVELS - 1) * NT)
                    else:
                        pool.wait_ge(s_ap[c], s)
                    tl = scan_tile(c, s)
                    for h in range(NH):
                        j = tl * 8 + c * NH + h
                        last = nc.gpsimd.tensor_scalar(kg[c][:, h], ktok[:, tl, h], ekg[:, j:j + 1], 1.0,
                                                       ALU.mult, ALU.mult)
                    last.then_inc(s_kg[c], 1)
            split_pairs(u, 4, first=1)
            for layer in range(2):
                if layer == 1:
                    split_pairs(SEG["pool"]["u"], 1)

                    def pool_normed(k):
                        pool.wait_ge(s_aff, PRIMED + 16 + max(k - 1, 0))
                        nc.gpsimd.tensor_tensor(pad[k % 2], x[:, k, :], rstd, ALU.mult).then_inc(s_a, 1)

                    def pool_lo(k):
                        if k < KD // 2:
                            return
                        pool.wait_ge(s_h, PRIMED + 16 + k)
                        pool.wait_ge(s_hi, 16 + k + 1)
                        nc.gpsimd.tensor_tensor(hlo[:, k, :], h32[k % 2], hhi[:, k, :].bitcast(F32),
                                                ALU.subtract).then_inc(s_h, 1)

                    pool.wait_ge(s_rstd, 3)
                    pool_normed(0)
                    pool_normed(1)
                    for k in range(KD):
                        if k + 2 < KD:
                            pool_normed(k + 2)
                        if k >= 2:
                            pool.wait_ge(s_h, PRIMED + 16 + k - 1)
                        pool.wait_ge(s_mean, k + 1)
                        for pc, c0, n, _ in POOL_RANGES:
                            last = nc.gpsimd.tensor_tensor(h32[k % 2][:, c0:c0 + n],
                                                           psum_w[:, 2 + k % 2, c0:c0 + n],
                                                           hp[:, k, pc:pc + n], ALU.subtract)
                        last.then_inc(s_mixed, 1)
                        if k:
                            pool_lo(k - 1)
                    pool_lo(KD - 1)
                for g, nf in enumerate(GROUPS):
                    split_pairs(SEG["up", layer, g]["u"], nf)
                    split_pairs(SEG["down", layer, g]["u"], 4, nf * P)
            pool.wait_ge(s_rstd, 5)
            pool.wait_ge(s_xg, KD)
            for k in range(2, KD, 3):
                nc.gpsimd.tensor_tensor(yout[:, k, :], yout[:, k, :], rstd, ALU.mult).then_inc(s_ychunk[1], 1)

        @block.tensor
        def _(pe):
            def products(pr, s, tiles, hi, lo, ks, wait_k=None):
                last = None
                for j, (tile, k) in enumerate(zip(tiles, ks)):
                    if wait_k is not None:
                        wait_k(j)
                    cs = slice(tile * P, tile * P + P)
                    for q, (wt, act) in enumerate(((whi, hi), (whi, lo), (wlo, hi))):
                        for b in range(2):
                            last = nc.tensor.matmul(pair[pr][:, b], wt[s][:, cs],
                                                    act[:, k, b * HALF:(b + 1) * HALF],
                                                    start=(j == 0 and q == 0),
                                                    stop=(j == len(tiles) - 1 and q == 2))
                return last

            def ada(n):
                b = batch_of(n)
                s = n % 2
                if n == batches[b][0] and b:
                    pe.wait_ge(s_mod, b)
                pe.wait_ge(s_ada_lo, n + 1)
                for k in range(4):
                    for q, w in enumerate(ada_split(n)):
                        last = nc.tensor.matmul(ada_row(n), c_parts[:, q, 4 * s + k, :],
                                                w[:, k * ADA_COLS:(k + 1) * ADA_COLS],
                                                start=(s == 0 and k == 0 and q == 0),
                                                stop=(s == 1 and k == 3 and q == 1))
                last.then_inc(s_ada_pe, 1)

            def ada_columns(g):
                b = batch_of(2 * g)
                pe.wait_ge(s_ada_cp, g + 1)
                for h in range(2):
                    at = ADA_COLS + 2 * (2 * g + h - batches[b][0])
                    last = nc.tensor.matmul(ps[:, col_bank[b], at:at + 2], ada_rows[:, h * P:(h + 1) * P],
                                            col("sel")[0:4], start=True, stop=True)
                last.then_inc(s_ada_t, 1)

            def ada_direct(n):
                b = batch_of(n)
                if n == batches[b][0]:
                    if col_bank[b]:
                        pe.wait_ge(s_rstd, 2 if b == NT + 1 else 4)
                    else:
                        pe.wait_ge(s_ev["A"], SEG["pool"]["A"])
                j = n - batches[NT + 2][0]
                if 0 <= j < ADA_POOL:
                    pe.wait_ge(s_ada_pool, 16)
                    src = ada_pool[:, j, :]
                else:
                    use = (ADA_LAST - ADA_FIRST) // 4 + ADA_USES[n % 2].index(n)
                    pe.wait_ge(s_ada[n % 2], 16 * (use + 1))
                    src = ada_raw[n % 2][:]
                for k in range(KD):
                    at = ADA_COLS + 2 * (n - batches[b][0])
                    last = nc.tensor.matmul(ps[:, col_bank[b], at:at + 2], src[:, k * P:(k + 1) * P],
                                            silu_c[:, k, :], start=(k == 0), stop=(k == KD - 1))
                last.then_inc(s_ada_pe, 1)

            def norm_sums(q):
                pe.wait_ge(s_acc, 9 * (q + 1))
                if q:
                    pe.wait_ge(s_mod, (None, NT + 1, NT + 2, NT + 2, NT + 4)[q])
                for b in range(2):
                    last = nc.tensor.matmul(pair["X"][:, b], ones, acc[:, b * HALF:(b + 1) * HALF],
                                            start=True, stop=True)
                last.then_inc(s_norm, 1)

            pe.wait_ge(s_const, 16)
            norm_sums(0)
            pe.wait_ge(s_c_parts, 1)
            for g in range(ADA_FIRST // 2):
                ada(2 * g)
                if g:
                    ada_columns(g - 1)
                ada(2 * g + 1)
            ada_columns(ADA_FIRST // 2 - 1)

            def in_unit(u, half_u, s, wait_k=None):
                pe.wait_ge(s_split, u + 1)
                pe.wait_ge(s_ev["AB"[s]], half_u + PRIMED)
                products("AB"[s], s, range(KD), hhi, hlo, range(KD), wait_k).then_inc(s_unit, 1)

            with pe.Fori(0, NQKV // 2) as i:
                for s in range(2):
                    in_unit(i * 2 + s, i, s, (lambda j: pe.wait_ge(s_h, PRIMED + j + 1)) if s == 0 else None)
            pe.wait_ge(s_mod, 1)
            for k in range(KD):
                for q, (a, b) in enumerate(((wba_hi, hhi), (wba_hi, hlo), (wba_lo, hhi))):
                    for h in range(2):
                        last = nc.tensor.matmul(pair["C"][0:16, h], a[:, k, :], b[:, k, h * HALF:(h + 1) * HALF],
                                                start=(k == 0 and q == 0), stop=(k == KD - 1 and q == 2))
            last.then_inc(s_bat, 1)
            with pe.Fori(NQKV // 2, (NQKV + NGATE) // 2) as i:
                for s in range(2):
                    in_unit(i * 2 + s, i, s)
            pe.wait_ge(s_gd, 1)
            for tl, c0 in enumerate(TILES):
                last = nc.tensor.transpose(ps[:, 7, 16 * tl:16 * tl + 16], acc[0:16, c0:c0 + P],
                                           ident[0:16, 0:16])
            last.then_inc(s_ba, 1)
            with pe.Fori(0, 2) as i:
                for j in range(6):
                    in_unit(i * 6 + (NQKV + NGATE + j), i * 3 + (NQKV + NGATE + j) // 2, j % 2)
                    if j in L2_AFTER:
                        m = L2_AFTER.index(j)
                        pe.wait_ge(s_l2sq, i * 4 + (m + 1))
                        if j == L2_AFTER[0]:
                            pe.wait_ge(s_ga, 1)
                            pe.wait_ge(s_gd, 2)
                        pe.wait_ge(s_l2ln, i * 4 + (PRIMED + m))
                        for b in range(2):
                            last = nc.tensor.matmul(pair["X"][:, b], ones, sq[m % 2][:, b * HALF:(b + 1) * HALF],
                                                    start=True, stop=True)
                        last.then_inc(s_l2sum, 1)
            pe.wait_ge(s_gd, 6)
            pe.wait_ge(s_l2ln, PRIMED + 8)
            gv = g_log.rearrange("p (t j) -> p t j", t=NT)
            gps = ps[:, 7, 128:168].rearrange("p (t j) -> p t j", t=NT)
            for d in range(2):
                nc.tensor.matmul(gps[:, :, 4 * d:4 * d + 4], (tri_u, tri_l)[d], gv[:, :, 4 * d:4 * d + 4],
                                 start=True, stop=True)
            nc.tensor.matmul(ps[:, 7, 192:232], ones, g_log, start=True, stop=True).then_inc(s_gsum, 1)

            pe.wait_ge(s_l2, 8)

            def tokens(n, j):
                if n + j:
                    pe.wait_ge(s_tok, 2 * n + j)
                for h in range(NH):
                    last = nc.tensor.transpose(bank[6][:, h], qkv[:, 4 + 4 * j + h, TILES[n]:TILES[n] + P], ident)
                last.then_inc(s_tr, 1)

            def prepare(n, p):
                c0 = TILES[n]
                if p == 0:
                    if n:
                        pe.wait_ge(s_am, 2 * n)
                    tokens(n, 0)
                elif p == 1:
                    tokens(n, 1)
                elif p in (2, 3):
                    c = p - 2
                    pe.wait_ge(s_tg[c], n + 1)
                    if c == 0:
                        pe.wait_ge(s_tok, 2 * n + 2)
                    else:
                        pe.wait_ge(s_dd[0], n + 1)
                    nc.tensor.matmul(bank[6], ones, dec[c], start=True, stop=True).then_inc(s_bc[c], 1)
                else:
                    if p == 4:
                        pe.wait_ge(s_dd[1], n + 1)
                    else:
                        for c in range(2):
                            pe.wait_ge(s_mt[c], n + 1)
                    for h in range(NH):
                        last = nc.tensor.matmul(bank[6][:, h], qkv[:, 4 + h, c0:c0 + P],
                                                qkv[:, (4 if p == 4 else 0) + h, c0:c0 + P], start=True, stop=True)
                    last.then_inc(s_gram, 1)

            pe.wait_ge(s_ga, 9)
            for p in "AB":
                pe.wait_ge(s_ev[p], PRIMED + 14)
            for p in range(6):
                prepare(0, p)
            for n in range(NT):
                for lv in range(LEVELS):
                    for c in range(2):
                        pe.wait_ge(s_bt[c], LEVELS * n + lv + 1)
                        if lv == 0:
                            if n:
                                pe.wait_ge(s_yc[c], (LEVELS - 1) * n)
                        else:
                            pe.wait_ge(s_up[c], LEVELS * n + lv)
                            if lv > 1:
                                pe.wait_ge(s_yc[c], (LEVELS - 1) * n + lv - 1)
                        for h in range(NH):
                            last = nc.tensor.matmul(bank[2 + c][:, h], bt[c][(LEVELS * n + lv) % 2][:, h],
                                                    ident if lv == 0 else tt[c][:, h], start=True, stop=True)
                        last.then_inc(s_y[c], 1)
                    g = ADA_FIRST // 2 + ADA_SLOTS.index((n, lv)) if (n, lv) in ADA_SLOTS else None
                    if g is not None:
                        if g - 1 not in batch_end:
                            ada_columns(g - 1)
                        ada(2 * g)
                    if lv == 0:
                        if g is not None:
                            ada(2 * g + 1)
                        continue
                    for c in range(2):
                        zb, ztb = ((4, 5), (0, 1))[c]
                        pe.wait_ge(s_yc[c], (LEVELS - 1) * n + lv)
                        for h in range(NH):
                            if lv < LEVELS - 1:
                                nc.tensor.matmul(bank[zb][:, h], rinv[:, 2 * n + c, h], ys[c][:, h],
                                                 start=True, stop=True)
                            last = nc.tensor.matmul(bank[ztb][:, h], ys[c][:, h], rinv[:, 2 * n + c, h],
                                                    start=True, stop=True)
                        last.then_inc(s_z[c], 1)
                    ada(2 * g + 1)
                    if n + 1 < NT:
                        prepare(n + 1, lv - 1)
                ada_columns(g)

            for s in range(NT):
                for c in range(2):
                    tl = scan_tile(c, s)
                    c0 = TILES[tl]
                    b0 = 4 * c
                    S = ss[c] if s < NT - 1 else sp_[c]
                    if s == 0:
                        pe.wait_ge(s_state, 32)
                        for cc in range(2):
                            pe.wait_ge(s_up[cc], LEVELS * NT)
                        pe.wait_ge(s_tok, 2 * NT)
                        pe.wait_ge(s_mod, NT + 1)
                    elif s == NT - 1:
                        pe.wait_ge(s_zero, 2)
                        pe.wait_ge(s_vn[c], s)
                    else:
                        pe.wait_ge(s_st[c], s)
                    if s:
                        pe.wait_ge(s_t[c], s)
                    for h in range(NH):
                        nc.tensor.matmul(bank[b0][:, h], qkv[:, 4 + h, c0:c0 + P], S[:, h],
                                         start=True, stop=True)
                    for h in range(NH):
                        last = nc.tensor.matmul(bank[b0 + 1][:, h], qkv[:, h, c0:c0 + P], S[:, h],
                                                start=True, stop=True)
                    last.then_inc(s_kq[c], 1)
                for c in range(2):
                    tl = scan_tile(c, s)
                    pe.wait_ge(s_r[c], s + 1)
                    for h in range(NH):
                        last = nc.tensor.matmul(bank[4 * c][:, h], rinv[:, 2 * tl + c, h], rr[c][:, h],
                                                start=True, stop=True)
                    last.then_inc(s_tr3[c], 1)
                for c in range(2):
                    tl = scan_tile(c, s)
                    pe.wait_ge(s_vn[c], s + 1)
                    pe.wait_ge(s_kg[c], s + 1)
                    pe.wait_ge(s_at[c], NT)
                    if s:
                        pe.wait_ge(s_to[c], s)
                    for h in range(NH):
                        nc.tensor.matmul(bank[4 * c + 2][:, h], kg[c][:, h], vn[c][:, h], start=True, stop=True)
                    for h in range(NH):
                        last = nc.tensor.matmul(bank[4 * c + 3][:, h], attn[:, 2 * tl + c, h], vn[c][:, h],
                                                start=True, stop=True)
                    last.then_inc(s_ap[c], 1)
            for n in range(NT):
                pe.wait_ge(s_on, n + 1)
                if n >= 4:
                    pe.wait_ge(s_oy, n - 3)
                for h in range(NH):
                    last = nc.tensor.transpose(bank[O_BANKS[n % 4]][:, h], osum[:, done_order[n], h], ident)
                last.then_inc(s_oT, 1)

            def accumulate(seg, nf, hi, lo, ready, ks=None):
                b = SEG[seg]
                ks = ks or range(nf)
                with pe.Fori(0, 4) as i:
                    for s in range(2):
                        n = "CB"[s]
                        pe.wait_ge(s_split, i * 2 + (b["u"] + s + 1))
                        pe.wait_ge(s_ev[n], i + b[n])
                        products(n, s, ks, hi, lo, ks, ready if s == 0 else None)\
                            .then_inc(s_unit, 1)

            def y_ready(j):
                if j in (0, NB):
                    pe.wait_ge(s_yready, NB + (NT if j else 0))

            accumulate("out", KD, hhi, hlo, y_ready, ks=[*range(NH, KD), *range(NH)])
            norm_sums(1)
            for n in range(ADA_LAST, ADA_LAST + ADA_DIRECT[0]):
                ada_direct(n)

            for layer in range(2):
                if layer == 1:
                    b = SEG["pool"]
                    for m in range(KD):
                        n = "CB"[m % 2]
                        if m % 2 == 0:
                            for n_ada in ADA_BEFORE[m // 2]:
                                ada_direct(n_ada)
                        if m % 4 == 0:
                            pe.wait_ge(s_split, b["u"] + m // 4 + 1)
                        pe.wait_ge(s_ev[n], b[n] + m // 2)
                        pe.wait_ge(s_h, PRIMED + 16 + 2 * (m // 2) + 2)
                        last = products(n, m // 4, (2 * (m % 4), 2 * (m % 4) + 1), hhi, hlo,
                                        (2 * (m // 2), 2 * (m // 2) + 1))
                        last.then_inc(s_unit if m % 4 == 3 else s_pm, 1)
                    norm_sums(3)
                    for n_ada in range(96 - ADA_DIRECT[2], 96):
                        ada_direct(n_ada)
                for g, nf in enumerate(GROUPS):
                    b = SEG["up", layer, g]
                    hr = 8 if layer == 0 else 24
                    with pe.Fori(0, nf) as i:
                        for s in range(2):
                            pe.wait_ge(s_split, i * 2 + (b["u"] + s + 1))
                            pe.wait_ge(s_ev["AB"[s]], i + b["AB"[s]])
                            wait_k = (lambda j: pe.wait_ge(s_h, PRIMED + hr + j + 1)) if s == 0 and g == 0 else None
                            products("AB"[s], s, range(KD), hhi, hlo, range(KD), wait_k).then_inc(s_unit, 1)
                    f = b["f"]
                    accumulate(("down", layer, g), nf, hidhi, hidlo, lambda j: pe.wait_ge(s_hid, f + j + 1))
                norm_sums(2 if layer == 0 else 4)

        @block.scalar
        def _(act):
            own = Steps(act, s_act)

            def rsqrt_of_sums(q):
                own.sync()
                own.tick(nc.scalar.activation(warm[:], eps_col, ACT.Ln))
                act.wait_ge(s_norm, q + 1)
                if q:
                    act.wait_ge(s_a, 8 * q)
                own.tick(nc.scalar.activation(halves(rstd), pair["X"], ACT.Ln, bias=eps_col, scale=1.0 / D))
                own.sync()
                nc.scalar.activation(rstd, rstd, ACT.Exp, scale=-0.5).then_inc(s_rstd, 1)

            def modulate(q, layer, part):
                if q:
                    rsqrt_of_sums(q)
                aff = 8 * q + PRIMED
                hi0 = (0, 8, None, 24)[q] + PRIMED
                with act.Fori(0, 2) as i:
                    for p in (0, 2):
                        for s in range(p, p + 2):
                            act.wait_ge(s_a, i * 4 + (8 * q + s + 1))
                            act.wait_ge(s_h, i * 4 + (hi0 + s - 3))
                            for c0, n, cd in RANGES:
                                last = nc.scalar.activation(hb[s][:, c0:c0 + n], pad[s % 2][:, c0:c0 + n],
                                                            ACT.Identity,
                                                            bias=mod[:, layer, 3 * part, ds(i * 4 + s, 1), cd],
                                                            scale=mod[:, layer, 3 * part + 1, ds(i * 4 + s, 1), cd])
                            last.then_inc(s_aff, 1)
                        for s in range(p, p + 2):
                            act.wait_ge(s_aff, i * 4 + (aff + s + 1))
                            nc.scalar.activation(hhi[:, i * 4 + s, :], hb[s], ACT.Copy).then_inc(s_hi, 1)

            def squares(q, name_of, base):
                with act.Fori(0, 4) as i:
                    for s in range(2):
                        act.wait_ge(name_of[s], i * base[s][1] + (base[s][0] + 1))
                        act.wait_ge(s_acc, i * 2 + (9 * q + 1))
                        nc.scalar.activation(sq[s], x[:, i * 2 + s, :], ACT.Square).then_inc(s_sq, 1)
                        if q == 4:
                            nc.scalar.activation(yout[:, i * 2 + s, :], x[:, i * 2 + s, :], ACT.Copy,
                                                 scale=g_final[:, ds(i * 2 + s, 1)]).then_inc(s_xg, 1)

            def squares_after(q, seg):
                b = SEG[seg]
                squares(q, (s_ev["C"], s_ev["B"]), ((b["C"], 1), (b["B"], 1)))

            def ada_hi(n):
                if n < ADA_FIRST:
                    if n % 4 == 0:
                        act.wait_ge(s_ada1[n // 4], 16)
                else:
                    act.wait_ge(s_ada[n % 4], 16 * ((n - ADA_FIRST) // 4 + 1))
                back = 4 if n < ADA_FIRST else 2
                if n >= back:
                    act.wait_ge(s_ada_pe, n - back + 1)
                nc.scalar.activation(ada_split(n)[0][:], ada_source(n), ACT.Copy).then_inc(s_ada_hi, 1)

            def ada_copy(g):
                act.wait_ge(s_ada_pe, 2 * g + 2)
                if g:
                    act.wait_ge(s_ada_t, g)
                nc.scalar.activation(ada_rows[:], ada_row(2 * g), ACT.Copy)\
                    .then_inc(s_ada_cp, 1)

            act.wait_ge(s_cols, 16)
            nc.scalar.activation(silu_c[:], cond, ACT.Silu).then_inc(s_silu_c, 1)
            squares(0, (s_x0, s_x0), ((0, 2), (1, 2)))
            for n in range(4):
                ada_hi(n)
                if n == 1:
                    rsqrt_of_sums(0)
            for g in range(ADA_FIRST // 2):
                ada_copy(g)
                for n in (2 * g + 4, 2 * g + 5):
                    if n < ADA_FIRST:
                        ada_hi(n)
            act.wait_ge(s_fold, 1)
            modulate(0, 0, 0)

            with act.Fori(0, NQKV // 2) as i:
                for s in range(2):
                    act.wait_ge(s_unit, i * 2 + (s + 1))
                    act.wait_ge(s_conv, i * 2 + PRIMED)
                    nc.scalar.activation(halves(pad[s]), pair["AB"[s]], ACT.Copy).then_inc(s_ev["AB"[s]], 1)
                    act.wait_ge(s_conv, i * 2 + (PRIMED + s + 1))
                    nc.scalar.activation(qkv[:, i * 2 + s, :], cv[s], ACT.Silu).then_inc(s_silu, 1)
            with act.Fori(0, NGATE // 2) as i:
                for s in range(2):
                    act.wait_ge(s_unit, i * 2 + (NQKV + s + 1))
                    nc.scalar.activation(halves(sgate[:, i * 2 + s, :]), pair["AB"[s]], ACT.Silu)\
                        .then_inc(s_ev["AB"[s]], 1)
            act.wait_ge(s_ba, 1)
            act.wait_ge(s_fill, 3)
            bav = ps[:, 7, 0:16 * NT].rearrange("p (t j) -> p t j", t=NT)

            def tiles(v):
                return v.rearrange("p (t j) -> p t j", t=NT)
            nc.scalar.activation(tiles(tmp_a), bav[:, :, 0:8], ACT.Exp, scale=-1.0).then_inc(s_ga, 1)
            nc.scalar.activation(e_alog, col("a_log"), ACT.Exp).then_inc(s_ga, 1)
            act.wait_ge(s_gd, 2)
            nc.scalar.activation(tmp_c, tmp_b, ACT.Abs).then_inc(s_ga, 1)
            act.wait_ge(s_ga, 3)
            nc.scalar.activation(tmp_c, tmp_c, ACT.Exp, scale=-1.0).then_inc(s_ga, 1)
            act.wait_ge(s_ga, 4)
            nc.scalar.activation(tmp_c, tmp_c, ACT.Ln, bias=1.0).then_inc(s_ga, 1)
            act.wait_ge(s_silu, PRIMED + NQKV)
            act.wait_ge(s_acc, 9)
            with act.Fori(0, 2) as i:
                def c_gate(s):
                    act.wait_ge(s_unit, i * 6 + (NQKV + NGATE + 3 * s + 1))
                    act.wait_ge(s_ev["BA"[s]], i * 3 + (PRIMED + 6 + 2 * s))
                    nc.scalar.activation(halves(h32[s]), pair["AB"[s]], ACT.Copy).then_inc(s_ev["AB"[s]], 1)

                def square(m):
                    act.wait_ge(s_l2ln, i * 4 + (PRIMED + max(m - 1, 0)))
                    nc.scalar.activation(sq[m % 2], qkv[:, ds(i * 4 + m, 1), :], ACT.Square).then_inc(s_l2sq, 1)

                def log(m):
                    act.wait_ge(s_l2sum, i * 4 + (m + 1))
                    nc.scalar.activation(halves(lnn[:, i * 4 + m, :]), pair["X"], ACT.Ln, bias=eps_col)\
                        .then_inc(s_l2ln, 1)

                c_gate(0)
                square(0)
                square(1)
                log(0)
                square(2)
                log(1)
                c_gate(1)
                square(3)
                log(2)
                log(3)
            for u in range(8):
                act.wait_ge(s_l2ln, PRIMED + u + 1)
                nc.scalar.activation(lnn[:, u, :], lnn[:, u, :], ACT.Exp, scale=-0.5,
                                     bias=scale_col if u < 4 else 0.0).then_inc(s_l2r, 1)
            act.wait_ge(s_gsum, 1)
            nc.scalar.activation(gcs, ps[:, 7, 128:168], ACT.Copy).then_inc(s_ga, 1)
            nc.scalar.activation(egc, ps[:, 7, 128:168], ACT.Exp).then_inc(s_ga, 1)
            nc.scalar.activation(etot, ps[:, 7, 192:232], ACT.Exp).then_inc(s_ga, 1)
            nc.scalar.activation(tmp_c, ps[:, 7, 192:232], ACT.Copy).then_inc(s_ga, 1)
            act.wait_ge(s_gd, 7)
            nc.scalar.activation(ekg, tmp_a, ACT.Exp).then_inc(s_ga, 1)

            act.wait_ge(s_unit, 28)
            ada_hi(ADA_FIRST)

            def prepare(n, p):
                if p < 2:
                    act.wait_ge(s_tr, 2 * n + p + 1)
                    nc.scalar.activation((ktok, vtok)[p][:, n], bank[6], ACT.Copy).then_inc(s_tok, 1)
                elif p < 4:
                    act.wait_ge(s_dd[p - 2], n + 1)
                    nc.scalar.activation(dec[p - 2], dec[p - 2], ACT.Exp).then_inc(s_dx[p - 2], 1)

            act.wait_ge(s_l2, 8)
            for p in range(4):
                prepare(0, p)
            for n in range(NT):
                for lv in range(LEVELS):
                    g = ADA_FIRST // 2 + ADA_SLOTS.index((n, lv)) if (n, lv) in ADA_SLOTS else None
                    if g is not None:
                        if g - 1 not in batch_end:
                            ada_copy(g - 1)
                        ada_hi(2 * g + 1)
                    for c in range(2 if lv else 0):
                        act.wait_ge(s_y[c], LEVELS * n + lv + 1)
                        if (LEVELS - 1) * n + lv > 1:
                            act.wait_ge(s_z[c], (LEVELS - 1) * n + lv - 1)
                        nc.scalar.activation(ys[c], bank[2 + c], ACT.Copy).then_inc(s_yc[c], 1)
                    if g is not None and 2 * g + 2 < ADA_LAST:
                        ada_hi(2 * g + 2)
                    if lv and n + 1 < NT:
                        prepare(n + 1, lv - 1)
                ada_copy(g)
            def o_squares(n):
                c, s = done_visits[n]
                act.wait_ge(s_to[c], s + 1)
                own.sync()
                for h in range(NH):
                    own.tick(nc.scalar.activation(junk[:, h], osum[:, done_order[n], h], ACT.Square,
                                                  accum_out=ssq[:, 0, n * NH + h:n * NH + h + 1]))

            for s in range(NT):
                for c in range(2):
                    act.wait_ge(s_kq[c], s + 1)
                    if s:
                        act.wait_ge(s_to[c], s)
                    tl = scan_tile(c, s)
                    for h in range(NH):
                        j = tl * 8 + c * NH + h
                        last = nc.scalar.activation(to[c][:, h], bank[4 * c + 1][:, h], ACT.Copy,
                                                    scale=egc[:, j:j + 1])
                    last.then_inc(s_t[c], 1)
                for c in range(2):
                    tl = scan_tile(c, s)
                    act.wait_ge(s_tr3[c], s + 1)
                    for h in range(NH):
                        j = tl * 8 + c * NH + h
                        last = nc.scalar.activation(vn[c][:, h], bank[4 * c][:, h], ACT.Copy, scale=beta[:, j:j + 1])
                    last.then_inc(s_vn[c], 1)
                for n, (_, s_done) in enumerate(done_visits):
                    if s_done == s - 1:
                        o_squares(n)
            own.sync()
            own.tick(nc.scalar.activation(warm[:], eps_col, ACT.Ln))
            o_squares(NT - 1)
            own.sync()
            own.tick(nc.scalar.activation(ssq[:, 1], ssq[:, 0], ACT.Ln, bias=eps_col, scale=1.0 / DK))
            own.sync()
            nc.scalar.activation(ssq[:, 1], ssq[:, 1], ACT.Exp, scale=-0.5).then_inc(s_orr, 1)
            for j in range(NB):
                nc.scalar.activation(hhi[:, 4 + j, :], yb[:, j, :], ACT.Copy).then_inc(s_yhi, 1)
            for n in range(NT):
                act.wait_ge(s_oy, n + 1)
                c0 = TILES[done_order[n]]
                nc.scalar.activation(hhi[:, 0:NH, c0:c0 + P], chain[n % 3][0], ACT.Copy).then_inc(s_yhi, 1)

            squares_after(1, "out")
            modulate(1, 0, 1)
            for layer in range(2):
                if layer == 1:
                    rsqrt_of_sums(2)

                    def pool_modulate(k):
                        act.wait_ge(s_a, 16 + k + 1)
                        for (pc, c0, n, cd) in POOL_RANGES:
                            last = nc.scalar.activation(hp[:, k, pc:pc + n], pad[k % 2][:, c0:c0 + n], ACT.Identity,
                                                        bias=mod[:, 1, 0, k, cd:cd + 1],
                                                        scale=mod[:, 1, 1, k, cd:cd + 1])
                        last.then_inc(s_aff, 1)

                    def pool_squares(g):
                        for s in range(2):
                            act.wait_ge(s_ev["CB"[s]], SEG["pool"]["CB"[s]] + g + 1)
                            act.wait_ge(s_acc, 9 * 3 + 2 * g + 1)
                            nc.scalar.activation(sq[s], x[:, 2 * g + s, :], ACT.Square).then_inc(s_sq, 1)

                    pool_modulate(0)
                    for k in range(KD):
                        if k + 1 < KD:
                            pool_modulate(k + 1)
                        act.wait_ge(s_mixed, k + 1)
                        nc.scalar.activation(hhi[:, k, :], h32[k % 2], ACT.Copy).then_inc(s_hi, 1)
                        if k % 2 and k > 1:
                            pool_squares(k // 2 - 1)
                    pool_squares(KD // 2 - 1)
                    modulate(3, 1, 1)
                for g, nf in enumerate(GROUPS):
                    b = SEG["up", layer, g]
                    u, f = b["u"], b["f"]
                    with act.Fori(0, nf) as i:
                        act.wait_ge(s_unit, i * 2 + (u + 1))
                        act.wait_ge(s_conv, i + (PRIMED + NQKV + NB + f))
                        nc.scalar.activation(halves(pad[0]), pair["A"], ACT.Copy).then_inc(s_ev["A"], 1)
                        act.wait_ge(s_conv, i + (PRIMED + NQKV + NB + f + 1))
                        act.wait_ge(s_ev["B"], i + b["B"])
                        nc.scalar.activation(cv[1], cv[0], ACT.Silu).then_inc(s_silu, 1)
                        act.wait_ge(s_ev["B"], i + (b["B"] + 1))
                        nc.scalar.activation(hidhi[:, i, :], h32[0], ACT.Copy).then_inc(s_hid_hi, 1)
                squares_after(2 if layer == 0 else 4, ("down", layer, 2))
            rsqrt_of_sums(4)

        @block.vector
        def _(dve):
            own = Steps(dve, s_dve)

            def add_squares(i, q, s):
                dve.wait_ge(s_sq, i * 2 + (8 * q + s + 1))
                dve.wait_ge(s_acc, i * 2 + (9 * q + s + 1))
                nc.vector.tensor_tensor(acc, acc, sq[s], ALU.add).then_inc(s_acc, 1)

            def clear_acc(q):
                if q:
                    dve.wait_ge(s_norm, q)
                nc.vector.memset(acc, 0.0).then_inc(s_acc, 1)

            def update_x(seg, layer, part, q=None):
                b = SEG[seg]
                if q is not None:
                    clear_acc(q)
                with dve.Fori(0, 4) as i:
                    for s in range(2):
                        n = "CB"[s]
                        k = i * 2 + s
                        dve.wait_ge(s_unit, i * 2 + (b["u"] + s + 1))
                        for bk, pc, ln, xc, cd in PIECES:
                            last = nc.vector.scalar_tensor_tensor(
                                out=x[:, k, xc:xc + ln], in0=pair[n][:, bk, pc:pc + ln],
                                scalar=mod[:, layer, 3 * part + 2, ds(k, 1), cd],
                                in1=x[:, k, xc:xc + ln], op0=ALU.mult, op1=ALU.add)
                        last.then_inc(s_ev[n], 1)
                    if q is not None:
                        for s in range(2):
                            add_squares(i, q, s)

            def add_batch(b):
                first, n = batches[b]
                if b <= NT:
                    dve.wait_ge(s_ada_t, batch_end[b] + 1)
                else:
                    dve.wait_ge(s_ada_pe, first + n)
                nc.vector.tensor_tensor(mod_n[:, first:first + n, :],
                                        ps[:, col_bank[b], ADA_COLS:ADA_COLS + 2 * n]
                                        .rearrange("p (n c) -> p n c", c=2),
                                        b_ada[:, first:first + n, :], ALU.add).then_inc(s_mod, 1)

            def fold_scale(layer, part, g):
                v = mod[:, layer, 3 * part + 1]
                return nc.vector.scalar_tensor_tensor(out=v, in0=v, scalar=1.0, in1=g[:, layer],
                                                      op0=ALU.add, op1=ALU.mult)

            def apply_norm(q, lo0):
                dve.wait_ge(s_rstd, q + 1)
                def normed(k, s, waited):
                    dve.wait_ge(s_aff, waited)
                    nc.vector.tensor_tensor(pad[s], x[:, k, :], rstd, ALU.mult).then_inc(s_a, 1)

                def lo(k, s, waited):
                    dve.wait_ge(s_hi, waited)
                    nc.vector.tensor_tensor(hlo[:, k, :], hb[s], hhi[:, k, :].bitcast(F32),
                                            ALU.subtract).then_inc(s_h, 1)

                for s in range(2):
                    normed(s, s, 8 * q + PRIMED)
                for k in range(KD):
                    if k + 2 < KD:
                        normed(k + 2, k % 2, 8 * q + PRIMED + k + 1)
                    lo(k, k % 4, lo0 + k + 1)

            def conv(src, dst, taps, per=2):
                own.tick(nc.vector.tensor_scalar(dst[:, 1:W - 1], src[:, 1:W - 1], taps[1], None, ALU.mult))
                own.sync()
                own.tick(nc.vector.scalar_tensor_tensor(out=dst[:, 1:W - 1], in0=src[:, 0:W - 2], scalar=taps[0],
                                                        in1=dst[:, 1:W - 1], op0=ALU.mult, op1=ALU.add))
                own.sync()
                nc.vector.scalar_tensor_tensor(out=dst[:, 1:W - 1], in0=src[:, 2:W], scalar=taps[2],
                                               in1=dst[:, 1:W - 1], op0=ALU.mult, op1=ALU.add)\
                    .then_inc(s_conv, 1)

            def zero_pads(bufs):
                for v in bufs:
                    for a, b in ((0, S0), (S0 + SEQ_S, P0), (P0 + SEQ_P, W)):
                        last = nc.vector.memset(v[:, a:b], 0.0)
                return last

            nc.vector.memset(eps_col, EPS).then_inc(s_fill, 1)
            nc.vector.memset(scale_col, -0.5 * float(np.log(DK))).then_inc(s_fill, 1)
            zero_pads(h32 + cv).then_inc(s_fill, 1)
            clear_acc(0)
            dve.wait_ge(s_silu_c, 1)
            for q in range(2):
                own.tick(nc.vector.tensor_copy(c_parts[:, q, :, 0:2], silu_c[:]))
            nc.vector.memset(c_parts[:, 1, :, 2:4].bitcast(F32), 0.0)
            own.sync()
            nc.vector.tensor_tensor(c_parts[:, 0, :, 2:4], silu_c[:], c_parts[:, 0, :, 0:2].bitcast(F32),
                                    ALU.subtract).then_inc(s_c_parts, 1)
            dve.wait_ge(s_x, 16)
            dve.wait_ge(s_pe, 16)
            def add_position(k):
                v = x[:, k, S0:S0 + SEQ_S].rearrange("p (r g) -> p r g", r=ROWS)
                if k < KD // 2:
                    tab = pe_tab[:, k, 0:ROWS].unsqueeze(2).to_broadcast([P, ROWS, GRID_W])
                else:
                    tab = pe_tab[:, k - KD // 2, ROWS:].unsqueeze(1).to_broadcast([P, ROWS, GRID_W])
                nc.vector.tensor_tensor(v, v, tab, ALU.add).then_inc(s_x0, 1)

            for k in range(2):
                add_position(k)
            for i in range(KD // 2):
                if i + 1 < KD // 2:
                    for s in range(2):
                        add_position(i * 2 + 2 + s)
                for s in range(2):
                    add_squares(i, 0, s)
            dve.wait_ge(s_cols, 16)
            own.tick(nc.vector.tensor_copy(wba_hi[:], w_ba))
            own.sync()
            own.tick(nc.vector.tensor_tensor(wba_lo[:], w_ba, wba_hi[:].bitcast(F32), ALU.subtract))
            for n in range(ADA_FIRST):
                dve.wait_ge(s_ada_hi, n + 1)
                hi, lo = ada_split(n)
                nc.vector.tensor_tensor(lo[:], ada_source(n), hi[:].bitcast(F32),
                                        ALU.subtract).then_inc(s_ada_lo, 1)
            add_batch(0)
            dve.wait_ge(s_mod, 1)
            fold_scale(0, 0, g_mix).then_inc(s_fold, 1)
            apply_norm(0, 0)

            with dve.Fori(0, NQKV // 2) as i:
                own.enter(i, 4)
                for s in range(2):
                    dve.wait_ge(s_ev["AB"[s]], i + (PRIMED + 1))
                    dve.wait_ge(s_silu, i * 2 + PRIMED)
                    conv(pad[s], cv[s], [tap_qkv[:, j, ds(i * 2 + s, 1)] for j in range(3)])
            own.leave(NQKV // 2)
            dve.wait_ge(s_bat, 1)
            nc.vector.tensor_copy(halves(acc)[0:16], pair["C"][0:16]).then_inc(s_gd, 1)
            dve.wait_ge(s_ba, 1)
            dve.wait_ge(s_ga, 1)
            bav = ps[:, 7, 0:16 * NT].rearrange("p (t j) -> p t j", t=NT)

            def tiles(v):
                return v.rearrange("p (t j) -> p t j", t=NT)
            nc.vector.tensor_tensor(tiles(tmp_b), bav[:, :, 8:16], tiles(col("dt_bias")), ALU.add).then_inc(s_gd, 1)
            nc.vector.tensor_scalar(tmp_a, tmp_a, 1.0, None, ALU.add).then_inc(s_gd, 1)
            dve.wait_ge(s_gd, 3)
            nc.vector.reciprocal(beta, tmp_a).then_inc(s_gd, 1)
            dve.wait_ge(s_ga, 5)
            nc.vector.scalar_tensor_tensor(out=tmp_d, in0=tmp_b, scalar=0.0, in1=tmp_c,
                                           op0=ALU.max, op1=ALU.add).then_inc(s_gd, 1)
            dve.wait_ge(s_gd, 5)
            nc.vector.scalar_tensor_tensor(out=g_log, in0=tmp_d, scalar=-1.0, in1=e_alog,
                                           op0=ALU.mult, op1=ALU.mult).then_inc(s_gd, 1)
            dve.wait_ge(s_silu, PRIMED + NQKV)
            with dve.Fori(0, 2) as i:
                own.enter(i, 4)
                for s in range(2):
                    u0 = NQKV + NGATE + 3 * s
                    pc, ph = "AB"[s], "BA"[s]
                    dve.wait_ge(s_ev[pc], i * 3 + (PRIMED + u0 // 2 + 1))
                    dve.wait_ge(s_unit, i * 6 + (u0 + 2))
                    nc.vector.tensor_tensor(halves(pad[s]), halves(h32[s]), pair[ph], ALU.mult)\
                        .then_inc(s_ev[ph], 1)
                    dve.wait_ge(s_ev[ph], i * 3 + (PRIMED + (u0 + 1) // 2 + 1))
                    conv(pad[s], cv[s], [tap_b[:, j, ds(i * 2 + s, 1)] for j in range(3)])
                    dve.wait_ge(s_conv, i * 2 + (PRIMED + NQKV + s + 1))
                    dve.wait_ge(s_unit, i * 6 + (u0 + 3))
                    nc.vector.tensor_tensor(halves(yb[:, i * 2 + s, :]), halves(cv[s]), pair[pc], ALU.mult)\
                        .then_inc(s_ev[pc], 1)
            own.leave(2)

            for u in range(8):
                dve.wait_ge(s_l2r, u + 1)
                nc.vector.tensor_tensor(qkv[:, u, :], qkv[:, u, :], lnn[:, u, :], ALU.mult).then_inc(s_l2, 1)
            dve.wait_ge(s_ga, 9)
            nc.vector.tensor_tensor(tmp_a, tmp_c, gcs, ALU.subtract).then_inc(s_gd, 1)
            nc.vector.tensor_scalar(negegc, egc, -1.0, None, ALU.mult).then_inc(s_gd, 1)
            dve.wait_ge(s_gd, 8)

            id4 = ident.unsqueeze(1).to_broadcast([P, NH, P])

            def tri_g(n, c):
                for h in range(NH):
                    j = n * 8 + c * NH + h
                    last = nc.vector.tensor_scalar(dec[c][:, h], (tri_u, tri_l)[c], g_log[:, j:j + 1], None, ALU.mult)
                last.then_inc(s_tg[c], 1)

            def prepare(n, p):
                if p == 1:
                    for c in range(2):
                        tri_g(n, c)
                elif p in (2, 3):
                    c = p - 2
                    dve.wait_ge(s_bc[c], n + 1)
                    for h in range(NH):
                        j = n * 8 + c * NH + h
                        last = nc.vector.tensor_scalar(dec[c][:, h], bank[6][:, h], gcs[:, j:j + 1], 0.0,
                                                       ALU.subtract, ALU.min)
                    last.then_inc(s_dd[c], 1)
                elif p == 4:
                    dve.wait_ge(s_gram, 2 * n + 1)
                    for c in range(2):
                        dve.wait_ge(s_dx[c], n + 1)
                        if n:
                            dve.wait_ge(s_bt[c], LEVELS * n)
                        for h in range(NH):
                            j = n * 8 + c * NH + h
                            last = nc.vector.scalar_tensor_tensor(
                                out=mt[c][:, h], in0=dec[c][:, h], scalar=beta[:, j:j + 1],
                                in1=bank[6][:, h], op0=ALU.mult, op1=ALU.mult)
                        last.then_inc(s_mt[c], 1)
                elif p == 5:
                    dve.wait_ge(s_gram, 2 * n + 2)
                    for c in range(2):
                        nc.vector.tensor_tensor(attn[:, 2 * n + c], dec[c], bank[6], ALU.mult).then_inc(s_am, 1)
                    for c in range(2):
                        dve.wait_ge(s_am, 2 * n + 1 + c)
                        a = attn[:, 2 * n + c]
                        nc.vector.tensor_tensor(a, a, tri_mask(c), ALU.mult).then_inc(s_at[c], 1)

            for p in range(6):
                prepare(0, p)
            for n in range(NT):
                for c in range(2):
                    dve.wait_ge(s_y[c], LEVELS * n + 1)
                    nc.vector.tensor_tensor(tt[c], id4, bank[2 + c], ALU.subtract)
                    nc.vector.tensor_tensor(rinv[:, 2 * n + c], id4, bt[c][(LEVELS * n) % 2], ALU.subtract)\
                        .then_inc(s_up[c], 1)
                for lv in range(1, LEVELS):
                    for c in range(2):
                        zb, ztb = ((4, 5), (0, 1))[c]
                        dve.wait_ge(s_z[c], (LEVELS - 1) * n + lv)
                        if lv < LEVELS - 1:
                            nc.vector.tensor_tensor(tt[c], tt[c], bank[zb], ALU.subtract)
                        r = rinv[:, 2 * n + c]
                        nc.vector.tensor_tensor(r, r, bank[ztb], ALU.subtract).then_inc(s_up[c], 1)
                    if n + 1 < NT:
                        prepare(n + 1, lv - 1)
                add_batch(n + 1)
            dve.wait_ge(s_mod, NT + 1)
            fold_scale(0, 1, g_ffn).then_inc(s_fold, 1)

            dve.wait_ge(s_ada_lo, ADA_LAST)
            for c in range(2):
                nc.vector.memset(sp_[c], 0.0).then_inc(s_zero, 1)
            for s in range(NT):
                for c in range(2):
                    tl = scan_tile(c, s)
                    dve.wait_ge(s_kq[c], s + 1)
                    for h in range(NH):
                        j = tl * 8 + c * NH + h
                        last = nc.vector.scalar_tensor_tensor(
                            out=rr[c][:, h], in0=bank[4 * c][:, h], scalar=negegc[:, j:j + 1],
                            in1=vtok[:, tl, h], op0=ALU.mult, op1=ALU.add)
                    last.then_inc(s_r[c], 1)
                for c in range(2):
                    tl = scan_tile(c, s)
                    S = ss[c] if s < NT - 1 else sp_[c]
                    dve.wait_ge(s_ap[c], s + 1)
                    for h in range(NH):
                        j = tl * 8 + c * NH + h
                        last = nc.vector.scalar_tensor_tensor(
                            out=S[:, h], in0=S[:, h], scalar=etot[:, j:j + 1], in1=bank[4 * c + 2][:, h],
                            op0=ALU.mult, op1=ALU.add)
                    last.then_inc(s_st[c], 1)
                for c in range(2):
                    tl = scan_tile(c, s)
                    dve.wait_ge(s_t[c], s + 1)
                    if first_visit(c, s):
                        nc.vector.tensor_tensor(osum[:, tl], to[c], bank[4 * c + 3], ALU.add).then_inc(s_to[c], 1)
                    else:
                        dve.wait_ge(s_to[1 - c], s + 1 if s == NT - 1 else NT - 1 - s)
                        own.tick(nc.vector.tensor_tensor(osum[:, tl], osum[:, tl], to[c], ALU.add))
                        own.sync()
                        nc.vector.tensor_tensor(osum[:, tl], osum[:, tl], bank[4 * c + 3], ALU.add)\
                            .then_inc(s_to[c], 1)
            dve.wait_ge(s_orr, 1)
            for n in range(NT):
                o = osum[:, done_order[n]]
                nc.vector.tensor_tensor(o, o, ssq[:, 1, n * NH:(n + 1) * NH].unsqueeze(2).to_broadcast([P, NH, P]),
                                        ALU.mult).then_inc(s_on, 1)
            for v in (hhi, hlo):
                for a, b in ((0, S0), (S0 + SEQ_S, P0), (P0 + SEQ_P, W)):
                    nc.vector.memset(v[:, 0:NH, a:b].bitcast(F32), 0.0)
            for j in range(NB):
                dve.wait_ge(s_yhi, j + 1)
                nc.vector.tensor_tensor(hlo[:, 4 + j, :], yb[:, j, :], hhi[:, 4 + j, :].bitcast(F32),
                                        ALU.subtract).then_inc(s_yready, 1)
            def gated(n):
                c0 = TILES[done_order[n]]
                dve.wait_ge(s_oT, n + 1)
                if n >= 3:
                    dve.wait_ge(s_yready, NB + n - 2)
                nc.vector.scalar_tensor_tensor(out=chain[n % 3][0], in0=bank[O_BANKS[n % 4]], scalar=g_o,
                                               in1=sgate[:, :, c0:c0 + P], op0=ALU.mult, op1=ALU.mult)\
                    .then_inc(s_oy, 1)

            gated(0)
            for n in range(NT):
                c0 = TILES[done_order[n]]
                if n + 1 < NT:
                    gated(n + 1)
                dve.wait_ge(s_yhi, NB + n + 1)
                nc.vector.tensor_tensor(hlo[:, 0:NH, c0:c0 + P], chain[n % 3][0],
                                        hhi[:, 0:NH, c0:c0 + P].bitcast(F32), ALU.subtract).then_inc(s_yready, 1)
            dve.wait_ge(s_yready, NB + NT)
            zero_pads(h32 + cv).then_inc(s_fill, 1)

            update_x("out", 0, 0, q=1)
            apply_norm(1, 8)
            add_batch(NT + 1)

            def pooled(k):
                gi = k // 2
                win = 2 << gi
                if k:
                    dve.wait_ge(s_mean, k)
                src, m = hp[:, k, :], WP
                for lv in range(gi + 1):
                    m -= 1 << lv
                    dst = psum_w[:, lv % 2, :]
                    own.tick(nc.vector.tensor_tensor(dst[:, 0:m], src[:, 0:m], src[:, (1 << lv):(1 << lv) + m],
                                                     ALU.add))
                    own.sync()
                    src = dst
                if k >= 2:
                    dve.wait_ge(s_mixed, k - 1)
                for pc, c0, n, _ in POOL_RANGES:
                    last = nc.vector.tensor_tensor(psum_w[:, 2 + k % 2, c0:c0 + n],
                                                   src[:, pc - win // 2:pc - win // 2 + n],
                                                   inv_n[:, gi, c0:c0 + n], ALU.mult)
                last.then_inc(s_mean, 1)

            for layer in range(2):
                if layer == 1:
                    zero_pads(cv)
                    for a in (0, PADW + SEQ_S, WP - PADW):
                        own.tick(nc.vector.memset(hp[:, :, a:a + PADW], 0.0))
                    own.sync()
                    dve.wait_ge(s_rstd, 3)
                    dve.wait_ge(s_inv, 16)
                    b = SEG["pool"]

                    def pool_update(m):
                        n = "CB"[m % 2]
                        if m % 4 < 3:
                            dve.wait_ge(s_pm, 3 * (m // 4) + m % 4 + 1)
                        else:
                            dve.wait_ge(s_unit, b["u"] + m // 4 + 1)
                        for bk, pc, ln, xc, cd in PIECES:
                            last = nc.vector.scalar_tensor_tensor(
                                out=x[:, m, xc:xc + ln], in0=pair[n][:, bk, pc:pc + ln],
                                scalar=mod[:, 1, 2, m, cd:cd + 1], in1=x[:, m, xc:xc + ln],
                                op0=ALU.mult, op1=ALU.add)
                        last.then_inc(s_ev[n], 1)

                    clear_acc(3)
                    for k in range(KD):
                        dve.wait_ge(s_aff, PRIMED + 16 + k + 1)
                        pooled(k)
                        if 0 < k <= KD // 2:
                            dve.wait_ge(s_hi, 16 + k)
                            nc.vector.tensor_tensor(hlo[:, k - 1, :], h32[(k - 1) % 2],
                                                    hhi[:, k - 1, :].bitcast(F32), ALU.subtract).then_inc(s_h, 1)
                        if k % 2 and k > 1:
                            pool_update(k - 3)
                            pool_update(k - 2)
                        if k % 2 == 0 and k > 2:
                            for s in range(2):
                                add_squares(k // 2 - 2, 3, s)
                    for s in range(2):
                        add_squares(KD // 2 - 2, 3, s)
                    add_batch(NT + 2)
                    dve.wait_ge(s_mod, NT + 3)
                    fold_scale(1, 1, g_ffn).then_inc(s_fold, 1)
                    for m in range(KD - 2, KD):
                        pool_update(m)
                    for s in range(2):
                        add_squares(KD // 2 - 1, 3, s)
                    apply_norm(3, 24)
                    add_batch(NT + 3)
                    dve.wait_ge(s_mod, NT + 4)
                for g, nf in enumerate(GROUPS):
                    b = SEG["up", layer, g]
                    u, f = b["u"], b["f"]
                    with dve.Fori(0, nf) as i:
                        own.enter(i, 2)
                        dve.wait_ge(s_ev["A"], i + (b["A"] + 1))
                        dve.wait_ge(s_silu, i + (PRIMED + NQKV + f))
                        conv(pad[0], cv[0], [tap_ffn[:, layer, j, ds(i + GROUP_AT[g], 1)] for j in range(3)])
                        dve.wait_ge(s_silu, i + (PRIMED + NQKV + f + 1))
                        dve.wait_ge(s_unit, i * 2 + (u + 2))
                        dve.wait_ge(s_hid_hi, i + (f + PRIMED))
                        nc.vector.tensor_tensor(halves(h32[0]), halves(cv[1]), pair["B"], ALU.mult)\
                            .then_inc(s_ev["B"], 1)
                        dve.wait_ge(s_hid_hi, i + (f + PRIMED + 1))
                        nc.vector.tensor_tensor(hidlo[:, i, :], h32[0], hidhi[:, i, :].bitcast(F32),
                                                ALU.subtract).then_inc(s_hid, 1)
                    own.leave(nf)
                    if layer == 0 and g == 2:
                        fold_scale(1, 0, g_mix)
                        nc.vector.tensor_tensor(mod[:, 1, 2], mod[:, 1, 2], g_pool, ALU.mult).then_inc(s_fold, 1)
                    update_x(("down", layer, g), layer, 1, q=((2, 4)[layer] if g == 2 else None))
            dve.wait_ge(s_rstd, 5)
            dve.wait_ge(s_xg, KD)
            for k in range(KD):
                if k % 3 != 2:
                    nc.vector.tensor_tensor(yout[:, k, :], yout[:, k, :], rstd, ALU.mult).then_inc(s_ychunk[0], 1)


IN_ORDER = list(range(NQKV + NGATE)) + [NQKV + NGATE + p * NB + j for j in range(NB) for p in (1, 2, 0)]


def kernel(**inputs):
    import concourse.bacc as bacc
    from concourse.bass_utils import run_bass_kernel_spmd

    a = {k: np.asarray(v) for k, v in inputs.items()}

    def tiles(w, rows):
        k, n = w.shape
        return np.ascontiguousarray(
            w.reshape(k // P, P, n // P, P).transpose(2, 1, 0, 3).reshape(n // P, P, rows * P))

    def chunks(v):
        v = v.reshape(v.shape[:-1] + (-1, P))
        return np.moveaxis(v, -1, 0)

    def twice(v):
        return np.repeat(v[..., None], 2, axis=-1)

    arrays = {}
    x = np.zeros((P, KD, W), np.float32)
    x[:, :, S0:S0 + SEQ_S] = a["x_sample"][0].T.reshape(KD, P, SEQ_S).transpose(1, 0, 2)
    x[:, :, P0:P0 + SEQ_P] = a["x_prompt"][0].T.reshape(KD, P, SEQ_P).transpose(1, 0, 2)
    arrays["x"] = x
    w_in = a["w_in_ab"][0]
    nqg = (NQKV + NGATE) * P
    main = tiles(np.concatenate([w_in[:, :nqg], w_in[:, nqg + 16:]], axis=1), KD)
    arrays["w_in"] = main[IN_ORDER]
    arrays["w_out"] = tiles(a["w_out_ab"][0], KD)
    wp = a["w_pool"][0].reshape(4, 2, P, 2, P).transpose(2, 0, 3, 1, 4)
    arrays["w_pool"] = np.ascontiguousarray(wp.reshape(P, 2, SLOT).transpose(1, 0, 2))
    arrays["w_gu"] = np.concatenate([
        np.stack([tiles(a["w_ffn_gate"][l], KD), tiles(a["w_ffn_up"][l], KD)], axis=1).reshape(2 * NF, P, SLOT)
        for l in range(2)])
    for g, nf in enumerate(GROUPS):
        rows = slice(GROUP_AT[g] * P, (GROUP_AT[g] + nf) * P)
        arrays[f"w_dn{g}"] = np.concatenate([tiles(a["w_ffn_down"][l][rows], nf) for l in range(2)])
    w_ada = np.concatenate([a["w_ada"][0], a["w_ada"][1]], axis=1)
    groups = w_ada[:, :ADA_LAST * P].reshape(2, 4, P, ADA_LAST // 2, ADA_COLS)
    arrays["w_ada"] = np.concatenate([
        groups.transpose(3, 0, 2, 1, 4).reshape(ADA_LAST, P, SLOT), tiles(w_ada[:, ADA_LAST * P:], KD)])
    ncol = nqg
    packed = {
        "norm_mix": twice(chunks(a["norm_mix_g"])),
        "norm_ffn": twice(chunks(a["norm_ffn_g"])),
        "pool_scale": twice(chunks(a["pool_scale"][0])),
        "final": chunks(a["final_norm_g"]),
        "tap_qkv": chunks(a["conv_qkv"][0]),
        "tap_b": chunks(a["conv_b"][0]),
        "tap_ffn": chunks(a["ffn_conv"]),
        "o_norm": a["o_norm_g"][0][:, None],
        "a_log": np.broadcast_to(a["a_log"][0].reshape(1, 1, 8), (P, NT, 8)),
        "dt_bias": np.broadcast_to(a["dt_bias"][0].reshape(1, 1, 8), (P, NT, 8)),
        "w_ba": w_in[:, ncol:ncol + 16].reshape(KD, P, 16).transpose(1, 0, 2),
        "cond": np.stack([chunks(a["c"][0]), chunks(a["c_ctx"])], axis=-1),
        "sel": (np.arange(P)[:, None] % 2 == np.arange(2)[None, :]).astype(np.float32),
        "b_ada": twice(chunks(a["b_ada"].reshape(-1))),
    }
    cols = np.zeros((P, NCOLS), np.float32)
    for name, (at, n) in COLS.items():
        cols[:, at:at + n] = packed[name].reshape(P, n)
    arrays["cols"] = cols
    arrays["state"] = np.ascontiguousarray(a["state_delta"][0, 0].transpose(2, 0, 1, 3))

    quarter = D // 4
    omega = (1.0 / (10000.0 ** (np.arange(quarter, dtype=np.float32) / quarter))).astype(np.float32)

    def sincos(n):
        e = np.arange(n, dtype=np.float32)[:, None] * omega[None, :]
        return np.concatenate([np.sin(e), np.cos(e)], axis=-1)

    pe = np.zeros((P, 4, ROWS + GRID_W), np.float32)
    pe[:, :, :ROWS] = sincos(ROWS).T.reshape(4, P, ROWS).transpose(1, 0, 2)
    pe[:, :, ROWS:] = sincos(GRID_W).T.reshape(4, P, GRID_W).transpose(1, 0, 2)
    arrays["pe"] = pe
    r, c = np.arange(P)[:, None], np.arange(P)[None, :]
    arrays["const"] = np.stack([r == c, r <= c, r >= c, r >= 0 * c], axis=1).astype(np.float32)
    lm = np.zeros((P, 2 * LEVELS, P), np.float16)
    for lv in range(LEVELS):
        b = 1 << lv
        same = r // (2 * b) == c // (2 * b)
        lm[:, lv] = same & (r // b % 2 == 0) & (c // b % 2 == 1)
        lm[:, LEVELS + lv] = same & (r // b % 2 == 1) & (c // b % 2 == 0)
    arrays["lmask"] = lm
    inv = np.zeros((P, 4, W), np.float32)
    for gi in range(4):
        w = 2 << gi
        for c0, n, _ in RANGES:
            tk = np.arange(n)
            inv[:, gi, c0:c0 + n] = 1.0 / (np.clip(tk - w // 2 + w, 0, n) - np.clip(tk - w // 2, 0, n))
    arrays["inv_n"] = inv

    nc = bacc.Bacc("TRN2", target_bir_lowering=False, num_devices=1)
    t = {}
    for name, v in arrays.items():
        t[name] = nc.dram_tensor(f"in_{name}", v.shape, mybir.dt.from_np(v.dtype), kind="ExternalInput").ap()
    t["y"] = nc.dram_tensor("out_y", (P, KD, SEQ_S + SEQ_P), F32, kind="ExternalOutput").ap()
    t["new_state"] = nc.dram_tensor("out_state", (P, 2, NH, P), F32, kind="ExternalOutput").ap()
    build(nc, t)
    res = run_bass_kernel_spmd(nc, [{f"in_{k}": v for k, v in arrays.items()}], core_ids=[0]).results[0]
    y = res["out_y"].transpose(2, 1, 0).reshape(SEQ_S + SEQ_P, D)
    y_sample = np.ascontiguousarray(y[:SEQ_S])[None]
    y_prompt = np.ascontiguousarray(y[SEQ_S:])[None]
    new_state = np.ascontiguousarray(res["out_state"].transpose(1, 2, 0, 3))[None, None]
    return y_prompt, y_sample, new_state
```
